# Optimizing a Trainium2 kernel written in Bass

```python
import jax, jax.numpy as jnp
from jax import lax
import numpy as np
import math

D_MODEL = 1024
BATCH = 1
SEQ = 512
DEPTH = 1

CHUNK = 64
N_META = 16
Q_BLOCK = 128
D_MIX = D_MODEL
FOX_HEADS = 8
FOX_HEAD_DIM = 64
FOX_WIDTH = FOX_HEADS * FOX_HEAD_DIM
HG_HEADS = 4
HG_EXPAND = 128
HG_HEAD_V = (D_MIX - FOX_WIDTH) // HG_HEADS
HG_K = HG_HEADS * HG_EXPAND
HG_V = HG_HEADS * HG_HEAD_V
D_FF = -(-8 * D_MODEL // (3 * 256)) * 256
EPS = 1e-6
MASK_VALUE = -1e30
LOG_F_MIN = -30.0
IN_SIZES = (FOX_WIDTH, FOX_WIDTH, FOX_WIDTH, FOX_HEADS, HG_K, HG_K, HG_V, HG_V)
IN_COLS = sum(IN_SIZES)


def rms_norm(x, w):
    xf = x.astype(jnp.float32)
    y = xf * lax.rsqrt(jnp.mean(xf * xf, axis=-1, keepdims=True) + EPS)
    return (y * w.astype(jnp.float32)).astype(x.dtype)

def forgetting_attention(q, k, v, log_f):
    B, L, H, Dh = q.shape
    n_blk = -(-L // Q_BLOCK)
    Lp = n_blk * Q_BLOCK
    pad = Lp - L
    padf = lambda a: jnp.pad(a, [(0, 0), (0, pad)] + [(0, 0)] * (a.ndim - 2))
    q, k, v, log_f = padf(q), padf(k), padf(v), padf(log_f)
    c = jnp.cumsum(log_f, axis=1)
    cT = c.transpose(0, 2, 1)
    scale = Dh ** -0.5
    key_pos = jnp.arange(Lp)
    qb = q.reshape(B, n_blk, Q_BLOCK, H, Dh).transpose(1, 0, 2, 3, 4)
    cb = c.reshape(B, n_blk, Q_BLOCK, H).transpose(1, 0, 3, 2)

    def block(args):
        i, q_i, c_i = args
        s = jnp.einsum('bqhd,bkhd->bhqk', q_i, k, preferred_element_type=jnp.float32) * scale
        s = s + (c_i[..., :, None] - cT[:, :, None, :])
        q_pos = i * Q_BLOCK + jnp.arange(Q_BLOCK)
        s = jnp.where(key_pos[None, :] <= q_pos[:, None], s, MASK_VALUE)
        p = jax.nn.softmax(s, axis=-1)
        return jnp.einsum('bhqk,bkhd->bqhd', p.astype(v.dtype), v)

    o = lax.map(block, (jnp.arange(n_blk), qb, cb))
    return o.transpose(1, 0, 2, 3, 4).reshape(B, Lp, H, Dh)[:, :L]

def hgrn2_recurrence(q, k, v, log_f):
    B, L, H, K = q.shape
    V = v.shape[-1]
    pad = (-L) % CHUNK
    padf = lambda a: jnp.pad(a, ((0, 0), (pad, 0), (0, 0), (0, 0)))
    q, k, v, log_f = padf(q), padf(k), padf(v), padf(log_f)
    Lp = L + pad
    n = Lp // CHUNK
    to_chunks = lambda a: a.reshape(B, n, CHUNK, H, a.shape[-1]).transpose(1, 0, 3, 2, 4)
    causal = jnp.tril(jnp.ones((CHUNK, CHUNK), dtype=bool))[:, :, None]

    def step(S, inp):
        q_c, k_c, v_c, g_c = inp
        b = jnp.cumsum(g_c, axis=2)
        o_inter = jnp.einsum('bhtk,bhkv->bhtv', q_c * jnp.exp(b), S)
        rel = b[:, :, :, None, :] - b[:, :, None, :, :]
        decay = jnp.where(causal, jnp.exp(jnp.where(causal, rel, 0.0)), 0.0)
        A = jnp.einsum('bhtk,bhsk,bhtsk->bhts', q_c, k_c, decay)
        o_intra = jnp.einsum('bhts,bhsv->bhtv', A, v_c)
        b_last = b[:, :, -1]
        k_dec = k_c * jnp.exp(b_last[:, :, None, :] - b)
        S = jnp.exp(b_last)[..., None] * S + jnp.einsum('bhsk,bhsv->bhkv', k_dec, v_c)
        return S, o_inter + o_intra

    S0 = jnp.zeros((B, H, K, V), jnp.float32)
    _, o = lax.scan(step, S0, (to_chunks(q), to_chunks(k), to_chunks(v), to_chunks(log_f)))
    o = o.transpose(1, 0, 3, 2, 4).reshape(B, Lp, H, V)
    return o[:, pad:]

def first_inputs(seed: int = 0) -> dict:
    key = jax.random.key(seed)
    ks = jax.random.split(key, 14)
    nrm = lambda k, shape, s: jax.random.normal(k, shape, jnp.float32) * s
    return {
        "x": nrm(ks[0], (BATCH, SEQ, D_MODEL), 1.0),
        "meta": nrm(ks[1], (N_META, D_MODEL), 1.0),
        "norm_mix_w": 1.0 + nrm(ks[2], (DEPTH, D_MODEL), 0.02),
        "w_in": nrm(ks[3], (DEPTH, D_MODEL, IN_COLS), D_MODEL ** -0.5),
        "fox_f_bias": 2.0 + nrm(ks[4], (DEPTH, FOX_HEADS), 0.5),
        "hgrn_lb_raw": nrm(ks[5], (DEPTH, HG_K), 1.0),
        "hgrn_norm_w": 1.0 + nrm(ks[6], (DEPTH, HG_HEAD_V), 0.02),
        "w_out": nrm(ks[7], (DEPTH, D_MIX, D_MODEL), D_MIX ** -0.5),
        "norm_ffn_w": 1.0 + nrm(ks[8], (DEPTH, D_MODEL), 0.02),
        "w_ffn_gate": nrm(ks[9], (DEPTH, D_MODEL, D_FF), D_MODEL ** -0.5),
        "w_ffn_up": nrm(ks[10], (DEPTH, D_MODEL, D_FF), D_MODEL ** -0.5),
        "w_ffn_down": nrm(ks[11], (DEPTH, D_FF, D_MODEL), D_FF ** -0.5),
        "norm_final_w": 1.0 + nrm(ks[12], (D_MODEL,), 0.02),
    }

def first_block(x, meta, norm_mix_w, w_in, fox_f_bias, hgrn_lb_raw, hgrn_norm_w, w_out,
              norm_ffn_w, w_ffn_gate, w_ffn_up, w_ffn_down, norm_final_w):
    B = x.shape[0]
    h = jnp.concatenate([jnp.broadcast_to(meta[None].astype(x.dtype), (B, N_META, D_MODEL)), x], axis=1)
    L = h.shape[1]
    s_lb = jax.nn.softmax(hgrn_lb_raw.astype(jnp.float32), axis=0)
    lower_bounds = jnp.cumsum(s_lb, axis=0) - s_lb[0]
    split_at = tuple(int(v) for v in np.cumsum(IN_SIZES)[:-1])

    for l in range(DEPTH):
        u = rms_norm(h, norm_mix_w[l])
        proj = u @ w_in[l]
        fq, fk, fv, ff, hq, hf, hi, hg = jnp.split(proj, split_at, axis=-1)

        fox_log_f = jax.nn.log_sigmoid(ff.astype(jnp.float32) + fox_f_bias[l].astype(jnp.float32))
        hs = (B, L, FOX_HEADS, FOX_HEAD_DIM)
        fox_out = forgetting_attention(fq.reshape(hs), fk.reshape(hs), fv.reshape(hs), fox_log_f)
        fox_out = fox_out.reshape(B, L, FOX_WIDTH).astype(h.dtype)

        lb = lower_bounds[l]
        one_minus_f = (1.0 - lb) * jax.nn.sigmoid(-hf.astype(jnp.float32))
        log_f = jnp.maximum(jnp.log1p(-one_minus_f), LOG_F_MIN)
        k_in = -jnp.expm1(log_f)
        q_h = jax.nn.silu(hq.astype(jnp.float32)) * (HG_EXPAND ** -0.5)
        ks_ = (B, L, HG_HEADS, HG_EXPAND)
        o_h = hgrn2_recurrence(q_h.reshape(ks_), k_in.reshape(ks_),
                               hi.astype(jnp.float32).reshape(B, L, HG_HEADS, HG_HEAD_V),
                               log_f.reshape(ks_))
        o_h = rms_norm(o_h, hgrn_norm_w[l])
        hgrn_out = (o_h.reshape(B, L, HG_V) * jax.nn.silu(hg.astype(jnp.float32))).astype(h.dtype)

        mixed = jnp.concatenate([fox_out, hgrn_out], axis=-1) @ w_out[l]
        h = h + mixed

        u = rms_norm(h, norm_ffn_w[l])
        h = h + (jax.nn.silu(u @ w_ffn_gate[l]) * (u @ w_ffn_up[l])) @ w_ffn_down[l]

    return rms_norm(h, norm_final_w)[:, N_META:]


DEPTH_2 = 2

N_MEM = 256
A_HEADS = 4
A_QK_DIM = 64
A_V_DIM = 2 * A_QK_DIM
A_QK_COLS = A_HEADS * 2 * A_QK_DIM
A_WIDTH = A_HEADS * A_V_DIM
POOL_WINDOWS = (2, 4, 8, 16)
POOL_GROUPS = len(POOL_WINDOWS)
POOL_GROUP_DIM = (D_MODEL // 2) // POOL_GROUPS
POOL_WIDTH = POOL_GROUPS * POOL_GROUP_DIM
EVEN_IN = 2 * A_QK_COLS + A_WIDTH + POOL_WIDTH
EVEN_MIX = A_WIDTH + POOL_WIDTH
CONV_WIDTH = 3
CONV_DIM = D_MODEL
X_HEADS = 4
X_HEAD_DIM = D_MODEL // X_HEADS
D_FF_2 = 4 * D_MODEL
REL_BUCKETS = 32
REL_MAX_EXACT = REL_BUCKETS // 2
REL_MAX_DIST = 128
N_EVEN = (DEPTH_2 + 1) // 2
N_ODD = DEPTH_2 // 2


def rms_norm_2(x, g):
    xf = x.astype(jnp.float32)
    y = xf * lax.rsqrt(jnp.mean(xf * xf, axis=-1, keepdims=True) + EPS)
    return (y * g.astype(jnp.float32)).astype(x.dtype)

def t5_bucket(n):
    small = n < REL_MAX_EXACT
    nf = jnp.maximum(n, 1).astype(jnp.float32)
    large = REL_MAX_EXACT + (jnp.log(nf / REL_MAX_EXACT)
                             / math.log(REL_MAX_DIST / REL_MAX_EXACT)
                             * (REL_BUCKETS - REL_MAX_EXACT)).astype(jnp.int32)
    large = jnp.minimum(large, REL_BUCKETS - 1)
    return jnp.where(small, n, large)

def diff_attention(q1, q2, k1, k2, v, lam, bias_dist):
    B, S = q1.shape[0], q1.shape[1]
    nb = S // Q_BLOCK
    scale = A_QK_DIM ** -0.5
    qb1 = q1.reshape(B, nb, Q_BLOCK, A_HEADS, A_QK_DIM).transpose(1, 0, 2, 3, 4)
    qb2 = q2.reshape(B, nb, Q_BLOCK, A_HEADS, A_QK_DIM).transpose(1, 0, 2, 3, 4)
    starts = jnp.arange(nb, dtype=jnp.int32) * Q_BLOCK
    kpos = jnp.arange(S, dtype=jnp.int32)

    def block(args):
        qa, qc, start = args
        qpos = start + jnp.arange(Q_BLOCK, dtype=jnp.int32)
        dist = qpos[:, None] - kpos[None, :]
        causal = dist >= 0
        bias = bias_dist[:, jnp.clip(dist, 0, S - 1)]

        def probs(q, k):
            s = jnp.einsum('bqhd,bkhd->bhqk', q, k).astype(jnp.float32) * scale + bias
            s = jnp.where(causal, s, -jnp.inf)
            return jax.nn.softmax(s, axis=-1)

        a = probs(qa, k1) - lam * probs(qc, k2)
        return jnp.einsum('bhqk,bkhd->bqhd', a.astype(v.dtype), v)

    out = lax.map(block, (qb1, qb2, starts))
    return out.transpose(1, 0, 2, 3, 4).reshape(B, S, A_HEADS, A_V_DIM)

def multi_scale_pool(u, pool_w, pool_scale):
    B, S = u.shape[0], u.shape[1]
    ug = u.reshape(B, S, POOL_GROUPS, POOL_GROUP_DIM).astype(jnp.float32)
    c = jnp.concatenate([jnp.zeros((B, 1, POOL_GROUPS, POOL_GROUP_DIM), jnp.float32),
                         jnp.cumsum(ug, axis=1)], axis=1)
    t = jnp.arange(S, dtype=jnp.int32)
    pooled = []
    for gi, w in enumerate(POOL_WINDOWS):
        cg = c[:, :, gi]
        cp = jnp.concatenate([jnp.zeros((B, w - 1, POOL_GROUP_DIM), jnp.float32), cg], axis=1)
        win_sum = cg[:, 1:] - cp[:, :S]
        count = jnp.minimum(t + 1, w).astype(jnp.float32)[None, :, None]
        pooled.append(win_sum / count - ug[:, :, gi])
    p = jnp.stack(pooled, axis=2).astype(u.dtype)
    y = jnp.einsum('bsgc,gcd->bsgd', p, pool_w) * pool_scale.reshape(POOL_GROUPS, POOL_GROUP_DIM)
    return y.reshape(B, S, POOL_WIDTH)

def even_mixer(h, w_in, w_out, lq1, lk1, lq2, lk2, subln_g, pool_w, pool_scale,
               bias_dist, lambda_init):
    B, S = h.shape[0], h.shape[1]
    proj = h @ w_in
    q = proj[..., :A_QK_COLS].reshape(B, S, A_HEADS, 2, A_QK_DIM)
    k = proj[..., A_QK_COLS:2 * A_QK_COLS].reshape(B, S, A_HEADS, 2, A_QK_DIM)
    v = proj[..., 2 * A_QK_COLS:2 * A_QK_COLS + A_WIDTH].reshape(B, S, A_HEADS, A_V_DIM)
    u = proj[..., 2 * A_QK_COLS + A_WIDTH:]
    lam = (jnp.exp(jnp.sum(lq1.astype(jnp.float32) * lk1.astype(jnp.float32)))
           - jnp.exp(jnp.sum(lq2.astype(jnp.float32) * lk2.astype(jnp.float32)))
           + lambda_init)
    o = diff_attention(q[..., 0, :], q[..., 1, :], k[..., 0, :], k[..., 1, :], v, lam, bias_dist)
    o = (rms_norm_2(o, subln_g) * (1.0 - lambda_init)).reshape(B, S, A_WIDTH)
    y = multi_scale_pool(u, pool_w, pool_scale)
    return jnp.concatenate([o, y], axis=-1) @ w_out

def odd_mixer(h, w_in, conv_w, w_out):
    S = h.shape[1]
    proj = h @ w_in
    b_gate = proj[..., :CONV_DIM]
    c_gate = proj[..., CONV_DIM:2 * CONV_DIM]
    z = c_gate * proj[..., 2 * CONV_DIM:]
    zp = jnp.pad(z, ((0, 0), (CONV_WIDTH - 1, 0), (0, 0)))
    y = zp[:, 0:S] * conv_w[0]
    for tap in range(1, CONV_WIDTH):
        y = y + zp[:, tap:tap + S] * conv_w[tap]
    return (b_gate * y) @ w_out

def cross_attention(h, mem_n, wq, wkv, wo):
    B, S = h.shape[0], h.shape[1]
    M = mem_n.shape[1]
    q = (h @ wq).reshape(B, S, X_HEADS, X_HEAD_DIM)
    kv = (mem_n @ wkv).reshape(B, M, 2, X_HEADS, X_HEAD_DIM)
    s = jnp.einsum('bshd,bmhd->bhsm', q, kv[:, :, 0]).astype(jnp.float32) * X_HEAD_DIM ** -0.5
    p = jax.nn.softmax(s, axis=-1)
    o = jnp.einsum('bhsm,bmhd->bshd', p.astype(h.dtype), kv[:, :, 1]).reshape(B, S, D_MODEL)
    return o @ wo

def sq_relu_mlp(h, w1, w2):
    a = jax.nn.relu(h @ w1)
    return (a * a) @ w2

def second_inputs(seed: int = 0) -> dict:
    key = jax.random.key(seed)
    ks = iter(jax.random.split(key, 32))
    f32 = jnp.float32

    def nrm(shape, scale):
        return jax.random.normal(next(ks), shape, f32) * scale

    def gain(shape):
        return 1.0 + nrm(shape, 0.02)

    return {
        "x": nrm((BATCH, SEQ, D_MODEL), 1.0),
        "mem": nrm((BATCH, N_MEM, D_MODEL), 1.0),
        "rel_bias": nrm((REL_BUCKETS, A_HEADS), 0.5),
        "mem_norm_g": gain((D_MODEL,)),
        "norm_mix_g": gain((DEPTH_2, D_MODEL)),
        "norm_xattn_g": gain((DEPTH_2, D_MODEL)),
        "norm_mlp_g": gain((DEPTH_2, D_MODEL)),
        "final_norm_g": gain((D_MODEL,)),
        "ab_w_in": nrm((N_EVEN, D_MODEL, EVEN_IN), D_MODEL ** -0.5),
        "ab_w_out": nrm((N_EVEN, EVEN_MIX, D_MODEL), EVEN_MIX ** -0.5),
        "lambda_q1": nrm((N_EVEN, A_QK_DIM), 0.1),
        "lambda_k1": nrm((N_EVEN, A_QK_DIM), 0.1),
        "lambda_q2": nrm((N_EVEN, A_QK_DIM), 0.1),
        "lambda_k2": nrm((N_EVEN, A_QK_DIM), 0.1),
        "subln_g": gain((N_EVEN, A_V_DIM)),
        "pool_w": nrm((N_EVEN, POOL_GROUPS, POOL_GROUP_DIM, POOL_GROUP_DIM), POOL_GROUP_DIM ** -0.5),
        "pool_scale": 1.0 + nrm((N_EVEN, POOL_WIDTH), 0.1),
        "conv_w_in": nrm((N_ODD, D_MODEL, 3 * CONV_DIM), D_MODEL ** -0.5),
        "conv_w": nrm((N_ODD, CONV_WIDTH, CONV_DIM), CONV_WIDTH ** -0.5),
        "conv_w_out": nrm((N_ODD, CONV_DIM, D_MODEL), CONV_DIM ** -0.5),
        "xattn_wq": nrm((DEPTH_2, D_MODEL, D_MODEL), D_MODEL ** -0.5),
        "xattn_wkv": nrm((DEPTH_2, D_MODEL, 2 * D_MODEL), D_MODEL ** -0.5),
        "xattn_wo": nrm((DEPTH_2, D_MODEL, D_MODEL), D_MODEL ** -0.5),
        "mlp_w1": nrm((DEPTH_2, D_MODEL, D_FF_2), D_MODEL ** -0.5),
        "mlp_w2": nrm((DEPTH_2, D_FF_2, D_MODEL), D_FF_2 ** -0.5),
    }

def second_block(x, mem, rel_bias, mem_norm_g, norm_mix_g, norm_xattn_g, norm_mlp_g,
              final_norm_g, ab_w_in, ab_w_out, lambda_q1, lambda_k1, lambda_q2,
              lambda_k2, subln_g, pool_w, pool_scale, conv_w_in, conv_w, conv_w_out,
              xattn_wq, xattn_wkv, xattn_wo, mlp_w1, mlp_w2):
    S = x.shape[1]
    buckets = t5_bucket(jnp.arange(S, dtype=jnp.int32))
    bias_dist = rel_bias.astype(jnp.float32)[buckets].T
    mem_n = rms_norm_2(mem, mem_norm_g)
    h = x
    for l in range(DEPTH_2):
        i = l // 2
        hn = rms_norm_2(h, norm_mix_g[l])
        if l % 2 == 0:
            lambda_init = 0.8 - 0.6 * math.exp(-0.3 * l)
            h = h + even_mixer(hn, ab_w_in[i], ab_w_out[i], lambda_q1[i], lambda_k1[i],
                               lambda_q2[i], lambda_k2[i], subln_g[i], pool_w[i],
                               pool_scale[i], bias_dist, lambda_init)
        else:
            h = h + odd_mixer(hn, conv_w_in[i], conv_w[i], conv_w_out[i])
        h = h + cross_attention(rms_norm_2(h, norm_xattn_g[l]), mem_n,
                                xattn_wq[l], xattn_wkv[l], xattn_wo[l])
        h = h + sq_relu_mlp(rms_norm_2(h, norm_mlp_g[l]), mlp_w1[l], mlp_w2[l])
    return rms_norm_2(h, final_norm_g)


def setup_inputs(seed=0):
    out = dict(first_inputs(seed))
    for name, value in second_inputs(seed + 1).items():
        if name != "x":
            out[name + "_2"] = value
    return out


def reference(
    x, meta, norm_mix_w, w_in, fox_f_bias, hgrn_lb_raw, hgrn_norm_w, w_out, norm_ffn_w,
    w_ffn_gate, w_ffn_up, w_ffn_down, norm_final_w, mem_2, rel_bias_2, mem_norm_g_2,
    norm_mix_g_2, norm_xattn_g_2, norm_mlp_g_2, final_norm_g_2, ab_w_in_2, ab_w_out_2,
    lambda_q1_2, lambda_k1_2, lambda_q2_2, lambda_k2_2, subln_g_2, pool_w_2, pool_scale_2,
    conv_w_in_2, conv_w_2, conv_w_out_2, xattn_wq_2, xattn_wkv_2, xattn_wo_2, mlp_w1_2,
    mlp_w2_2,
):
    x = first_block(
        x, meta, norm_mix_w, w_in, fox_f_bias, hgrn_lb_raw, hgrn_norm_w, w_out, norm_ffn_w,
        w_ffn_gate, w_ffn_up, w_ffn_down, norm_final_w,
    )
    return second_block(
        x, mem_2, rel_bias_2, mem_norm_g_2, norm_mix_g_2, norm_xattn_g_2, norm_mlp_g_2,
        final_norm_g_2, ab_w_in_2, ab_w_out_2, lambda_q1_2, lambda_k1_2, lambda_q2_2,
        lambda_k2_2, subln_g_2, pool_w_2, pool_scale_2, conv_w_in_2, conv_w_2, conv_w_out_2,
        xattn_wq_2, xattn_wkv_2, xattn_wo_2, mlp_w1_2, mlp_w2_2,
    )


_drawn_inputs = setup_inputs


def setup_inputs(seed=0):
    import zlib

    import numpy as np

    out = dict(_drawn_inputs(seed))
    spreads = {}
    factors = {'hgrn_norm_w': 4.074,
     'norm_ffn_w': 2.821,
     'mem_norm_g_2': 8.0,
     'norm_xattn_g_2': 8.0,
     'final_norm_g_2': 7.862,
     'lambda_q1_2': 3.111,
     'lambda_k1_2': 8.0,
     'subln_g_2': 4.857,
     'norm_mlp_g_2': 3.09}
    for name, (base, spread) in spreads.items():
        noise = np.random.default_rng([zlib.crc32(name.encode()), seed]).standard_normal(out[name].shape)
        drawn = base * np.exp(spread * noise) if base else spread * noise
        out[name] = __import__('jax').numpy.asarray(drawn.astype(out[name].dtype))
    for name, factor in factors.items():
        out[name] = (out[name] * factor).astype(out[name].dtype)
    return out
```

```python
import concourse.bass as bass
from concourse import mybir
from collections import deque
import numpy as np

F32 = mybir.dt.float32
F32R = mybir.dt.float32r
U8 = mybir.dt.uint8
ACT = mybir.ActivationFunctionType
ALU = mybir.AluOpType
AX = mybir.AxisListType

NT = 512
NM = 16
NA = NT + NM
EPS = 1e-6
FMIN = float(np.exp(-30.0))
LAMBDA_INIT = 0.2
WINDOWS = (2, 4, 8, 16)
LEVELS = (2, 4, 8, 16, 32, 64)

V_MIX, V_FFN, V_FIN, V_MEM = 0, 8, 16, 24
V_MIX2, V_XA2, V_MLP2, V_FIN2 = 32, 48, 64, 80
V_LB, V_HN, V_SUB, V_PS, V_CONV, V_FB, V_LAM, V_REL = 88, 92, 93, 94, 98, 122, 123, 127
NVEC = 131
C_ID, C_CAUSAL, C_ONEHOT, C_SEL, C_CINV = 0, 128, 256, 640, 1664
NCONST = 1728

HIDDEN = (8, 8, 6)


def plan():
    out = []

    def lot(name, nk, cols, k0=0):
        out.append([(name, k0 + k, c) for k in range(nk) for c in cols])

    def wide(name, nk, c0, n, k0=0):
        for c in range(c0, c0 + n, 4):
            lot(name, nk, range(c, c + 4), k0)

    wide("w_in", 8, 0, 8)
    lot("ff", 8, [0])
    wide("w_in", 8, 8, 4)
    wide("hgrn", 8, 0, 16)
    wide("w_out", 8, 0, 8)
    f0 = 0
    for nh in HIDDEN:
        for j in range(f0, f0 + nh, 2):
            out.append([(n, k, c) for k in range(8)
                        for n, c in (("w_ffn_gate", j), ("w_ffn_gate", j + 1), ("w_ffn_up", j), ("w_ffn_up", j + 1))])
        wide("w_ffn_down", nh, 0, 8, f0)
        f0 += nh
    wide("ab_w_in_2", 8, 0, 16)
    wide("ab_w_out_2", 8, 0, 8)
    for l in range(2):
        if l == 1:
            for j in range(8):
                lot("conv_w_in_2", 8, [j, 8 + j, 16 + j])
            wide("conv_w_out_2", 8, 0, 8)
        wide(f"xattn_wkv_2.{l}", 8, 0, 16)
        wide(f"xattn_wq_2.{l}", 8, 0, 8)
        wide(f"xattn_wo_2.{l}", 8, 0, 8)
        for c in range(4):
            wide(f"mlp_w1_2.{l}", 8, 8 * c, 8)
            wide(f"mlp_w2_2.{l}", 8, 0, 8, 8 * c)
    return out


def call(fn, *args, **kwargs):
    return lambda e: fn(*args, **kwargs)


class Engine:

    def __init__(self, sem):
        self.sem, self.n, self.ops, self.seen = sem, 0, [], {}

    def wait(self, *tokens):
        for t in tokens:
            if t is None:
                continue
            sem, n = t
            if self.seen.get(id(sem), 0) < n:
                self.seen[id(sem)] = n
                self.ops.append(lambda e, sem=sem, n=n: e.wait_ge(sem, n))

    def do(self, fn, *tokens):
        self.wait(*tokens)
        self.n += 1
        self.ops.append(lambda e: fn(e).then_inc(self.sem, 1))
        return (self.sem, self.n)

    def go(self, fn):
        self.ops.append(fn)

    def run(self, e):
        for op in self.ops:
            op(e)


def build(nc, A, out, scratch):
    held = []

    def new_sem(name):
        cm = nc.semaphore(name)
        held.append(cm)
        return cm.__enter__()

    pe, act, dve, pool, sp = (Engine(new_sem(f"s_{n}")) for n in ("pe", "act", "dve", "pool", "sp"))
    at = [16512]

    def sb(name, shape, dt=F32, offset=None):
        size = (int(np.prod(shape[1:])) * (1 if dt == U8 else 4) + 63) // 64 * 64
        if offset is None:
            offset = at[0]
            at[0] += size
            assert at[0] <= 229344, (name, at[0])
        return nc.alloc_sbuf_tensor_at(name, shape, dt, offset=offset)

    def arena(begin, end):
        p = [begin]

        def get(name, shape, dt=F32):
            t = sb(name, shape, dt, p[0])
            p[0] += (int(np.prod(shape[1:])) * (1 if dt == U8 else 4) + 63) // 64 * 64
            assert p[0] <= end, (name, p[0], end)
            return t
        return get

    bank = []
    for i in range(8):
        cm = nc.psum_tensor(f"ps{i}", [128, 512], F32)
        held.append(cm)
        bank.append(cm.__enter__())
    free = deque((i, None) for i in range(8))

    def take():
        i, tok = free.popleft()
        pe.wait(tok)
        return i

    def give(i, tok):
        free.append((i, tok))

    NR, NS = 3, 4
    raw = sb("raw", [128, NR, 1024])
    WH = sb("WH", [128, NS, 1024], F32R)
    WL = sb("WL", [128, NS, 1024], F32R)
    H = sb("H", [128, 8, NA])
    cst = sb("cst", [128, NCONST])
    msk = sb("msk", [128, 7, 128], U8)
    vec = sb("vec", [128, NVEC])
    ones = sb("ones", [128, 128])
    RB = sb("RB", [128, NA])
    RS = sb("RS", [128, NA])
    RC = sb("RC", [128, 5])
    RCs = sb("RCs", [128, 5])
    ACC = sb("ACC", [128, NA])
    SQ = sb("SQ", [128, 2, NA])
    eps = sb("eps", [128, 1])
    u0 = at[0]
    UH = sb("UH", [128, 8, NA], F32R)
    UL = sb("UL", [128, 8, NA], F32R)
    u1 = at[0]
    h0 = at[0]
    HH = sb("HH", [128, 8, NT], F32R)
    HL = sb("HL", [128, 8, NT], F32R)
    t0 = at[0]
    END = 229344
    ident = cst[:, C_ID:C_ID + 128]
    causal = cst[:, C_CAUSAL:C_CAUSAL + 128]

    s_c = new_sem("s_cst")
    s_h = [new_sem(f"s_h{i}") for i in range(4)]

    def load(dst, src, sem):
        sp.ops.append(lambda e: e.dma_start(dst, src).then_inc(sem, 16))

    load(vec[:, :], A["vecs"], s_c)
    for i in range(4):
        load(H[:, 2 * i:2 * i + 2, :], A["hT"].rearrange("(k p) n -> p k n", p=128)[:, 2 * i:2 * i + 2, :], s_h[i])

    tiles = [t for lot in plan() for t in lot]
    assert len(tiles) % 8 == 0
    NU = len(tiles) // 8
    s_w = [new_sem(f"s_w{i}") for i in range(NR)]
    wdram = A["stream"]

    class Stream:
        made = 0
        lo = {}
        used = {}
        pos = 0

    st = Stream()

    def split(u):
        r, s = u % NR, u % NS
        if u >= NR:
            sp.wait(st.lo[u - NR])
        load(raw[:, r, :], wdram[u], s_w[r])
        landed = (s_w[r], 16 * (u // NR + 1))
        hi = act.do(call(nc.scalar.activation, WH[:, s, :], raw[:, r, :], ACT.Copy), landed, st.used.get(u - NS))
        st.lo[u] = dve.do(call(nc.vector.tensor_tensor, WL[:, s, :], raw[:, r, :], WH[:, s, :].bitcast(F32),
                                                    ALU.subtract), hi, landed, st.used.get(u - NS))

    def weights(n):
        u, j = st.pos // 8, st.pos % 8
        assert j + n <= 8
        if j == 0:
            while st.made < min(u + 3, NU):
                split(st.made)
                st.made += 1
            pe.wait(st.lo[u])
        st.pos += n
        c = slice(128 * j, 128 * (j + n))
        return WH[:, u % NS, c], WL[:, u % NS, c], (u if st.pos % 8 == 0 else None)

    def mm(o, l, r, start, stop):
        pe.go(call(nc.tensor.matmul, o, l, r, start=start, stop=stop, skip_group_check=True))

    def mmt(o, l, r, start, stop, *tokens):
        return pe.do(call(nc.tensor.matmul, o, l, r, start=start, stop=stop, skip_group_check=True), *tokens)

    def passes(o, ah, al, bh, bl, start, stop, token):
        mm(o, ah, bh, start, False)
        mm(o, ah, bl, False, False)
        return (mmt if token else mm)(o, al, bh, False, stop)

    def lin(nk, nm, XH, XL, ready, evac, n0=NM, n=NT, rem=None, hook=None):
        bk = [take() for _ in range(nm)]
        rb = take() if rem else None
        fin = []
        for k in range(nk):
            pe.wait(*ready[k])
            for m in range(nm):
                wh, wl, last = weights(1)
                end = k == nk - 1
                passes(bank[bk[m]][:, 0:n], wh, wl, XH[:, k, n0:n0 + n], XL[:, k, n0:n0 + n], k == 0, end, False)
                if rem:
                    passes(bank[rb][:, NM * m:NM * m + NM], wh, wl, XH[:, k, 0:NM], XL[:, k, 0:NM],
                           k == 0 and m == 0, end, False)
                if end or last is not None:
                    prev = pe.ops.pop()
                    tok = pe.do(prev)
                    if last is not None:
                        st.used[last] = tok
                    if end:
                        fin.append(tok)
            if hook and k == (1 if nk > 1 else 0):
                hook()
        toks = []
        for m in range(nm):
            t = evac(m, bank[bk[m]][:, 0:n], fin[m])
            give(bk[m], t)
            toks.append(t)
        if rem:
            give(rb, rem(bank[rb][:, 0:NM * nm].rearrange("p (m n) -> p m n", n=NM), fin[-1]))
        return fin

    def lin_tok(nk, XH, XL, ready, chunks, evac):
        bk = [take() for _ in chunks]
        for k in range(nk):
            pe.wait(*ready[k])
            wh, wl, last = weights(4)
            for i, c in enumerate(chunks):
                tok = passes(bank[bk[i]][:, :], XH[:, k, c:c + 128], XL[:, k, c:c + 128], wh, wl, k == 0,
                             k == nk - 1, True)
            if last is not None:
                st.used[last] = tok
        for i, c in enumerate(chunks):
            give(bk[i], evac(i, bank[bk[i]], tok))

    class Norm:
        acc = None
        read = None
        sq = [None, None]
        rb = None
        rc = None
    nm_ = Norm()

    def square_in(k, src, n0, n, tok):
        c = slice(n0, n0 + n)
        if k == 0:
            nm_.acc = pool.do(call(nc.gpsimd.tensor_tensor, ACC[:, c], src, src, ALU.mult), tok, nm_.read)
        else:
            s = SQ[:, k % 2, c]
            a = pool.do(call(nc.gpsimd.tensor_tensor, s, src, src, ALU.mult), tok, nm_.sq[k % 2])
            nm_.acc = pool.do(call(nc.gpsimd.tensor_tensor, ACC[:, c], ACC[:, c], s, ALU.add), a, nm_.acc)
            nm_.sq[k % 2] = nm_.acc

    def inv_rms(ranges, chunks, users):
        last = None
        for n0, n in ranges:
            b = take()
            t = mmt(bank[b][:, 0:n], ones[:, :], ACC[:, n0:n0 + n], True, True, nm_.acc, t_ones)
            a = act.do(call(nc.scalar.activation, RS[:, n0:n0 + n], bank[b][:, 0:n], ACT.Sqrt,
                                                              bias=eps[:, :], scale=1.0 / 1024), t, nm_.rb, t_eps)
            give(b, a)
            last = dve.do(call(nc.vector.reciprocal, RB[:, n0:n0 + n], RS[:, n0:n0 + n]), a, *users)
        if chunks:
            b = take()
            for i, c in enumerate(chunks):
                t = mmt(bank[b][:, i:i + 1], ACC[:, c:c + 128], ones[:, 0:1], True, True)
            k = len(chunks)
            a = act.do(call(nc.scalar.activation, RCs[:, 0:k], bank[b][:, 0:k], ACT.Sqrt, bias=eps[:, :],
                                              scale=1.0 / 1024), t, nm_.rc)
            give(b, a)
            nm_.rc = dve.do(call(nc.vector.reciprocal, RC[:, 0:k], RCs[:, 0:k]), a, *users)
        nm_.read = t
        nm_.rb = last
        return last

    def hilo(hi, lo, src, w, tok, *free_):
        if w is None:
            a = act.do(call(nc.scalar.activation, hi, src, ACT.Copy), tok, *free_)
            return dve.do(call(nc.vector.tensor_tensor, lo, src, hi.bitcast(F32), ALU.subtract), a, tok, *free_)
        a = act.do(call(nc.scalar.activation, hi, src, ACT.Copy, scale=w), tok, *free_)
        return dve.do(call(nc.vector.scalar_tensor_tensor, lo, src, w, hi.bitcast(F32), ALU.mult, ALU.subtract),
                      a, tok, *free_)

    ready = [[] for _ in range(8)]
    all_col = slice(0, NA)
    xc = slice(NM, NA)
    CH = [NM + 128 * i for i in range(4)]

    def residual(m0, wcol, last=True):
        def evac(m, p, tok):
            k = m0 + m
            t = dve.do(call(nc.vector.tensor_tensor, H[:, k, xc], p, H[:, k, xc], ALU.add), tok, h_tok[k])
            h_tok[k] = t
            if last:
                if wcol is not None:
                    ready[k] = [hilo(UH[:, k, xc], UL[:, k, xc], H[:, k, xc], vec[:, wcol + k:wcol + k + 1], t)]
                square_in(k, H[:, k, xc], NM, NT, t)
            return t
        return evac

    h_tok = [None] * 8

    t_ones = dve.do(call(nc.vector.memset, ones[:, :], 1.0))
    t_eps = dve.do(call(nc.vector.memset, eps[:, :], EPS))
    t_vec = (s_c, 16)
    t_cst = (s_c, 48)

    P1 = arena(t0, END)
    OM = P1("OM", [128, 4, NA])
    V2 = P1("V2", [128, 5, NT])
    r0 = t0 + (4 * NA + 5 * NT) * 4
    Q = P1("Q", [128, 4, NT])
    K = P1("K", [128, 4, NA])
    V = P1("V", [128, 5, NT])
    CT = P1("CT", [8, NA])
    CC = P1("CC", [128, 4, 8])
    small = P1("small", [128, 32])
    NB = P1("NB", [128, NA])
    S2 = P1("S2", [128, 2, NA])
    PM = P1("PM", [16, NT])
    PT = P1("PT", [128, 4, NT])
    FZ = sb("FZ", [8, 3, NA], F32, t0 + (4 * NA + 5 * NT + 4 * NT + 4 * NA + 5 * NT + NA + 32 + 32 + NA + 2 * NA + NT) * 4)
    HQ = sb("HQ", [128, 4, NT], F32, t0 - 4 * NT * 4)
    HG = sb("HG", [128, 4, NT], F32, t0 - 12 * NT * 4)
    MF = sb("MF", [128, 7, 128], F32, h0)

    for k in range(8):
        t = (s_h[k // 2], 16)
        ready[k] = [hilo(UH[:, k, :], UL[:, k, :], H[:, k, :], vec[:, V_MIX + k:V_MIX + k + 1], t, t_vec)]
        square_in(k, H[:, k, :], 0, NA, t)

    def load_constants():
        load(cst[:, :], A["consts"], s_c)
        load(MF[:, :, :], A["masks"].rearrange("p (l n) -> p l n", l=7), s_c)
        return dve.do(call(nc.vector.tensor_copy, msk[:, :, :], MF[:, :, :]), (s_c, 48))


    def first_hook():
        inv_rms([(NM, NT), (0, NM)], [0] + CH, [])

    def times_r(dst, extra=None):
        def evac(m, p, tok):
            if extra is None:
                return dve.do(call(nc.vector.tensor_tensor, dst[:, m, dst.shape[2] - NT:], p, RB[:, xc], ALU.mult), tok,
                              nm_.rb)
            return dve.do(call(nc.vector.scalar_tensor_tensor, dst[:, m, :], p, extra, RB[:, xc], ALU.mult, ALU.mult),
                          tok, nm_.rb)
        return evac

    def rem_r(dst):
        def evac(p, tok):
            r = RB[:, 0:NM].unsqueeze(1).broadcast_to([128, 4, NM])
            return dve.do(call(nc.vector.tensor_tensor, dst[:, :, 0:NM], p, r, ALU.mult), tok, nm_.rb)
        return evac

    def rows_r(dst, off):
        def evac(i, p, tok):
            rows = NM if (off == 0 and i == 0) else 128
            return act.do(call(nc.scalar.activation, dst[0:rows, i, :], p[0:rows, :], ACT.Copy,
                                                 scale=RC[0:rows, i:i + 1]), tok, nm_.rc)
        return evac

    lin(8, 4, UH, UL, ready, times_r(Q, 0.125), hook=first_hook)
    t_msk = load_constants()
    lin(8, 4, UH, UL, ready, times_r(K), rem=rem_r(K))

    def ff_evac(m, p, tok):
        return dve.do(call(nc.vector.tensor_tensor, FZ[:, 0, NM:NA], p[0:8, :], RB[0:8, NM:NA], ALU.mult), tok, nm_.rb)

    def ff_rem(p, tok):
        return dve.do(call(nc.vector.tensor_tensor, FZ[:, 0, 0:NM], p[0:8, 0, :], RB[0:8, 0:NM], ALU.mult), tok)

    lin(8, 1, UH, UL, ready, ff_evac, rem=ff_rem)
    t_z = (dve.sem, dve.n)
    t_z = dve.do(call(nc.vector.tensor_scalar, FZ[:, 0, :], FZ[:, 0, :], vec[0:8, V_FB:V_FB + 1], None, ALU.add),
                 t_z, t_vec)
    t = dve.do(call(nc.vector.scalar_tensor_tensor, FZ[:, 1, :], FZ[:, 0, :], -1.0, FZ[:, 0, :], ALU.mult, ALU.max), t_z)
    t = act.do(call(nc.scalar.activation, FZ[:, 1, :], FZ[:, 1, :], ACT.Exp, scale=-1.0), t)
    t = act.do(call(nc.scalar.activation, FZ[:, 2, :], FZ[:, 1, :], ACT.Ln, bias=ones[0:8, 0:1]), t)
    t = dve.do(call(nc.vector.scalar_tensor_tensor, FZ[:, 1, :], FZ[:, 0, :], 0.0, FZ[:, 2, :], ALU.min,
                                                ALU.subtract), t)
    t0_ = dve.do(call(nc.vector.memset, FZ[:, 2, :], 1.0), t)
    t_ct = dve.do(call(nc.vector.tensor_tensor_scan, CT[:, :], FZ[:, 2, :], FZ[:, 1, :], 0.0, ALU.mult, ALU.add), t0_)
    b = take()
    for i in range(4):
        t = pe.do(call(nc.tensor.transpose, bank[b][:, 8 * i:8 * i + 8], CT[:, CH[i]:CH[i] + 128],
                                            cst[0:8, C_ID:C_ID + 8]), t_ct, t_cst)
    t_cc = act.do(call(nc.scalar.activation, CC[:, :, :], bank[b][:, 0:32].rearrange("p (i h) -> p i h", h=8),
                                         ACT.Copy), t)
    give(b, t_cc)
    lin_tok(8, UH, UL, ready, [0] + CH, rows_r(V, 0))
    t_v = (act.sem, act.n)

    def silu_r(dst, tmp_scale=None):
        def evac(m, p, tok):
            a = dve.do(call(nc.vector.tensor_tensor, dst[:, m, :], p, RB[:, xc], ALU.mult), tok, nm_.rb)
            act.do(call(nc.scalar.activation, dst[:, m, :], dst[:, m, :], ACT.Silu), a)
            return a
        return evac

    lin(8, 4, UH, UL, ready, silu_r(HQ))
    t_hq = (act.sem, act.n)
    lin(8, 4, UH, UL, ready, times_r(OM), rem=rem_r(OM))
    t_om = (dve.sem, dve.n)
    lin_tok(8, UH, UL, ready, [0] + CH, rows_r(V2, 0))
    t_v2 = (act.sem, act.n)
    lin(8, 4, UH, UL, ready, silu_r(HG))
    t_hg = (act.sem, act.n)
    t_u_free = (pe.sem, pe.n)

    def pipeline(items, stages):
        for step in range(len(items) + len(stages) - 1):
            for s in reversed(range(len(stages))):
                if 0 <= step - s < len(items):
                    stages[s](items[step - s])

    nS = [None, None]
    nPT = [None]
    nNB = [None]
    mfree = {}

    def fox_bias(h):
        b, b2 = take(), take()
        sel = cst[0:8, C_SEL + 128 * h:C_SEL + 128 * h + 128]
        mmt(bank[b][:, :], sel, CT[:, NM:NA], True, True, t_cst, t_ct)
        t = mmt(bank[b2][:, 0:NM], sel, CT[:, 0:NM], True, True)
        act.do(call(nc.scalar.activation, NB[:, NM:NA], bank[b][:, :], ACT.Copy), t, nNB[0])
        t = act.do(call(nc.scalar.activation, NB[:, 0:NM], bank[b2][:, 0:NM], ACT.Copy))
        give(b, t)
        give(b2, t)
        return t

    items = [dict(h=h, i=i, n=h * 4 + i) for h in range(8) for i in range(4)]
    head = [dict() for _ in range(8)]

    def f0(x):
        h, i = x["h"], x["i"]
        if i == 0:
            head[h]["nb"] = fox_bias(h)
        rows = slice(64 * (h % 2), 64 * (h % 2) + 64)
        ns = NM + 128 * (i + 1)
        lhs = Q[rows, h // 2, 128 * i:128 * i + 128]
        x["b"] = [(take(), 0, min(ns, 512))]
        if ns > 512:
            x["b"].append((take(), 512, ns - 512))
        for b, c, n in x["b"]:
            x["t"] = mmt(bank[b][:, 0:n], lhs, K[rows, h // 2, c:c + n], True, True)

    def f1(x):
        h, i, s = x["h"], x["i"], x["n"] % 2
        for b, c, n in x["b"]:
            t = dve.do(call(nc.vector.scalar_tensor_tensor, 
                S2[:, s, c:c + n], bank[b][:, 0:n], CC[:, i, h:h + 1], NB[:, c:c + n], ALU.add, ALU.add),
                x["t"], head[h]["nb"], t_cc, nS[s])
            give(b, t)
        nNB[0] = t
        d = S2[:, s, NM + 128 * i:NM + 128 * i + 128]
        t = pool.do(call(nc.gpsimd.affine_select, out=d, in_=d, compare_op=ALU.is_ge, fill=-1e30, base=0,
                                              pattern=[[-1, 128]], channel_multiplier=1), t)
        ns = NM + 128 * (i + 1)
        m = small[:, 4 * (x["n"] % 8):4 * (x["n"] % 8) + 4]
        t = dve.do(call(nc.vector.tensor_reduce, m[:, 0:1], S2[:, s, 0:ns], AX.X, ALU.max, negate=True), t,
                   mfree.get(x["n"] % 8))
        x["e"] = act.do(call(nc.scalar.activation, S2[:, s, 0:ns], S2[:, s, 0:ns], ACT.Exp, bias=m[:, 0:1],
                                               accum_out=m[:, 1:2]), t)

    def f2(x):
        h, i, s = x["h"], x["i"], x["n"] % 2
        ns = NM + 128 * (i + 1)
        m = small[:, 4 * (x["n"] % 8):4 * (x["n"] % 8) + 4]
        t = dve.do(call(nc.vector.reciprocal, m[:, 2:3], m[:, 1:2]), x["e"])
        t = dve.do(call(nc.vector.tensor_scalar, S2[:, s, 0:ns], S2[:, s, 0:ns], m[:, 2:3], None, ALU.mult), t)
        mfree[x["n"] % 8] = t
        b, b2 = take(), take()
        pe.wait(t)
        pe.go(call(nc.tensor.transpose, bank[b2][0:NM, 0:128], S2[:, s, 0:NM], ident))
        for j in range(i + 1):
            t = pe.do(call(nc.tensor.transpose, bank[b][:, 128 * j:128 * j + 128],
                                                 S2[:, s, NM + 128 * j:NM + 128 * j + 128], ident))
        nS[s] = t
        x["tb"] = (b, b2, t)

    def f3(x):
        h, i = x["h"], x["i"]
        b, b2, t = x["tb"]
        tc = slice(128 * i, 128 * i + 128)
        a = act.do(call(nc.scalar.activation, PT[:, 0:i + 1, tc],
                                          bank[b][:, 0:128 * (i + 1)].rearrange("p (j n) -> p j n", n=128),
                                          ACT.Copy), t, nPT[0])
        give(b, a)
        d = dve.do(call(nc.vector.tensor_copy, PM[:, tc], bank[b2][0:NM, 0:128]), t, nPT[0])
        give(b2, d)
        if i == 3:
            o = take()
            r = slice(64 * (h % 2), 64 * (h % 2) + 64)
            hc = slice(64 * h, 64 * h + 64)
            pe.wait(a, d, t_v)
            mm(bank[o][r, :], V[0:NM, 0, hc], PM[:, :], True, False)
            for j in range(4):
                tt = mmt(bank[o][r, 128 * j:NT], V[:, 1 + j, hc], PT[:, j, 128 * j:NT], False, j == 3)
            nPT[0] = tt
            a = act.do(call(nc.scalar.activation, HH[r, h // 2, :], bank[o][r, :], ACT.Copy), tt)
            t = dve.do(call(nc.vector.tensor_tensor, HL[r, h // 2, :], bank[o][r, :], HH[r, h // 2, :].bitcast(F32),
                                                 ALU.subtract), a)
            give(o, t)
            head[h]["out"] = t

    pe.wait((dve.sem, dve.n))
    pipeline(items, [f0, f1, f2, f3])
    t_fox = (dve.sem, dve.n)
    t_fox_pe = (pe.sem, pe.n)
    ready_o = [[head[2 * k + 1]["out"]] for k in range(4)] + [[] for _ in range(4)]

    after = [t_fox, t_fox_pe, (act.sem, act.n), (pool.sem, pool.n)]
    for e_ in (dve, act, pool, pe):
        e_.wait(*after)
    R = arena(r0, END)
    U = arena(u0, u1)
    FG = U("FG", [128, 4, NA])
    B = U("B", [128, 4, NA])
    XL2 = U("XL2", [128, 2, 4, NT])
    GT = sb("GT", [128, 4, NA], F32, u0 + 2 * 4 * NA * 4)
    OH = sb("OH", [128, 4, NT], F32, u0 + 2 * 4 * NA * 4)
    EX = R("EX", [128, 4, NT])
    QE = R("QE", [128, 4, NT])
    KD = R("KD", [128, 4, 400])
    KT = R("KT", [128, 2, 4, 128])
    AT = R("AT", [128, 4, 4, 128])
    ST = R("ST", [128, 2, 4, 128])
    MS = R("MS", [128, NA])
    EL = R("EL", [128, 4, 4])
    LB = R("LB", [128, 6, 4])
    TN = R("TN", [128, 2, NT])

    lbr = vec[:, V_LB:V_LB + 4]
    t = dve.do(call(nc.vector.tensor_tensor, LB[:, 0, :], lbr, lbr, ALU.subtract), t_vec)
    t = act.do(call(nc.scalar.activation, LB[:, 1, :], LB[:, 0, :], ACT.Exp), t)
    t = dve.do(call(nc.vector.reciprocal, LB[:, 2, :], LB[:, 1, :]), t)
    t = dve.do(call(nc.vector.tensor_tensor, LB[:, 3, :], LB[:, 1, :], LB[:, 2, :], ALU.mult), t)
    t = dve.do(call(nc.vector.tensor_tensor, LB[:, 4, :], LB[:, 3, :], LB[:, 3, :], ALU.subtract), t)
    t_lb = dve.do(call(nc.vector.tensor_scalar, LB[:, 5, :], LB[:, 4, :], -1.0, 1.0, ALU.mult, ALU.add), t)
    t = act.do(call(nc.scalar.activation, OM[:, :, :], OM[:, :, :], ACT.Sigmoid, scale=-1.0), t_om)
    dve.wait(t, t_lb)
    for h in range(4):
        t = dve.do(call(nc.vector.tensor_scalar, OM[:, h, :], OM[:, h, :], LB[:, 5, h:h + 1], None, ALU.mult))
    t_k = t
    t = dve.do(call(nc.vector.tensor_scalar, FG[:, :, :], OM[:, :, :], -1.0, 1.0, ALU.mult, ALU.add), t)
    t_f = dve.do(call(nc.vector.tensor_scalar, FG[:, :, :], FG[:, :, :], FMIN, None, ALU.max), t)
    t_g = act.do(call(nc.scalar.activation, GT[:, :, :], FG[:, :, :], ACT.Ln), t_f)
    t_q = pool.do(call(nc.gpsimd.tensor_scalar, HQ[:, :, :], HQ[:, :, :], float(128 ** -0.5), None, ALU.mult), t_hq)
    t = dve.do(call(nc.vector.memset, MS[:, :], 1.0))
    dve.wait(t)
    for c in (0, 16, 144, 272, 400):
        t = dve.do(call(nc.vector.memset, MS[:, c:c + 1], 0.0))
    dve.wait(t_g, t)
    for h in range(4):
        t_b = dve.do(call(nc.vector.tensor_tensor_scan, B[:, h, :], MS[:, :], GT[:, h, :], 0.0, ALU.mult, ALU.add))

    def every(x, n, free_n):
        return x.unsqueeze(x.ndim).broadcast_to(list(x.shape) + [n])

    ends = [15, 143, 271, 399]
    t = pool.do(call(nc.gpsimd.tensor_tensor, KD[:, :, 0:16], every(B[:, :, 15], 16, 0), B[:, :, 0:16], ALU.subtract), t_b)
    kd4 = KD[:, :, 16:400].rearrange("p h (c n) -> p h c n", n=128)
    b4 = B[:, :, 16:400].rearrange("p h (c n) -> p h c n", n=128)
    t = pool.do(call(nc.gpsimd.tensor_tensor, kd4, every(b4[:, :, :, 127], 128, 0), b4, ALU.subtract))
    t = act.do(call(nc.scalar.activation, KD[:, :, :], KD[:, :, :], ACT.Exp), t)
    t_kd = pool.do(call(nc.gpsimd.tensor_tensor, KD[:, :, :], KD[:, :, :], OM[:, :, 0:400], ALU.mult), t, t_k)
    t_el = act.do(call(nc.scalar.activation, EL[:, :, 0:3], b4[:, :, :, 127], ACT.Exp), t_b)
    t = act.do(call(nc.scalar.activation, QE[:, :, :], B[:, :, xc], ACT.Exp), t_b)
    t_qe = pool.do(call(nc.gpsimd.tensor_tensor, QE[:, :, :], QE[:, :, :], HQ[:, :, :], ALU.mult), t, t_q)
    t_at = pool.do(call(nc.gpsimd.memset, AT[:, :, :, :], 0.0))

    xfree = [None, None]
    exfree = None
    atok = t_at

    def level(l, lhs, rhs, tok, xs):
        nonlocal atok
        pe.wait(tok)
        for c in range(4):
            b = take()
            for h in range(4):
                n = slice(128 * c, 128 * c + 128)
                t = mmt(bank[b][:, 128 * h:128 * h + 128], lhs[:, h, n], rhs[:, h, n], True, True)
            m = msk[:, l, :].unsqueeze(1).broadcast_to([128, 4, 128])
            atok = dve.do(call(nc.vector.copy_predicated, 
                AT[:, c, :, :], m, bank[b][:, :].rearrange("p (h n) -> p h n", n=128)), t, atok, t_msk)
            give(b, atok)
        for x in xs:
            xfree[x] = t

    def pairs(x, t):
        return x.rearrange("p h (n t) -> p h n t", t=2)[:, :, :, t]

    X0, X1 = XL2[:, 0], XL2[:, 1]
    omx, fgx, bx = OM[:, :, xc], FG[:, :, xc], B[:, :, xc]
    dve.wait(t_b, t_q)
    ex0 = EX[:, :, 0:256]
    t1 = dve.do(call(nc.vector.reciprocal, ex0, pairs(fgx, 1)))
    dve.do(call(nc.vector.tensor_copy, pairs(X0, 0), pairs(omx, 0)), t1)
    t = dve.do(call(nc.vector.tensor_tensor, pairs(X0, 1), pairs(omx, 1), ex0, ALU.mult), t1)
    exfree = t
    pool.do(call(nc.gpsimd.tensor_copy, pairs(X1, 0), pairs(HQ[:, :, :], 0)), t_b, t_q)
    t2 = pool.do(call(nc.gpsimd.tensor_tensor, pairs(X1, 1), pairs(HQ[:, :, :], 1), pairs(fgx, 1), ALU.mult))
    pe.wait(t)
    level(0, X0, X1, t2, [0, 1])

    def halves(x, n, t):
        return x.rearrange("p h (b t n) -> p h b t n", t=2, n=n)[:, :, :, t, :]

    for l, n in enumerate(LEVELS):
        mid = halves(bx, n, 0)[:, :, :, n - 1]
        midb = every(mid, n, 0)
        X = XL2[:, l % 2]
        a = pool.do(call(nc.gpsimd.tensor_tensor, halves(EX[:, :, :], n, 0), midb, halves(bx, n, 0),
                                                           ALU.subtract), exfree)
        d = dve.do(call(nc.vector.tensor_tensor, halves(EX[:, :, :], n, 1), halves(bx, n, 1), midb,
                                                          ALU.subtract), exfree)
        x = act.do(call(nc.scalar.activation, EX[:, :, :], EX[:, :, :], ACT.Exp), a, d)
        a = pool.do(call(nc.gpsimd.tensor_tensor, halves(X, n, 0), halves(EX[:, :, :], n, 0),
                                                        halves(omx, n, 0), ALU.mult), x, xfree[l % 2])
        d = dve.do(call(nc.vector.tensor_tensor, halves(X, n, 1), halves(EX[:, :, :], n, 1),
                                                       halves(HQ[:, :, :], n, 1), ALU.mult), x, xfree[l % 2])
        pool.wait(d, a)
        dve.wait(a, d)
        pe.wait(a)
        level(l + 1, X, X, d, [l % 2])

    ktf = [None, None]
    stt = [None, None]
    t_oh = xfree[0]
    for c in range(5):
        n0, n = (0, 16) if c == 0 else (NM + 128 * (c - 1), 128)
        if c >= 1:
            b = take()
            pe.wait(t_qe, atok, stt[c % 2], t_v2)
            for h in range(4):
                o = bank[b][:, 128 * h:128 * h + 128]
                mm(o, ST[:, c % 2, h, :], QE[:, h, n0 - NM:n0 - NM + 128], True, False)
                t = mmt(o, V2[:, c, 128 * h:128 * h + 128], AT[:, c - 1, h, :], False, True)
            sread = t
            t_o = dve.do(call(nc.vector.tensor_copy, OH[:, :, 128 * (c - 1):128 * c],
                                                           bank[b][:, :].rearrange("p (h n) -> p h n", n=128)),
                         t, xfree[0], xfree[1])
            give(b, t_o)
        if c == 4:
            break
        b = take()
        pe.wait(t_kd, t_cst)
        for h in range(4):
            t = pe.do(call(nc.tensor.transpose, bank[b][0:n, 128 * h:128 * h + 128],
                                                                  KD[:, h, n0:n0 + n], ident))
        a = act.do(call(nc.scalar.activation, KT[0:n, c % 2, :, :],
                                                        bank[b][0:n, :].rearrange("p (h n) -> p h n", n=128),
                                                        ACT.Copy), t, ktf[c % 2])
        give(b, a)
        b = take()
        pe.wait(a, t_v2)
        for h in range(4):
            t = mmt(bank[b][:, 128 * h:128 * h + 128], KT[0:n, c % 2, h, :], V2[0:n, c, 128 * h:128 * h + 128],
                    True, True)
        ktf[c % 2] = t
        if c == 0:
            s = dve.do(call(nc.vector.tensor_copy, ST[:, 1, :, :], bank[b][:, :].rearrange("p (h n) -> p h n", n=128)),
                       t)
        else:
            dve.wait(t, t_el, stt[c % 2], sread)
            for h in range(4):
                s = dve.do(call(nc.vector.scalar_tensor_tensor, 
                    ST[:, (c + 1) % 2, h, :], ST[:, c % 2, h, :], EL[:, h, c - 1:c],
                    bank[b][:, 128 * h:128 * h + 128], ALU.mult, ALU.add))
        stt[(c + 1) % 2] = s
        give(b, s)

    def head_norm(src, dsth, wcol, tok, gate, tmp, wtok, free_=()):
        a = None
        ts = []
        rsf = [None, None]
        for h in range(4):
            q = tmp[:, h % 2, :]
            a = pool.do(call(nc.gpsimd.tensor_tensor, q, src[:, h, :], src[:, h, :], ALU.mult), tok, rsf[h % 2])
            b = take()
            t = mmt(bank[b][:, :], ones[:, :], q, True, True, a)
            a = act.do(call(nc.scalar.activation, q, bank[b][:, :], ACT.Sqrt, bias=eps[:, :], scale=1.0 / 128), t)
            give(b, a)
            t = dve.do(call(nc.vector.reciprocal, q, q), a)
            t = dve.do(call(nc.vector.scalar_tensor_tensor, src[:, h, :], src[:, h, :], wcol, q, ALU.mult,
                                                                  ALU.mult), t, wtok)
            rsf[h % 2] = t
            if gate is not None:
                t = dve.do(call(nc.vector.tensor_tensor, src[:, h, :], src[:, h, :], gate[:, h, :], ALU.mult), t)
            ts.append([hilo(HH[:, dsth + h, :], HL[:, dsth + h, :], src[:, h, :], None, t, *free_)])
        return ts

    ready_o[4:] = head_norm(OH, 4, vec[:, V_HN:V_HN + 1], t_o, HG, TN, t_hg, [t_qe])

    nocare = [(dve.sem, dve.n), (act.sem, act.n), (pool.sem, pool.n), (pe.sem, pe.n)]

    def fence():
        toks = [(x.sem, x.n) for x in (pe, act, dve, pool) if x.n]
        for x in (pe, act, dve, pool):
            x.wait(*toks)

    fence()
    for g in range(2):
        lin(8, 4, HH, HL, ready_o, residual(4 * g, V_FFN), n0=0)

    def rms_hook():
        inv_rms([(NM, NT)], [], [])

    F = arena(t0, END)
    T = F("T", [128, 12, NT])
    tfree = [None] * 12
    tn = [0]

    def temp():
        i = tn[0] % 12
        tn[0] += 1
        return T[:, i, :], i

    ready_h = [[] for _ in range(8)]

    f0_ = 0
    first = True
    for ci, nh in enumerate(HIDDEN):
        for j in range(0, nh, 2):
            store = {}

            def evac(m, p, tok, j=j):
                if m < 2:
                    x, i = temp()
                    y, i2 = temp()
                    a = dve.do(call(nc.vector.tensor_tensor, x, p, RB[:, xc], ALU.mult), tok, nm_.rb, tfree[i])
                    s = act.do(call(nc.scalar.activation, y, x, ACT.Silu), a, tfree[i2])
                    tfree[i] = s
                    store[m] = (y, i2, s)
                    return a
                y, i2, s = store[m - 2]
                x, i = temp()
                k = j + m - 2
                a = dve.do(call(nc.vector.tensor_tensor, x, p, RB[:, xc], ALU.mult), tok, nm_.rb, tfree[i])
                t = dve.do(call(nc.vector.tensor_tensor, x, x, y, ALU.mult), a, s)
                tfree[i2] = t
                t = hilo(HH[:, k, :], HL[:, k, :], x, None, t)
                ready_h[k] = [t]
                tfree[i] = t
                return a
            lin(8, 4, UH, UL, ready, evac, hook=rms_hook if first else None)
            first = False
        lastc = ci == len(HIDDEN) - 1
        for g in range(2):
            lin(nh, 4, HH, HL, ready_h, residual(4 * g, None, last=lastc), n0=0)

    def between(w_out_, w_next):
        rms_hook()
        for k in range(8):
            t = dve.do(call(nc.vector.scalar_tensor_tensor, H[:, k, xc], H[:, k, xc],
                                                             vec[:, w_out_ + k:w_out_ + k + 1],
                                                             RB[:, xc], ALU.mult, ALU.mult), nm_.rb, nm_.acc)
            h_tok[k] = t
            if w_next is not None:
                ready[k] = [hilo(UH[:, k, xc], UL[:, k, xc], H[:, k, xc],
                                 vec[:, w_next + k:w_next + k + 1], t)]
                square_in(k, H[:, k, xc], NM, NT, t)

    between(V_FIN, V_MIX2)

    fence()
    G0 = arena(t0, END)
    KM = G0("KM", [128, 8, 256])
    VM = G0("VM", [128, 2, 1024])
    g0 = t0 + 16384
    G = arena(g0, END)
    Q = G("Q3", [128, 4, NT])
    K = G("K3", [128, 4, NT])
    V = G("V3", [128, 4, NT])
    YU = G("YU", [128, 4, NT])
    LA = G("LA", [64, 2])
    LM = G("LM", [128, 4])
    small = G("small3", [128, 64])
    BH = G("BH", [128, 4, NT])

    GB = sb("GB", [128, 4, 384], F32, h0)
    s_b = new_sem("s_b")
    for h in range(4):
        b = take()
        rel = vec[0:32, V_REL + h:V_REL + h + 1].broadcast_to([32, 128])
        t = mmt(bank[b][:, 0:384], rel, cst[0:32, C_ONEHOT:C_ONEHOT + 384], True, True, t_cst, t_vec)
        t = act.do(call(nc.scalar.activation, GB[:, h, :], bank[b][:, 0:384], ACT.Copy), t)
        give(b, t)
    sp.wait(t)
    load(scratch, GB[:, :, :], s_b)
    sp.wait((s_b, 16))
    skew = bass.AP(scratch.tensor, 127, [[1535, 128], [384, 4], [1, 256]])
    load(BH[:, :, 256:512], skew, s_b)
    far = GB[:, :, 0:1].broadcast_to([128, 4, 256])
    dve.do(call(nc.vector.tensor_copy, BH[:, :, 0:256], far), t)
    diag = BH[:, :, 384:512]
    t_bh = dve.do(call(nc.vector.tensor_tensor, diag, diag, causal.unsqueeze(1).broadcast_to([128, 4, 128]), ALU.add),
                  (s_b, 32), t_cst)

    lv = lambda i: vec[0:64, V_LAM + i:V_LAM + i + 1]
    dve.do(call(nc.vector.tensor_tensor, LA[:, 0:1], lv(0), lv(1), ALU.mult), t_vec)
    t = dve.do(call(nc.vector.tensor_tensor, LA[:, 1:2], lv(2), lv(3), ALU.mult))
    b = take()
    t = mmt(bank[b][:, 0:2], ones[0:64, :], LA[:, :], True, True, t)
    t = act.do(call(nc.scalar.activation, LM[:, 0:2], bank[b][:, 0:2], ACT.Exp), t)
    give(b, t)
    t = dve.do(call(nc.vector.tensor_tensor, LM[:, 2:3], LM[:, 1:2], LM[:, 0:1], ALU.subtract), t)
    t_lm = dve.do(call(nc.vector.tensor_scalar, LM[:, 3:4], LM[:, 2:3], -LAMBDA_INIT, None, ALU.add), t)
    t_sg = dve.do(call(nc.vector.tensor_scalar, LM[:, 0:1], vec[:, V_SUB:V_SUB + 1], 1.0 - LAMBDA_INIT, None, ALU.mult), t_lm)

    lin(8, 4, UH, UL, ready, times_r(Q, 0.125), hook=lambda: inv_rms([(NM, NT)], CH, []))
    lin(8, 4, UH, UL, ready, times_r(K))
    lin_tok(8, UH, UL, ready, CH, rows_r(V, 1))
    t_v = (act.sem, act.n)
    lin(8, 4, UH, UL, ready, times_r(YU))
    fence()

    PWT = G("PWT", [128, 3, NT])
    U = arena(u0, u1)
    S4 = U("S4", [128, 2, 2, NT])
    PT = U("PT3", [128, 4, NT])
    OH = U("OH3", [128, 4, NT])
    TN = U("TN3", [128, 2, NT])
    PW = U("PW", [128, 4, 128])
    s_pw = new_sem("s_pw")
    sp.wait((pe.sem, pe.n))
    load(PW[:, :, :], A["pool_w"].rearrange("g c d -> c g d"), s_pw)
    pfree = None
    for g, w in enumerate(WINDOWS):
        src = YU[:, g, :]
        d, t = 1, None
        i = 0
        while d < w:
            dst = PWT[:, i % 2, :]
            pool.do(call(nc.gpsimd.tensor_copy, dst[:, 0:d], src[:, 0:d]), t, pfree)
            t = pool.do(call(nc.gpsimd.tensor_tensor, dst[:, d:NT], src[:, d:NT], src[:, 0:NT - d],
                                                                         ALU.add))
            src = dst
            d *= 2
            i += 1
        p = PWT[:, 2, :]
        u = YU[:, g, :]
        t = dve.do(call(nc.vector.scalar_tensor_tensor, p[:, w:NT], src[:, w:NT], 1.0 / w, u[:, w:NT],
                                                                  ALU.mult, ALU.subtract), t, pfree)
        ci = cst[:, C_CINV + 16 * g:C_CINV + 16 * g + w]
        t2 = dve.do(call(nc.vector.tensor_tensor, p[:, 0:w], src[:, 0:w], ci, ALU.mult), t_cst)
        t = dve.do(call(nc.vector.tensor_tensor, p[:, 0:w], p[:, 0:w], u[:, 0:w], ALU.subtract), t2)
        b = take()
        t = mmt(bank[b][:, :], PW[:, g, :], p, True, True, t, (s_pw, 16))
        pfree = t
        o = TN[:, g % 2, :]
        if g == 0:
            tnf = [None, None]
        t = dve.do(call(nc.vector.tensor_scalar, o, bank[b][:, :], vec[:, V_PS + g:V_PS + g + 1], None,
                                                            ALU.mult), t, tnf[g % 2])
        give(b, t)
        tnf[g % 2] = hilo(HH[:, 4 + g, :], HL[:, 4 + g, :], o, None, t)
        ready_h[4 + g] = [tnf[g % 2]]

    items = [dict(h=h, i=i, n=h * 4 + i) for h in range(4) for i in range(4)]
    sf = [None, None]
    smf = [None] * 4
    ptf = [None]
    t_oh = []

    def d0(x):
        h, i = x["h"], x["i"]
        ns = 128 * (i + 1)
        x["b"] = [take(), take()]
        for j in range(2):
            r = slice(64 * j, 64 * j + 64)
            x["t"] = mmt(bank[x["b"][j]][:, 0:ns], Q[r, h, 128 * i:128 * i + 128], K[r, h, 0:ns], True, True)

    def d1(x):
        h, i, s = x["h"], x["i"], x["n"] % 2
        ns = 128 * (i + 1)
        m = small[:, 8 * (x["n"] % 4):8 * (x["n"] % 4) + 8]
        x["e"] = []
        for j in range(2):
            S = S4[:, s, j, 0:ns]
            b = x["b"][j]
            t = dve.do(call(nc.vector.tensor_tensor, S, bank[b][:, 0:ns], BH[:, h, NT - ns:NT], ALU.add),
                       x["t"], sf[s], t_bh)
            give(b, t)
            t = dve.do(call(nc.vector.tensor_reduce, m[:, j:j + 1], S, AX.X, ALU.max, negate=True), t,
                       smf[x["n"] % 4])
            x["e"].append(act.do(call(nc.scalar.activation, S, S, ACT.Exp, bias=m[:, j:j + 1],
                                                                  accum_out=m[:, 2 + j:3 + j]), t))

    def d2(x):
        h, i, s = x["h"], x["i"], x["n"] % 2
        ns = 128 * (i + 1)
        m = small[:, 8 * (x["n"] % 4):8 * (x["n"] % 4) + 8]
        A_, B_ = S4[:, s, 0, 0:ns], S4[:, s, 1, 0:ns]
        t = dve.do(call(nc.vector.reciprocal, m[:, 4:6], m[:, 2:4]), *x["e"])
        t1 = dve.do(call(nc.vector.tensor_scalar, A_, A_, m[:, 4:5], None, ALU.mult), t)
        t2 = dve.do(call(nc.vector.tensor_tensor, m[:, 6:7], m[:, 5:6], LM[:, 3:4], ALU.mult), t_lm, t)
        t = dve.do(call(nc.vector.scalar_tensor_tensor, A_, B_, m[:, 6:7], A_, ALU.mult, ALU.add), t1, t2)
        smf[x["n"] % 4] = t
        b = take()
        pe.wait(t)
        for j in range(i + 1):
            t = pe.do(call(nc.tensor.transpose, bank[b][:, 128 * j:128 * j + 128],
                                                 S4[:, s, 0, 128 * j:128 * j + 128], ident))
        sf[s] = t
        x["tb"] = (b, t)

    def d3(x):
        h, i = x["h"], x["i"]
        b, t = x["tb"]
        a = act.do(call(nc.scalar.activation, PT[:, 0:i + 1, 128 * i:128 * i + 128],
                                          bank[b][:, 0:128 * (i + 1)].rearrange("p (j n) -> p j n", n=128),
                                          ACT.Copy), t, ptf[0])
        give(b, a)
        if i == 3:
            o = take()
            pe.wait(a, t_v)
            for j in range(4):
                t = mmt(bank[o][:, 128 * j:NT], V[:, j, 128 * h:128 * h + 128], PT[:, j, 128 * j:NT], j == 0, j == 3)
            ptf[0] = t
            a = act.do(call(nc.scalar.activation, OH[:, h, :], bank[o][:, :], ACT.Copy), t)
            give(o, a)
            t_oh.append(a)

    pipeline(items, [d0, d1, d2, d3])
    pool.wait(*tnf)
    ready_h[0:4] = head_norm(OH, 0, LM[:, 0:1], t_oh[-1], None, TN, t_sg, tnf)
    fence()
    for g in range(2):
        lin(8, 4, HH, HL, ready_h, residual(4 * g, V_XA2), n0=0)

    s_m = new_sem("s_m")

    def cross(l):
        nonlocal ready_h
        fence()
        G = arena(g0, END)
        MT = G(f"MT{l}", [128, 8, 256])
        MH = G(f"MH{l}", [128, 8, 256], F32R)
        ML = G(f"ML{l}", [128, 8, 256], F32R)
        AM = G(f"AM{l}", [128, 2, 256])
        RM = G(f"RM{l}", [128, 2, 256])
        RQ = G(f"RQ{l}", [128, 4])
        sp.wait((pe.sem, pe.n), (dve.sem, dve.n), (act.sem, act.n), (pool.sem, pool.n))
        load(MT[:, :, :], A["memT"].rearrange("(k p) n -> p k n", p=128), s_m)
        landed = (s_m, 16 * (l + 1))
        rm = []
        acc = None
        for k in range(8):
            rm.append([hilo(MH[:, k, :], ML[:, k, :], MT[:, k, :], vec[:, V_MEM + k:V_MEM + k + 1], landed)])
            if k == 0:
                acc = pool.do(call(nc.gpsimd.tensor_tensor, AM[:, 0, :], MT[:, 0, :], MT[:, 0, :], ALU.mult), landed)
            else:
                t = pool.do(call(nc.gpsimd.tensor_tensor, AM[:, 1, :], MT[:, k, :], MT[:, k, :], ALU.mult), acc)
                acc = pool.do(call(nc.gpsimd.tensor_tensor, AM[:, 0, :], AM[:, 0, :], AM[:, 1, :], ALU.add), t)
        tok = {}

        def mem_rms():
            b = take()
            mmt(bank[b][:, 0:256], ones[:, :], AM[:, 0, :], True, True, acc)
            for i in range(2):
                t = mmt(bank[b][:, 256 + i:257 + i], AM[:, 0, 128 * i:128 * i + 128], ones[:, 0:1], True, True)
            a = act.do(call(nc.scalar.activation, RM[:, 0, :], bank[b][:, 0:256], ACT.Sqrt, bias=eps[:, :],
                                              scale=1.0 / 1024), t)
            a2 = act.do(call(nc.scalar.activation, RQ[:, 0:2], bank[b][:, 256:258], ACT.Sqrt, bias=eps[:, :],
                                               scale=1.0 / 1024))
            give(b, a2)
            tok["r"] = dve.do(call(nc.vector.reciprocal, RM[:, 1, :], RM[:, 0, :]), a)
            tok["c"] = dve.do(call(nc.vector.reciprocal, RQ[:, 2:4], RQ[:, 0:2]), a2)

        for g in range(2):
            def evac(m, p, t, g=g):
                return dve.do(call(nc.vector.tensor_tensor, KM[:, 4 * g + m, :], p, RM[:, 1, :], ALU.mult), t, tok["r"])
            lin(8, 4, MH, ML, rm, evac, n0=0, n=256, hook=mem_rms if g == 0 else None)
        for g in range(2):
            def evac(i, p, t, g=g):
                return act.do(call(nc.scalar.activation, VM[:, i, 512 * g:512 * g + 512], p[:, :], ACT.Copy,
                                                     scale=RQ[:, 2 + i:3 + i]), t, tok["c"])
            lin_tok(8, MH, ML, rm, [0, 128], evac)
        fence()
        G = arena(g0, END)
        QX = G(f"QX{l}", [128, 8, NT])
        S = G(f"SX{l}", [128, 4, 2, 256])
        PT = G(f"PX{l}", [128, 2, 4, NT])
        small = G(f"small{l}x", [128, 64])

        for g in range(2):
            def evac(m, p, t, g=g):
                return dve.do(call(nc.vector.scalar_tensor_tensor, QX[:, 4 * g + m, :], p, 1.0 / 16, RB[:, xc], ALU.mult,
                                                               ALU.mult), t, nm_.rb)
            lin(8, 4, UH, UL, ready, evac, hook=rms_hook if g == 0 else None)
        items = [dict(h=h, i=i, n=4 * h + i) for h in range(2) for i in range(4)]
        sf = [None] * 4
        mf = [None] * 4
        ptf = [None, None]
        qt = (dve.sem, dve.n)
        pe.wait(qt, (act.sem, act.n))

        def c0(x):
            b = take()
            for j in range(2):
                for d in range(2):
                    k = 4 * x["h"] + 2 * j + d
                    t = mmt(bank[b][:, 256 * j:256 * j + 256], QX[:, k, 128 * x["i"]:128 * x["i"] + 128],
                            KM[:, k, :], d == 0, d == 1)
            x["b"], x["t"] = b, t

        def c1(x):
            s = x["n"] % 4
            b = x["b"]
            m = small[:, 8 * s:8 * s + 8]
            t = dve.do(call(nc.vector.tensor_reduce, m[:, 0:2], bank[b][:, :].rearrange("p (j n) -> p j n", j=2), AX.X,
                                                 ALU.max, negate=True), x["t"], mf[s])
            for j in range(2):
                x["e"] = act.do(call(nc.scalar.activation, S[:, s, j, :], bank[b][:, 256 * j:256 * j + 256], ACT.Exp,
                                                            bias=m[:, j:j + 1], accum_out=m[:, 2 + j:3 + j]),
                                t, sf[s])
            give(b, x["e"])

        def c2(x):
            s = x["n"] % 4
            m = small[:, 8 * s:8 * s + 8]
            t = dve.do(call(nc.vector.reciprocal, m[:, 4:6], m[:, 2:4]), x["e"])
            dve.wait(t)
            for j in range(2):
                t = dve.do(call(nc.vector.tensor_scalar, S[:, s, j, :], S[:, s, j, :], m[:, 4 + j:5 + j], None,
                                                          ALU.mult))
            mf[s] = t
            b = take()
            pe.wait(t)
            for j in range(4):
                t = pe.do(call(nc.tensor.transpose, bank[b][:, 128 * j:128 * j + 128],
                                                     S[:, s, j // 2, 128 * (j % 2):128 * (j % 2) + 128], ident))
            sf[s] = t
            x["tb"] = (b, t)

        def c3(x):
            b, t = x["tb"]
            h, i = x["h"], x["i"]
            a = act.do(call(nc.scalar.activation, PT[:, h % 2, :, 128 * i:128 * i + 128],
                                              bank[b][:, :].rearrange("p (j n) -> p j n", n=128), ACT.Copy), t,
                       ptf[h % 2])
            give(b, a)
            if i == 3:
                pe.wait(a)
                for d in range(4):
                    o = take()
                    k = 4 * h + d
                    for mb in range(2):
                        t = mmt(bank[o][:, :], VM[:, mb, 128 * k:128 * k + 128], PT[:, h % 2, 2 * (d // 2) + mb, :],
                                mb == 0, mb == 1)
                    t = hilo(HH[:, k, :], HL[:, k, :], bank[o][:, :], None, t)
                    give(o, t)
                    ready_h[k] = [t]
                ptf[h % 2] = t

        pipeline(items, [c0, c1, c2, c3])
        for g in range(2):
            lin(8, 4, HH, HL, ready_h, residual(4 * g, V_MLP2 + 8 * l), n0=0)

    def mlp(l, wnext):
        fence()
        F = arena(g0, END)
        T = F(f"TM{l}", [128, 8, NT])
        tf = [None] * 8
        n = 0
        first = True
        for c in range(4):
            for g in range(2):
                def evac(m, p, tok, g=g):
                    nonlocal n
                    i, j = n % 8, (n + 1) % 8
                    n += 2
                    x, y = T[:, i, :], T[:, j, :]
                    k = 4 * g + m
                    a = dve.do(call(nc.vector.scalar_tensor_tensor, x, p, 0.0, RB[:, xc], ALU.max, ALU.mult), tok, nm_.rb,
                               tf[i])
                    t = act.do(call(nc.scalar.activation, y, x, ACT.Square), a, tf[j])
                    tf[i] = t
                    tf[j] = hilo(HH[:, k, :], HL[:, k, :], y, None, t)
                    ready_h[k] = [tf[j]]
                    return a
                lin(8, 4, UH, UL, ready, evac, hook=rms_hook if first else None)
                first = False
            for g in range(2):
                lin(8, 4, HH, HL, ready_h, residual(4 * g, wnext, last=c == 3), n0=0)

    cross(0)
    mlp(0, V_MIX2 + 8)

    fence()
    F = arena(g0, END)
    T = F("TC", [128, 16, NT])
    tf = [None] * 16
    n_ = [0]

    def tmp():
        i = n_[0] % 16
        n_[0] += 1
        return T[:, i, :], i

    for j in range(8):
        got = {}

        def evac(m, p, tok, j=j):
            x, i = tmp()
            a = dve.do(call(nc.vector.tensor_tensor, x, p, RB[:, xc], ALU.mult), tok, nm_.rb, tf[i])
            got[m] = (x, i, a)
            if m == 2:
                (bx_, ib, tb), (cx, ic, tc), (xx, ix, tx) = got[0], got[1], got[2]
                t = dve.do(call(nc.vector.tensor_tensor, cx, cx, xx, ALU.mult), tc, tx)
                tf[ix] = t
                y, iy = tmp()
                w = [vec[:, V_CONV + 8 * q + j:V_CONV + 8 * q + j + 1] for q in range(3)]
                t2 = act.do(call(nc.scalar.activation, y, cx, ACT.Copy, scale=w[2]), t, tf[iy])
                t2 = dve.do(call(nc.vector.scalar_tensor_tensor, y[:, 1:NT], cx[:, 0:NT - 1], w[1], y[:, 1:NT], ALU.mult,
                                                             ALU.add), t2)
                t2 = dve.do(call(nc.vector.scalar_tensor_tensor, y[:, 2:NT], cx[:, 0:NT - 2], w[0], y[:, 2:NT], ALU.mult,
                                                             ALU.add), t2)
                tf[ic] = t2
                t2 = dve.do(call(nc.vector.tensor_tensor, y, y, bx_, ALU.mult), t2, tb)
                tf[ib] = t2
                tf[iy] = hilo(HH[:, j, :], HL[:, j, :], y, None, t2)
                ready_h[j] = [tf[iy]]
            return a
        lin(8, 3, UH, UL, ready, evac, hook=rms_hook if j == 0 else None)
    for g in range(2):
        lin(8, 4, HH, HL, ready_h, residual(4 * g, V_XA2 + 8), n0=0)
    cross(1)
    mlp(1, None)
    rms_hook()
    s_o = new_sem("s_o")
    for k in range(8):
        t = dve.do(call(nc.vector.scalar_tensor_tensor, H[:, k, xc], H[:, k, xc],
                                                         vec[:, V_FIN2 + k:V_FIN2 + k + 1],
                                                         RB[:, xc], ALU.mult, ALU.mult), nm_.rb, nm_.acc)
        sp.wait(t)
        load(out[128 * k:128 * k + 128, :], H[:, k, xc], s_o)
    sp.wait((s_o, 128), (s_b, 32))
    assert st.pos == len(tiles), (st.pos, len(tiles))

    block = nc.Block()
    with block:
        block.sync(lambda e: sp.run(e))
        block.scalar(lambda e: act.run(e))
        block.vector(lambda e: dve.run(e))
        block.gpsimd(lambda e: pool.run(e))
        block.tensor(lambda e: pe.run(e))
    for cm in reversed(held):
        cm.__exit__(None, None, None)


def buckets():
    import math
    out = []
    for n in range(256):
        if n < 16:
            out.append(n)
        else:
            out.append(min(16 + int(math.log(n / 16) / math.log(8) * 16 + 1e-9), 31))
    return out


def constants():
    c = np.zeros((128, NCONST), np.float32)
    c[:, C_ID:C_ID + 128] = np.eye(128)
    i = np.arange(128)
    c[:, C_CAUSAL:C_CAUSAL + 128] = np.where(i[None, :] <= i[:, None], 0.0, -1e30)
    bk = buckets()
    for j in range(384):
        c[bk[max(255 - j, 0)], C_ONEHOT + j] = 1.0
    for h in range(8):
        c[h, C_SEL + 128 * h:C_SEL + 128 * h + 128] = -1.0
    for g, w in enumerate(WINDOWS):
        for t in range(w):
            c[:, C_CINV + 16 * g + t] = 1.0 / min(t + 1, w)
    m = np.zeros((128, 7, 128), np.float32)
    s, t = i[:, None], i[None, :]
    m[:, 0] = (s // 2 == t // 2) & (s <= t)
    for l, n in enumerate(LEVELS):
        m[:, l + 1] = (s // (2 * n) == t // (2 * n)) & (s % (2 * n) < n) & (t % (2 * n) >= n)
    return c, m.reshape(128, 7 * 128)


def kernel(**inputs):
    import concourse.bacc as bacc
    from concourse.bass_utils import run_bass_kernel_spmd as run

    I = {k: np.asarray(v) for k, v in inputs.items()}
    w_in = I["w_in"][0]
    ff = np.zeros((1024, 128), np.float32)
    ff[:, 0:8] = w_in[:, 1536:1544]
    mats = {"w_in": w_in[:, 0:1536], "ff": ff, "hgrn": w_in[:, 1544:], "w_out": I["w_out"][0],
            "w_ffn_gate": I["w_ffn_gate"][0], "w_ffn_up": I["w_ffn_up"][0], "w_ffn_down": I["w_ffn_down"][0],
            "ab_w_in_2": I["ab_w_in_2"][0], "ab_w_out_2": I["ab_w_out_2"][0], "conv_w_in_2": I["conv_w_in_2"][0],
            "conv_w_out_2": I["conv_w_out_2"][0]}
    for n in ("xattn_wkv_2", "xattn_wq_2", "xattn_wo_2", "mlp_w1_2", "mlp_w2_2"):
        for l in range(2):
            mats[f"{n}.{l}"] = I[n][l]
    tiles = [t for lot in plan() for t in lot]
    stream = np.empty((len(tiles) // 8, 128, 1024), np.float32)
    for i, (n, k, c) in enumerate(tiles):
        stream[i // 8, :, 128 * (i % 8):128 * (i % 8) + 128] = mats[n][128 * k:128 * k + 128, 128 * c:128 * c + 128]

    vecs = np.zeros((128, NVEC), np.float32)

    def put(col, v):
        vecs[:, col:col + v.size // 128] = v.reshape(-1, 128).T

    put(V_MIX, I["norm_mix_w"][0])
    put(V_FFN, I["norm_ffn_w"][0])
    put(V_FIN, I["norm_final_w"])
    put(V_MEM, I["mem_norm_g_2"])
    for l in range(2):
        put(V_MIX2 + 8 * l, I["norm_mix_g_2"][l])
        put(V_XA2 + 8 * l, I["norm_xattn_g_2"][l])
        put(V_MLP2 + 8 * l, I["norm_mlp_g_2"][l])
    put(V_FIN2, I["final_norm_g_2"])
    put(V_LB, I["hgrn_lb_raw"][0])
    put(V_HN, I["hgrn_norm_w"][0])
    put(V_SUB, I["subln_g_2"][0])
    put(V_PS, I["pool_scale_2"][0])
    for q in range(3):
        put(V_CONV + 8 * q, I["conv_w_2"][0, q])
    vecs[0:8, V_FB] = I["fox_f_bias"][0]
    for i, n in enumerate(("lambda_q1_2", "lambda_k1_2", "lambda_q2_2", "lambda_k2_2")):
        vecs[0:64, V_LAM + i] = I[n][0]
    vecs[0:32, V_REL:V_REL + 4] = I["rel_bias_2"]
    consts, masks = constants()
    arrays = {
        "hT": np.ascontiguousarray(np.concatenate([I["meta"], I["x"][0]], 0).T),
        "memT": np.ascontiguousarray(I["mem_2"][0].T),
        "stream": stream, "vecs": vecs, "consts": consts, "masks": masks,
        "pool_w": np.ascontiguousarray(I["pool_w_2"][0]),
    }
    nc = bacc.Bacc("TRN2", target_bir_lowering=False, num_devices=1)
    A = {n: nc.dram_tensor(n, a.shape, mybir.dt.from_np(a.dtype), kind="ExternalInput").ap()
         for n, a in arrays.items()}
    out = nc.dram_tensor("outT", (1024, NT), F32, kind="ExternalOutput").ap()
    scratch = nc.dram_tensor("skew", (128, 4, 384), F32, kind="Internal").ap()
    build(nc, A, out, scratch)
    r = run(nc, [arrays], core_ids=[0])
    return np.ascontiguousarray(np.asarray(r.results[0]["outT"]).T)[None]
```

```python
import concourse.bass as bass
from concourse import mybir
from collections import deque
import numpy as np

F32 = mybir.dt.float32
F32R = mybir.dt.float32r
U8 = mybir.dt.uint8
ACT = mybir.ActivationFunctionType
ALU = mybir.AluOpType
AX = mybir.AxisListType

NT = 512
NM = 16
NA = NT + NM
EPS = 1e-6
FMIN = float(np.exp(-30.0))
LAMBDA_INIT = 0.2
WINDOWS = (2, 4, 8, 16)
LEVELS = (2, 4, 8, 16, 32, 64)

V_MIX, V_FFN, V_FIN, V_MEM = 0, 8, 16, 24
V_MIX2, V_XA2, V_MLP2, V_FIN2 = 32, 48, 64, 80
V_LB, V_HN, V_SUB, V_PS, V_CONV, V_FB, V_LAM, V_REL = 88, 92, 93, 94, 98, 122, 123, 127
NVEC = 131
C_ID, C_CAUSAL, C_ONEHOT, C_CINV = 0, 128, 256, 640
NCONST = 704

HIDDEN = (8, 8, 6)
ORDER2 = (4, 5, 6, 7, 0, 1, 2, 3)


def plan():
    out = []

    def lot(name, ks, cols):
        out.append([(name, k, c) for k in ks for c in cols])

    def wide(name, ks, c0, n, w=4):
        for c in range(c0, c0 + n, w):
            lot(name, ks, range(c, c + w))

    k8 = range(8)
    wide("w_in", k8, 0, 8)
    lot("ff", k8, [0])
    wide("w_in", k8, 8, 4)
    wide("hgrn", k8, 8, 4)
    wide("hgrn", k8, 0, 4)
    wide("hgrn", k8, 4, 4, 2)
    wide("hgrn", k8, 12, 4)
    wide("xattn_wkv_2.0", k8, 0, 16)
    wide("w_out", k8, 0, 8)
    f0 = 0
    for nh in HIDDEN:
        for j in range(f0, f0 + nh, 2):
            out.append([(n, k, c) for k in range(8)
                        for n, c in (("w_ffn_gate", j), ("w_ffn_gate", j + 1), ("w_ffn_up", j), ("w_ffn_up", j + 1))])
        wide("w_ffn_down", range(f0, f0 + nh), 0, 8)
        f0 += nh
    wide("ab_w_in_2", k8, 0, 16)
    wide("xattn_wkv_2.1", k8, 0, 16)
    wide("ab_w_out_2", ORDER2, 0, 8)
    for l in range(2):
        if l == 1:
            for j in range(8):
                lot("conv_w_in_2", k8, [j, 8 + j, 16 + j])
            wide("conv_w_out_2", k8, 0, 8)
        wide(f"xattn_wq_2.{l}", k8, 0, 8)
        wide(f"xattn_wo_2.{l}", k8, 0, 8)
        for c in range(4):
            wide(f"mlp_w1_2.{l}", k8, 8 * c, 8)
            wide(f"mlp_w2_2.{l}", range(8 * c, 8 * c + 8), 0, 8)
    return out


def call(fn, *args, **kwargs):
    return lambda e: fn(*args, **kwargs)


class Engine:

    def __init__(self, sem):
        self.sem, self.n, self.ops, self.seen = sem, 0, [], {}

    def wait(self, *tokens):
        for t in tokens:
            if t is None:
                continue
            sem, n = t
            if self.seen.get(id(sem), 0) < n:
                self.seen[id(sem)] = n
                self.ops.append(lambda e, sem=sem, n=n: e.wait_ge(sem, n))

    def do(self, fn, *tokens):
        self.wait(*tokens)
        self.n += 1
        self.ops.append(lambda e: fn(e).then_inc(self.sem, 1))
        return (self.sem, self.n)

    def go(self, fn):
        self.ops.append(fn)

    def run(self, e):
        for op in self.ops:
            op(e)


def build(nc, A, out, scratch, rows):
    held = []

    def new_sem(name):
        cm = nc.semaphore(name)
        held.append(cm)
        return cm.__enter__()

    pe, act, dve, pool, sp = (Engine(new_sem(f"s_{n}")) for n in ("pe", "act", "dve", "pool", "sp"))
    at = [16512]

    def sb(name, shape, dt=F32, offset=None):
        size = (int(np.prod(shape[1:])) * (1 if dt == U8 else 4) + 63) // 64 * 64
        if offset is None:
            offset = at[0]
            at[0] += size
            assert at[0] <= 229344, (name, at[0])
        return nc.alloc_sbuf_tensor_at(name, shape, dt, offset=offset)

    def arena(begin, end):
        p = [begin]

        def get(name, shape, dt=F32):
            t = sb(name, shape, dt, p[0])
            p[0] += (int(np.prod(shape[1:])) * (1 if dt == U8 else 4) + 63) // 64 * 64
            assert p[0] <= end, (name, p[0], end)
            return t
        return get

    bank = []
    for i in range(8):
        cm = nc.psum_tensor(f"ps{i}", [128, 512], F32)
        held.append(cm)
        bank.append(cm.__enter__())
    free = deque((i, None) for i in range(8))

    def take():
        i, tok = free.popleft()
        pe.wait(tok)
        return i

    def give(i, tok):
        free.append((i, tok))

    NR, NS = 3, 6
    raw = sb("raw", [128, NR, 1024])
    WH = sb("WH", [128, NS, 512], F32R)
    WL = sb("WL", [128, NS, 512], F32R)
    H = sb("H", [128, 8, NA])
    cst = sb("cst", [128, NCONST])
    msk = sb("msk", [128, 7, 128], U8)
    vec = sb("vec", [128, NVEC])
    ones = sb("ones", [128, 128])
    RB = sb("RB", [128, NA])
    RS = sb("RS", [128, NA])
    RC = sb("RC", [128, 5])
    RCs = sb("RCs", [128, 5])
    ACC = sb("ACC", [128, NA])
    SQ = sb("SQ", [128, 2, NA])
    eps = sb("eps", [128, 1])
    u0 = at[0]
    UH = sb("UH", [128, 8, NA], F32R)
    UL = sb("UL", [128, 8, NA], F32R)
    u1 = at[0]
    h0 = at[0]
    HH = sb("HH", [128, 8, NT], F32R)
    HL = sb("HL", [128, 8, NT], F32R)
    t0 = at[0]
    END = 229344
    END0, END1 = END - 16384, END - 32768
    KM, VM = [], []
    for l, o in enumerate((END0, END1)):
        KM.append(sb(f"KM{l}", [128, 8, 256], F32, o))
        VM.append(sb(f"VM{l}", [128, 2, 1024], F32, o + 8192))
    ident = cst[:, C_ID:C_ID + 128]
    causal = cst[:, C_CAUSAL:C_CAUSAL + 128]

    s_c = new_sem("s_cst")
    s_h = [new_sem(f"s_h{i}") for i in range(4)]

    def load(dst, src, sem):
        sp.ops.append(lambda e: e.dma_start(dst, src).then_inc(sem, 16))

    load(vec[:, :], A["vecs"], s_c)
    for i in range(4):
        load(H[:, 2 * i:2 * i + 2, :], A["hT"].rearrange("(k p) n -> p k n", p=128)[:, 2 * i:2 * i + 2, :], s_h[i])

    tiles = [t for lot in plan() for t in lot]
    assert len(tiles) % 8 == 0
    NU = len(tiles) // 8
    s_w = [new_sem(f"s_w{i}") for i in range(NR)]
    wdram = A["stream"]

    class Stream:
        made = 0
        lo = {}
        used = {}
        pos = 0

    st = Stream()

    def split(v):
        r, s, c = (v // 2) % NR, v % NS, slice(512 * (v % 2), 512 * (v % 2) + 512)
        if v % 2 == 0:
            sp.wait(st.lo.get(v - 2 * NR + 1))
            load(raw[:, r, :], wdram[v // 2], s_w[r])
        landed = (s_w[r], 16 * (v // 2 // NR + 1))
        hi = act.do(call(nc.scalar.activation, WH[:, s, :], raw[:, r, c], ACT.Copy), landed, st.used.get(v - NS))
        st.lo[v] = dve.do(call(nc.vector.tensor_tensor, WL[:, s, :], raw[:, r, c], WH[:, s, :].bitcast(F32),
                               ALU.subtract), hi, landed, st.used.get(v - NS))

    def weights(n):
        v, j = st.pos // 4, st.pos % 4
        assert j + n <= 4
        if j == 0:
            while st.made < min(v + 5, 2 * NU):
                split(st.made)
                st.made += 1
            pe.wait(st.lo[v])
        st.pos += n
        c = slice(128 * j, 128 * (j + n))
        return WH[:, v % NS, c], WL[:, v % NS, c], (v if st.pos % 4 == 0 else None)

    def mm(o, l, r, start, stop):
        pe.go(call(nc.tensor.matmul, o, l, r, start=start, stop=stop, skip_group_check=True))

    def mmt(o, l, r, start, stop, *tokens):
        return pe.do(call(nc.tensor.matmul, o, l, r, start=start, stop=stop, skip_group_check=True), *tokens)

    def passes(o, ah, al, bh, bl, start, stop, token):
        mm(o, ah, bh, start, False)
        mm(o, ah, bl, False, False)
        return (mmt if token else mm)(o, al, bh, False, stop)

    late = []

    def flush():
        while late:
            late.pop(0)()

    def lin_steps(nk, nm, XH, XL, ready, evac, ranges=((NM, NT),), hook=None, ks=None, hook_at=5):
        ks = ks or range(nk)
        bk, fin = {}, {}
        for i, k in enumerate(ks):
            pe.wait(*ready[k])
            end = i == nk - 1
            for m in range(nm):
                wh, wl, last = weights(1)
                for n0, n in ranges:
                    if i == 0:
                        bk[m, n0] = take()
                    o = bank[bk[m, n0]][:, 0:n]
                    mm(o, wh, XH[:, k, n0:n0 + n], i == 0, False)
                    mm(o, wh, XL[:, k, n0:n0 + n], False, False)
                for n0, n in ranges:
                    o = bank[bk[m, n0]][:, 0:n]
                    if end or last is not None:
                        fin[m, n0] = mmt(o, wl, XH[:, k, n0:n0 + n], False, end)
                    else:
                        mm(o, wl, XH[:, k, n0:n0 + n], False, end)
                if last is not None:
                    st.used[last] = fin[m, n0]
            if hook and i == hook_at:
                hook()
            if not end:
                yield
        for m in range(nm):
            for n0, n in ranges:
                give(bk[m, n0], evac(m, bank[bk[m, n0]][:, 0:n], fin[m, n0], n0, n))
        flush()
        yield

    def tok_steps(nk, XH, XL, ready, chunks, evac):
        bk = []
        for k in range(nk):
            pe.wait(*ready[k])
            wh, wl, last = weights(4)
            for i, c in enumerate(chunks):
                if k == 0:
                    bk.append(take())
                tok = passes(bank[bk[i]][:, :], XH[:, k, c:c + 128], XL[:, k, c:c + 128], wh, wl, k == 0,
                             k == nk - 1, True)
            st.used[last] = tok
            if k < nk - 1:
                yield
        for i, c in enumerate(chunks):
            give(bk[i], evac(i, bank[bk[i]], tok))
        yield

    def lin(*args, **kwargs):
        for _ in lin_steps(*args, **kwargs):
            pass

    def lin_tok(*args, **kwargs):
        for _ in tok_steps(*args, **kwargs):
            pass

    class Filler:

        def __init__(self, gens, rate):
            self.gens, self.rate, self.due = list(gens), rate, 0.0

        def __call__(self, n=1.0):
            self.due += n * self.rate
            while self.due >= 1 and self.gens:
                self.due -= 1
                self.one()

        def one(self):
            for _ in self.gens[0]:
                return
            self.gens.pop(0)
            if self.gens:
                self.one()

        def finish(self):
            while self.gens:
                self.one()

    class Norm:
        acc = None
        read = None
        sq = [None, None]
        rb = None
        rc = None
    nm_ = Norm()

    def square_in(k, src, n0, n, tok):
        c = slice(n0, n0 + n)
        if k == 0:
            nm_.acc = pool.do(call(nc.gpsimd.tensor_tensor, ACC[:, c], src, src, ALU.mult), tok, nm_.read)
        else:
            s = SQ[:, k % 2, c]
            a = pool.do(call(nc.gpsimd.tensor_tensor, s, src, src, ALU.mult), tok, nm_.sq[k % 2])
            nm_.acc = pool.do(call(nc.gpsimd.tensor_tensor, ACC[:, c], ACC[:, c], s, ALU.add), a, nm_.acc)
            nm_.sq[k % 2] = nm_.acc

    def inv_rms(ranges, chunks, users):
        last = None
        for n0, n in ranges:
            b = take()
            t = mmt(bank[b][:, 0:n], ones[:, :], ACC[:, n0:n0 + n], True, True, nm_.acc, t_ones)
            a = act.do(call(nc.scalar.activation, RS[:, n0:n0 + n], bank[b][:, 0:n], ACT.Sqrt,
                                                              bias=eps[:, :], scale=1.0 / 1024), t, nm_.rb, t_eps)
            give(b, a)
            last = dve.do(call(nc.vector.reciprocal, RB[:, n0:n0 + n], RS[:, n0:n0 + n]), a, *users)
        if chunks:
            b = take()
            for i, c in enumerate(chunks):
                t = mmt(bank[b][:, i:i + 1], ACC[:, c:c + 128], ones[:, 0:1], True, True)
            k = len(chunks)
            a = act.do(call(nc.scalar.activation, RCs[:, 0:k], bank[b][:, 0:k], ACT.Sqrt, bias=eps[:, :],
                                              scale=1.0 / 1024), t, nm_.rc)
            give(b, a)
            nm_.rc = dve.do(call(nc.vector.reciprocal, RC[:, 0:k], RCs[:, 0:k]), a, *users)
        nm_.read = t
        nm_.rb = last
        return last

    def hilo(hi, lo, src, w, tok, *free_):
        if w is None:
            a = act.do(call(nc.scalar.activation, hi, src, ACT.Copy), tok, *free_)
            return dve.do(call(nc.vector.tensor_tensor, lo, src, hi.bitcast(F32), ALU.subtract), a, tok, *free_)
        a = act.do(call(nc.scalar.activation, hi, src, ACT.Copy, scale=w), tok, *free_)
        return dve.do(call(nc.vector.scalar_tensor_tensor, lo, src, w, hi.bitcast(F32), ALU.mult, ALU.subtract),
                      a, tok, *free_)

    ready = [[] for _ in range(8)]
    all_col = slice(0, NA)
    xc = slice(NM, NA)
    CH = [NM + 128 * i for i in range(4)]

    def residual(m0, wcol, last=True, also=None):
        def evac(m, p, tok, n0, n):
            k = m0 + m
            src = H[:, k, xc]
            t = dve.do(call(nc.vector.tensor_tensor, src, p, src, ALU.add), tok, h_tok[k])
            h_tok[k] = t
            flush()
            if last:
                if wcol is not None:
                    w = wcol[:, k:k + 1]
                    a = act.do(call(nc.scalar.activation, UH[:, k, xc], src, ACT.Copy, scale=w), t, t_w2)

                    def lo():
                        ready[k] = [dve.do(call(nc.vector.scalar_tensor_tensor, UL[:, k, xc], src, w,
                                                UH[:, k, xc].bitcast(F32), ALU.mult, ALU.subtract), a, t)]
                    late.append(lo)
                if also:
                    also(k, src, t)
                square_in(k, src, NM, NT, t)
            return t
        return evac

    h_tok = [None] * 8

    t_ones = dve.do(call(nc.vector.memset, ones[:, :], 1.0))
    t_eps = dve.do(call(nc.vector.memset, eps[:, :], EPS))
    t_vec = t_w2 = (s_c, 16)
    t_cst = (s_c, 48)

    P1 = arena(t0, END)
    OM = P1("OM", [128, 4, NA])
    V2 = P1("V2", [128, 5, NT])
    r0 = t0 + (4 * NA + 5 * NT) * 4
    Q = P1("Q", [128, 4, NT])
    K = P1("K", [128, 4, NA])
    V = P1("V", [128, 5, NT])
    CT = P1("CT", [8, NA])
    CC = P1("CC", [128, 4, 8])
    small = P1("small", [128, 64])
    NB = P1("NB", [128, 2, NA])
    NSL = 5
    S2 = P1("S2", [128, NSL, NA])
    PM = P1("PM", [16, NT])
    PT = P1("PT", [128, 4, NT])
    FZ = sb("FZ", [8, 3, NA], F32, END0)
    HQ = sb("HQ", [128, 4, NT], F32, t0 - 4 * NT * 4)
    HG = sb("HG", [128, 4, NT], F32, t0 - 12 * NT * 4)
    MF = sb("MF", [128, 7, 128], F32, h0)

    for k in range(8):
        t = (s_h[k // 2], 16)
        ready[k] = [hilo(UH[:, k, :], UL[:, k, :], H[:, k, :], vec[:, V_MIX + k:V_MIX + k + 1], t, t_vec)]
        square_in(k, H[:, k, :], 0, NA, t)

    def load_constants():
        load(cst[:, :], A["consts"], s_c)
        load(MF[:, :, :], A["masks"].rearrange("p (l n) -> p l n", l=7), s_c)
        return dve.do(call(nc.vector.tensor_copy, msk[:, :, :], MF[:, :, :]), (s_c, 48))


    def first_hook():
        inv_rms([(NM, NT), (0, NM)], [0] + CH, [])

    def times_r(dst, extra=None):
        off = NA - dst.shape[2]

        def evac(m, p, tok, n0, n):
            o = dst[:, m, n0 - off:n0 - off + n]
            if extra is None:
                return dve.do(call(nc.vector.tensor_tensor, o, p, RB[:, n0:n0 + n], ALU.mult), tok, nm_.rb)
            return dve.do(call(nc.vector.scalar_tensor_tensor, o, p, extra, RB[:, n0:n0 + n], ALU.mult, ALU.mult),
                          tok, nm_.rb)
        return evac

    def rows_r(dst, off):
        def evac(i, p, tok):
            rows = NM if (off == 0 and i == 0) else 128
            return act.do(call(nc.scalar.activation, dst[0:rows, i, :], p[0:rows, :], ACT.Copy,
                                                 scale=RC[0:rows, i:i + 1]), tok, nm_.rc)
        return evac

    lin(8, 4, UH, UL, ready, times_r(Q, 0.125), hook=first_hook)
    t_msk = load_constants()
    TWO = ((0, NA // 2), (NA // 2, NA // 2))
    lin(8, 4, UH, UL, ready, times_r(K), ranges=TWO)

    def ff_evac(m, p, tok, n0, n):
        return dve.do(call(nc.vector.tensor_tensor, FZ[:, 0, n0:n0 + n], p[0:8, :], RB[0:8, n0:n0 + n], ALU.mult),
                      tok, nm_.rb)

    lin(8, 1, UH, UL, ready, ff_evac, ranges=TWO)
    t_z = (dve.sem, dve.n)
    t_z = dve.do(call(nc.vector.tensor_scalar, FZ[:, 0, :], FZ[:, 0, :], vec[0:8, V_FB:V_FB + 1], None, ALU.add),
                 t_z, t_vec)
    t = dve.do(call(nc.vector.scalar_tensor_tensor, FZ[:, 1, :], FZ[:, 0, :], -1.0, FZ[:, 0, :], ALU.mult, ALU.max), t_z)
    t = act.do(call(nc.scalar.activation, FZ[:, 1, :], FZ[:, 1, :], ACT.Exp, scale=-1.0), t)
    t = act.do(call(nc.scalar.activation, FZ[:, 2, :], FZ[:, 1, :], ACT.Ln, bias=ones[0:8, 0:1]), t)
    t = dve.do(call(nc.vector.scalar_tensor_tensor, FZ[:, 1, :], FZ[:, 0, :], 0.0, FZ[:, 2, :], ALU.min,
                                                ALU.subtract), t)
    t0_ = dve.do(call(nc.vector.memset, FZ[:, 2, :], -1.0), t)
    t = dve.do(call(nc.vector.tensor_scalar, FZ[:, 0, :], FZ[:, 2, :], -1.0, None, ALU.mult), t0_)
    t_ct = dve.do(call(nc.vector.tensor_tensor_scan, CT[:, :], FZ[:, 0, :], FZ[:, 1, :], 0.0, ALU.mult, ALU.add), t)
    t = dve.do(call(nc.vector.tensor_tensor, FZ[:, 1, :], CT[:, :], FZ[:, 2, :], ALU.mult), t_ct)
    s_nc = new_sem("s_nc")
    s_nb = [new_sem("s_nb0"), new_sem("s_nb1")]
    sp.wait(t)
    load(rows, FZ[:, 1, :], s_nc)
    b = take()
    for i in range(4):
        t = pe.do(call(nc.tensor.transpose, bank[b][:, 8 * i:8 * i + 8], CT[:, CH[i]:CH[i] + 128],
                                            cst[0:8, C_ID:C_ID + 8]), t_ct, t_cst)
    t_cc = act.do(call(nc.scalar.activation, CC[:, :, :], bank[b][:, 0:32].rearrange("p (i h) -> p i h", h=8),
                                         ACT.Copy), t)
    give(b, t_cc)
    lin_tok(8, UH, UL, ready, [0] + CH, rows_r(V, 0))
    t_v = (act.sem, act.n)

    lin_tok(8, UH, UL, ready, [0] + CH, rows_r(V2, 0))
    t_v2 = (act.sem, act.n)
    fill = Filler([lin_steps(8, 4, UH, UL, ready, times_r(HQ))]
                  + [lin_steps(8, 2, UH, UL, ready, times_r(OM[:, 2 * i:2 * i + 2, :]), ranges=TWO) for i in range(2)]
                  + [lin_steps(8, 4, UH, UL, ready, times_r(HG))], 0.9)

    def pipeline(items, stages, fill=None):
        for step in range(len(items) + len(stages) - 1):
            for s in reversed(range(len(stages))):
                if 0 <= step - s < len(items):
                    stages[s](items[step - s])
            if fill:
                fill()

    nS = [None] * NSL
    nPT = None
    nNB = [None, None]
    mfree = {}

    def fox_bias(h):
        if h == 0:
            sp.wait((s_nc, 16))
        sp.wait(nNB[h % 2])
        load(NB[:, h % 2, :], rows[h:h + 1, :].broadcast_to([128, NA]), s_nb[h % 2])
        return (s_nb[h % 2], 16 * (h // 2 + 1))

    items = [dict(h=h, i=i, n=h * 4 + i, ns=NM + 128 * (i + 1)) for h in range(8) for i in range(4)]
    head = [dict() for _ in range(8)]
    head[0]["nb"] = fox_bias(0)

    def f0(x):
        h, i, ns = x["h"], x["i"], x["ns"]
        rows_ = slice(64 * (h % 2), 64 * (h % 2) + 64)
        lhs = Q[rows_, h // 2, 128 * i:128 * i + 128]
        x["b"] = [(take(), 0, min(ns, 512))]
        if ns > 512:
            x["b"].append((take(), 512, ns - 512))
        for b, c, n in x["b"]:
            x["t"] = mmt(bank[b][:, 0:n], lhs, K[rows_, h // 2, c:c + n], True, True)

    def f1(x):
        h, i, s = x["h"], x["i"], x["n"] % NSL
        if i == 0 and h < 7:
            head[h + 1]["nb"] = fox_bias(h + 1)
        for b, c, n in x["b"]:
            t = dve.do(call(nc.vector.scalar_tensor_tensor, S2[:, s, c:c + n], bank[b][:, 0:n], CC[:, i, h:h + 1],
                            NB[:, h % 2, c:c + n], ALU.add, ALU.add), x["t"], head[h]["nb"], t_cc, nS[s])
            give(b, t)
        nNB[h % 2] = t
        d = S2[:, s, NM + 128 * i:NM + 128 * i + 128]
        x["t"] = pool.do(call(nc.gpsimd.affine_select, out=d, in_=d, compare_op=ALU.is_ge, fill=-1e30, base=0,
                              pattern=[[-1, 128]], channel_multiplier=1), t)

    def f2(x):
        s, ns = x["n"] % NSL, x["ns"]
        m = small[:, 4 * (x["n"] % 8):4 * (x["n"] % 8) + 4]
        t = dve.do(call(nc.vector.tensor_reduce, m[:, 0:1], S2[:, s, 0:ns], AX.X, ALU.max, negate=True), x["t"],
                   mfree.get(x["n"] % 8))
        x["e"] = act.do(call(nc.scalar.activation, S2[:, s, 0:ns], S2[:, s, 0:ns], ACT.Exp, bias=m[:, 0:1],
                             accum_out=m[:, 1:2]), t)

    def f3(x):
        s, ns = x["n"] % NSL, x["ns"]
        m = small[:, 4 * (x["n"] % 8):4 * (x["n"] % 8) + 4]
        t = dve.do(call(nc.vector.reciprocal, m[:, 2:3], m[:, 1:2]), x["e"])
        x["t"] = dve.do(call(nc.vector.tensor_scalar, S2[:, s, 0:ns], S2[:, s, 0:ns], m[:, 2:3], None, ALU.mult), t)
        mfree[x["n"] % 8] = x["t"]

    def f4(x):
        i, s = x["i"], x["n"] % NSL
        b, b2 = take(), take()
        pe.wait(x["t"])
        pe.go(call(nc.tensor.transpose, bank[b2][0:NM, 0:128], S2[:, s, 0:NM], ident))
        for j in range(i + 1):
            t = pe.do(call(nc.tensor.transpose, bank[b][:, 128 * j:128 * j + 128],
                           S2[:, s, NM + 128 * j:NM + 128 * j + 128], ident))
        nS[s] = t
        x["tb"] = (b, b2, t)

    def f5(x):
        i = x["i"]
        b, b2, t = x["tb"]
        tc = slice(128 * i, 128 * i + 128)
        a = act.do(call(nc.scalar.activation, PT[:, 0:i + 1, tc],
                        bank[b][:, 0:128 * (i + 1)].rearrange("p (j n) -> p j n", n=128), ACT.Copy), t, nPT)
        give(b, a)
        a = act.do(call(nc.scalar.activation, PM[:, tc], bank[b2][0:NM, 0:128], ACT.Copy), t)
        give(b2, a)
        x["a"] = a

    def f6(x):
        nonlocal nPT
        h = x["h"]
        if x["i"] < 3:
            return
        x["o"] = o = take()
        r = slice(64 * (h % 2), 64 * (h % 2) + 64)
        hc = slice(64 * h, 64 * h + 64)
        pe.wait(x["a"], t_v)
        mm(bank[o][r, :], V[0:NM, 0, hc], PM[:, :], True, False)
        for j in range(4):
            nPT = mmt(bank[o][r, 128 * j:NT], V[:, 1 + j, hc], PT[:, j, 128 * j:NT], False, j == 3)
        x["t"] = nPT

    def f7(x):
        h = x["h"]
        if x["i"] < 3:
            return
        o, r = x["o"], slice(64 * (h % 2), 64 * (h % 2) + 64)
        a = act.do(call(nc.scalar.activation, HH[r, h // 2, :], bank[o][r, :], ACT.Copy), x["t"])
        t = dve.do(call(nc.vector.tensor_tensor, HL[r, h // 2, :], bank[o][r, :], HH[r, h // 2, :].bitcast(F32),
                        ALU.subtract), a)
        give(o, t)
        head[h]["out"] = t

    pe.wait((dve.sem, dve.n))
    pipeline(items, [f0, f1, f2, f3, f4, f5, f6, f7], fill)
    fill.finish()
    t_om = t_hq = t_hg = (dve.sem, dve.n)
    ready_o = [[head[2 * k + 1]["out"]] for k in range(4)] + [[] for _ in range(4)]

    def fence():
        toks = [(x.sem, x.n) for x in (pe, act, dve, pool) if x.n]
        for x in (act, dve, pool, sp):
            x.wait(*toks)

    s_m = new_sem("s_m")

    def mem_steps(l, MH, ML, AM, RM, RQ):
        MT = sb(f"MT{l}", [128, 8, 256], F32, (END0, END1)[l])
        load(MT[:, :, :], A["memT"].rearrange("(k p) n -> p k n", p=128), s_m)
        landed = (s_m, 16 * (l + 1))
        rm = []
        for k in range(8):
            rm.append([hilo(MH[:, k, :], ML[:, k, :], MT[:, k, :], vec[:, V_MEM + k:V_MEM + k + 1], landed)])
            if k == 0:
                acc = pool.do(call(nc.gpsimd.tensor_tensor, AM[:, 0, :], MT[:, 0, :], MT[:, 0, :], ALU.mult), landed)
            else:
                t = pool.do(call(nc.gpsimd.tensor_tensor, AM[:, 1, :], MT[:, k, :], MT[:, k, :], ALU.mult), acc)
                acc = pool.do(call(nc.gpsimd.tensor_tensor, AM[:, 0, :], AM[:, 0, :], AM[:, 1, :], ALU.add), t)
        b = take()
        mmt(bank[b][:, 0:256], ones[:, :], AM[:, 0, :], True, True, acc)
        for i in range(2):
            t = mmt(bank[b][:, 256 + i:257 + i], AM[:, 0, 128 * i:128 * i + 128], ones[:, 0:1], True, True)
        a = act.do(call(nc.scalar.activation, RM[:, :], bank[b][:, 0:256], ACT.Sqrt, bias=eps[:, :],
                        scale=1.0 / 1024), t)
        a2 = act.do(call(nc.scalar.activation, RQ[:, 0:2], bank[b][:, 256:258], ACT.Sqrt, bias=eps[:, :],
                         scale=1.0 / 1024))
        give(b, a2)
        tr = dve.do(call(nc.vector.reciprocal, RM[:, :], RM[:, :]), a)
        tc = dve.do(call(nc.vector.reciprocal, RQ[:, 2:4], RQ[:, 0:2]), a2)
        read = rm[7]
        yield
        for g in range(2):
            def evac(m, p, t, n0, n):
                return dve.do(call(nc.vector.tensor_tensor, KM[l][:, 4 * g + m, :], p, RM[:, :], ALU.mult), t, tr,
                              acc, *read)
            yield from lin_steps(8, 4, MH, ML, rm, evac, ranges=((0, 256),))
        for g in range(2):
            def evac_v(i, p, t):
                return act.do(call(nc.scalar.activation, VM[l][:, i, 512 * g:512 * g + 512], p[:, :], ACT.Copy,
                                   scale=RQ[:, 2 + i:3 + i]), t, tc)
            yield from tok_steps(8, MH, ML, rm, [0, 128], evac_v)

    fence()
    R = arena(r0, END0)
    U = arena(u0, u1)
    FG = U("FG", [128, 2, NA])
    B = U("B", [128, 2, NA])
    GT = sb("GT", [128, 2, NA], F32, u0 + 2 * 2 * NA * 4)
    XL2 = U("XL2", [128, 2, 2, NT])
    EX2 = U("EX2", [128, 2, 2, NT])
    TN = sb("TN", [128, 2, NT], F32, u0 + 2 * 2 * NA * 4)
    QE = U("QE", [128, 2, NT])
    KT = U("KT", [128, 2, 2, 128])
    ST = U("ST", [128, 2, 2, 128])
    KD = R("KD", [128, 2, 400])
    AT = R("AT", [128, 4, 2, 128])
    MS = R("MS", [128, NA])
    EL = R("EL", [128, 4, 4])
    LB = R("LB", [128, 6, 4])
    OH = R("OH", [128, 4, NT])
    AM = R("AM", [128, 2, 256])
    RM = R("RM", [128, 256])
    RQ = R("RQ", [128, 4])
    MH = R("MH", [128, 8, 256], F32R)
    ML = R("ML", [128, 8, 256], F32R)
    fill = Filler([mem_steps(0, MH, ML, AM, RM, RQ)], 1.0)
    fill()

    lbr = vec[:, V_LB:V_LB + 4]
    t = dve.do(call(nc.vector.tensor_tensor, LB[:, 0, :], lbr, lbr, ALU.subtract), t_vec)
    t = act.do(call(nc.scalar.activation, LB[:, 1, :], LB[:, 0, :], ACT.Exp), t)
    t = dve.do(call(nc.vector.reciprocal, LB[:, 2, :], LB[:, 1, :]), t)
    t = dve.do(call(nc.vector.tensor_tensor, LB[:, 3, :], LB[:, 1, :], LB[:, 2, :], ALU.mult), t)
    t = dve.do(call(nc.vector.tensor_tensor, LB[:, 4, :], LB[:, 3, :], LB[:, 3, :], ALU.subtract), t)
    t_lb = dve.do(call(nc.vector.tensor_scalar, LB[:, 5, :], LB[:, 4, :], -1.0, 1.0, ALU.mult, ALU.add), t)
    t = act.do(call(nc.scalar.activation, OM[:, :, :], OM[:, :, :], ACT.Sigmoid, scale=-1.0), t_om)
    dve.wait(t, t_lb)
    for h in range(4):
        t_k = dve.do(call(nc.vector.tensor_scalar, OM[:, h, :], OM[:, h, :], LB[:, 5, h:h + 1], None, ALU.mult))
    t = act.do(call(nc.scalar.activation, HQ[:, :, :], HQ[:, :, :], ACT.Silu), t_hq)
    t_q = pool.do(call(nc.gpsimd.tensor_scalar, HQ[:, :, :], HQ[:, :, :], float(128 ** -0.5), None, ALU.mult), t)
    t_hg = act.do(call(nc.scalar.activation, HG[:, :, :], HG[:, :, :], ACT.Silu), t_hg)
    t = dve.do(call(nc.vector.memset, MS[:, :], 1.0))
    dve.wait(t)
    for c in (0, 16, 144, 272, 400):
        t_ms = dve.do(call(nc.vector.memset, MS[:, c:c + 1], 0.0))

    def every(x, n):
        return x.unsqueeze(x.ndim).broadcast_to(list(x.shape) + [n])

    def pairs(x, t):
        return x.rearrange("p h (n t) -> p h n t", t=2)[:, :, :, t]

    def halves(x, n, t):
        return x.rearrange("p h (b t n) -> p h b t n", t=2, n=n)[:, :, :, t, :]

    done = [(pe.sem, pe.n)]
    xfree, exfree, last_b = [None, None], [None, None], []
    t_oh = None
    t_qe_last = [None]

    def two_heads(p):
        nonlocal done, last_b, t_oh
        om, hq, el = OM[:, 2 * p:2 * p + 2], HQ[:, 2 * p:2 * p + 2], EL[:, 2 * p:2 * p + 2]
        omx, fgx, bx = om[:, :, xc], FG[:, :, xc], B[:, :, xc]
        t = dve.do(call(nc.vector.tensor_scalar, FG[:, :, :], om, -1.0, 1.0, ALU.mult, ALU.add), t_k, *done, *last_b)
        t_f = dve.do(call(nc.vector.tensor_scalar, FG[:, :, :], FG[:, :, :], FMIN, None, ALU.max), t)
        t_g = act.do(call(nc.scalar.activation, GT[:, :, :], FG[:, :, :], ACT.Ln), t_f, *done, *xfree)
        dve.wait(t_g, t_ms)
        for h in range(2):
            t_b = dve.do(call(nc.vector.tensor_tensor_scan, B[:, h, :], MS[:, :], GT[:, h, :], 0.0, ALU.mult,
                              ALU.add))
        fill(2)

        X0, X1 = XL2[:, 0], XL2[:, 1]
        ex0 = EX2[:, 0, :, 0:256]
        t1 = dve.do(call(nc.vector.reciprocal, ex0, pairs(fgx, 1)), t_b, exfree[0])
        dve.do(call(nc.vector.tensor_copy, pairs(X0, 0), pairs(omx, 0)), t1)
        ta = dve.do(call(nc.vector.tensor_tensor, pairs(X0, 1), pairs(omx, 1), ex0, ALU.mult), t1)
        exfree[0] = ta
        pool.do(call(nc.gpsimd.tensor_copy, pairs(X1, 0), pairs(hq, 0)), t_b, t_q)
        tb = pool.do(call(nc.gpsimd.tensor_tensor, pairs(X1, 1), pairs(hq, 1), pairs(fgx, 1), ALU.mult))
        atok = pool.do(call(nc.gpsimd.memset, AT[:, :, :, :], 0.0), *done)

        def produce(l):
            n, s = LEVELS[l], l % 2
            ex, X = EX2[:, (l + 1) % 2], XL2[:, s]
            midb = every(halves(bx, n, 0)[:, :, :, n - 1], n)
            a = pool.do(call(nc.gpsimd.tensor_tensor, halves(ex, n, 0), midb, halves(bx, n, 0), ALU.subtract),
                        exfree[(l + 1) % 2], t_b)
            d = dve.do(call(nc.vector.tensor_tensor, halves(ex, n, 1), halves(bx, n, 1), midb, ALU.subtract),
                       exfree[(l + 1) % 2], t_b, a)
            x = act.do(call(nc.scalar.activation, ex, ex, ACT.Exp), a, d)
            return ex, X, n, s, x

        def consume(l, lhs, rhs, a, d, xs):
            nonlocal atok
            pe.wait(a, d)
            for c in (0, 2):
                b = take()
                for cc in (c, c + 1):
                    for h in range(2):
                        o = 256 * (cc - c) + 128 * h
                        n = slice(128 * cc, 128 * cc + 128)
                        t = mmt(bank[b][:, o:o + 128], lhs[:, h, n], rhs[:, h, n], True, True)
                m = msk[:, l, :].unsqueeze(1).broadcast_to([128, 4, 128])
                atok = dve.do(call(nc.vector.copy_predicated, AT[:, c:c + 2, :, :].rearrange("p c h n -> p (c h) n"), m,
                                   bank[b][:, :].rearrange("p (h n) -> p h n", n=128)), t, atok, t_msk)
                give(b, atok)
            for x in xs:
                xfree[x] = t

        def ends():
            kd4 = KD[:, :, 16:400].rearrange("p h (c n) -> p h c n", n=128)
            b4 = B[:, :, 16:400].rearrange("p h (c n) -> p h c n", n=128)
            pool.do(call(nc.gpsimd.tensor_tensor, KD[:, :, 0:16], every(B[:, :, 15], 16), B[:, :, 0:16],
                         ALU.subtract), t_b, *done)
            t = pool.do(call(nc.gpsimd.tensor_tensor, kd4, every(b4[:, :, :, 127], 128), b4, ALU.subtract))
            t = act.do(call(nc.scalar.activation, KD[:, :, :], KD[:, :, :], ACT.Exp), t)
            t_el = act.do(call(nc.scalar.activation, el[:, :, 0:3], b4[:, :, :, 127], ACT.Exp), t_b)
            t2 = act.do(call(nc.scalar.activation, QE[:, :, :], bx, ACT.Exp), t_b, *done)
            t_kd = pool.do(call(nc.gpsimd.tensor_tensor, KD[:, :, :], KD[:, :, :], om[:, :, 0:400], ALU.mult), t, t_k)
            t_qe = pool.do(call(nc.gpsimd.tensor_tensor, QE[:, :, :], QE[:, :, :], hq, ALU.mult), t2, t_q)
            return t_kd, t_qe, t_el, t2

        nxt = produce(0)
        ready_x = (0, X0, X1, ta, tb, [0, 1])
        for l in range(len(LEVELS)):
            cur = nxt
            if l + 1 < len(LEVELS):
                nxt = produce(l + 1)
            consume(*ready_x)
            fill()
            ex, X, n, s, x = cur
            a = pool.do(call(nc.gpsimd.tensor_tensor, halves(X, n, 0), halves(ex, n, 0), halves(omx, n, 0), ALU.mult),
                        x, xfree[s])
            d = dve.do(call(nc.vector.tensor_tensor, halves(X, n, 1), halves(ex, n, 1), halves(hq, n, 1), ALU.mult),
                       x, xfree[s], t_q, a)
            exfree[(l + 1) % 2] = d
            ready_x = (l + 1, X, X, a, d, [s])
            if l == 2:
                t_kd, t_qe, t_el, t_e = ends()
        fill()
        consume(*ready_x)
        last_b = [d, a, t_kd, t_e, t_el, t_qe]

        ktf = [None, None]
        stt = [None, None]
        sread = None
        for c in range(5):
            n0, n = (0, 16) if c == 0 else (NM + 128 * (c - 1), 128)
            if c < 4:
                b = take()
                pe.wait(t_kd, t_cst)
                for h in range(2):
                    t = pe.do(call(nc.tensor.transpose, bank[b][0:n, 128 * h:128 * h + 128], KD[:, h, n0:n0 + n],
                                   ident))
                a = act.do(call(nc.scalar.activation, KT[0:n, c % 2, :, :],
                                bank[b][0:n, 0:256].rearrange("p (h n) -> p h n", n=128), ACT.Copy), t, ktf[c % 2],
                           *done)
                give(b, a)
            if c >= 1:
                bo = take()
                pe.wait(t_qe, atok, stt[c % 2], t_v2)
                for h in range(2):
                    o = bank[bo][:, 128 * h:128 * h + 128]
                    v = slice(128 * (2 * p + h), 128 * (2 * p + h) + 128)
                    mm(o, ST[:, c % 2, h, :], QE[:, h, n0 - NM:n0 - NM + 128], True, False)
                    to = mmt(o, V2[:, c, v], AT[:, c - 1, h, :], False, True)
                sread = to
                t_oh = act.do(call(nc.scalar.activation, OH[:, 2 * p:2 * p + 2, 128 * (c - 1):128 * c],
                                   bank[bo][:, 0:256].rearrange("p (h n) -> p h n", n=128), ACT.Copy), to)
                give(bo, t_oh)
            if c == 4:
                break
            fill()
            b = take()
            pe.wait(a, t_v2)
            for h in range(2):
                v = slice(128 * (2 * p + h), 128 * (2 * p + h) + 128)
                t = mmt(bank[b][:, 128 * h:128 * h + 128], KT[0:n, c % 2, h, :], V2[0:n, c, v], True, True)
            ktf[c % 2] = t
            if c == 0:
                s = dve.do(call(nc.vector.tensor_copy, ST[:, 1, :, :],
                                bank[b][:, 0:256].rearrange("p (h n) -> p h n", n=128)), t, *done)
            else:
                dve.wait(t, t_el, stt[c % 2], sread)
                for h in range(2):
                    s = dve.do(call(nc.vector.scalar_tensor_tensor, ST[:, (c + 1) % 2, h, :], ST[:, c % 2, h, :],
                                    el[:, h, c - 1:c], bank[b][:, 128 * h:128 * h + 128], ALU.mult, ALU.add))
            stt[(c + 1) % 2] = s
            give(b, s)
        done = [to]
        t_qe_last[0] = t_qe

    two_heads(0)
    two_heads(1)
    t_o = t_oh

    def head_norm(src, dsth, wcol, tok, gate, tmp, wtok, free_=()):
        xs = [dict(h=h, q=tmp[:, h % 2, :]) for h in range(4)]
        rsf = [None, None]

        def n0(x):
            h, q = x["h"], x["q"]
            x["t"] = pool.do(call(nc.gpsimd.tensor_tensor, q, src[:, h, :], src[:, h, :], ALU.mult), tok, rsf[h % 2],
                             *free_)

        def n1(x):
            q = x["q"]
            b = take()
            t = mmt(bank[b][:, :], ones[:, :], q, True, True, x["t"])
            a = act.do(call(nc.scalar.activation, q, bank[b][:, :], ACT.Sqrt, bias=eps[:, :], scale=1.0 / 128), t)
            give(b, a)
            t = dve.do(call(nc.vector.reciprocal, q, q), a)
            h = x["h"]
            t = dve.do(call(nc.vector.scalar_tensor_tensor, src[:, h, :], src[:, h, :], wcol, q, ALU.mult, ALU.mult),
                       t, wtok)
            rsf[h % 2] = t
            if gate is not None:
                t = dve.do(call(nc.vector.tensor_tensor, src[:, h, :], src[:, h, :], gate[:, h, :], ALU.mult), t)
            x["t"] = t
            x["a"] = act.do(call(nc.scalar.activation, HH[:, dsth + h, :], src[:, h, :], ACT.Copy), t, *free_)

        def n2(x):
            h = x["h"]
            x["r"] = dve.do(call(nc.vector.tensor_tensor, HL[:, dsth + h, :], src[:, h, :],
                                 HH[:, dsth + h, :].bitcast(F32), ALU.subtract), x["a"], x["t"], *free_)

        pipeline(xs, [n0, n1, n2])
        return [[x["r"]] for x in xs]

    fill.finish()
    ready_o[4:] = head_norm(OH, 4, vec[:, V_HN:V_HN + 1], t_o, HG, TN, t_hg, [t_q, t_qe_last[0], done[0]])

    fence()
    F = arena(t0, END0 - 4 * NT)
    T = F("T", [128, 12, NT])
    SZ = F("SZ", [128, 2, NT])
    ACC2 = sb("ACC2", [128, NT], F32, END0 - 4 * NT)
    WW = F("WW", [128, 8])
    t_w2 = dve.do(call(nc.vector.tensor_tensor, WW[:, :], vec[:, V_FIN:V_FIN + 8], vec[:, V_MIX2:V_MIX2 + 8],
                       ALU.mult), t_vec)
    for g in range(2):
        lin(8, 4, HH, HL, ready_o, residual(4 * g, vec[:, V_FFN:V_FFN + 8]), ranges=((0, NT),))

    def rms_hook():
        inv_rms([(NM, NT)], [], [])

    tfree = [None] * 12
    tn = [0]

    def temp():
        i = tn[0] % 12
        tn[0] += 1
        return T[:, i, :], i

    ready_h = [[] for _ in range(8)]

    f0_ = 0
    first = True
    for ci, nh in enumerate(HIDDEN):
        for j in range(0, nh, 2):
            store = {}

            def evac(m, p, tok, n0, n, j=j):
                if m < 2:
                    x, i = temp()
                    y, i2 = temp()
                    a = dve.do(call(nc.vector.tensor_tensor, x, p, RB[:, xc], ALU.mult), tok, nm_.rb, tfree[i])
                    s = act.do(call(nc.scalar.activation, y, x, ACT.Silu), a, tfree[i2])
                    tfree[i] = s
                    store[m] = (y, i2, s)
                    return a
                y, i2, s = store[m - 2]
                x, i = temp()
                k = j + m - 2
                a = dve.do(call(nc.vector.tensor_tensor, x, p, RB[:, xc], ALU.mult), tok, nm_.rb, tfree[i])
                t = dve.do(call(nc.vector.tensor_tensor, x, x, y, ALU.mult), a, s)
                tfree[i2] = t
                h = act.do(call(nc.scalar.activation, HH[:, k, :], x, ACT.Copy), t)
                flush()

                def lo():
                    t2 = dve.do(call(nc.vector.tensor_tensor, HL[:, k, :], x, HH[:, k, :].bitcast(F32),
                                     ALU.subtract), h, t)
                    ready_h[k] = [t2]
                    tfree[i] = t2
                late.append(lo)
                return a
            lin(8, 4, UH, UL, ready, evac, hook=rms_hook if first else None)
            first = False
        lastc = ci == len(HIDDEN) - 1
        acc2 = None
        sz = [None, None]

        def also(k, src, t):
            nonlocal acc2
            z = SZ[:, k % 2, :]
            a = act.do(call(nc.scalar.activation, z, src, ACT.Square, scale=vec[:, V_FIN + k:V_FIN + k + 1]), t,
                       sz[k % 2])
            if k == 0:
                acc2 = pool.do(call(nc.gpsimd.tensor_copy, ACC2[:, :], z), a)
            else:
                acc2 = pool.do(call(nc.gpsimd.tensor_tensor, ACC2[:, :], ACC2[:, :], z, ALU.add), a, acc2)
            sz[k % 2] = acc2
        for g in range(2):
            lin(nh, 4, HH, HL, ready_h, residual(4 * g, WW[:, :] if lastc else None, last=lastc,
                                                 also=also if lastc else None), ranges=((0, NT),), hook=None)

    t_x = None

    def double_hook():
        nonlocal t_x
        b, b2 = take(), take()
        t = mmt(bank[b][:, :], ones[:, :], ACC[:, xc], True, True, nm_.acc)
        t2 = mmt(bank[b2][:, :], ones[:, :], ACC2[:, :], True, True, acc2)
        a = act.do(call(nc.scalar.activation, R1[:, 0, :], bank[b][:, :], ACT.Sqrt, bias=eps[:, :],
                        scale=1.0 / 1024), t)
        give(b, a)
        a = dve.do(call(nc.vector.reciprocal, R1[:, 0, :], R1[:, 0, :]), a)
        d = dve.do(call(nc.vector.tensor_tensor, R1[:, 1, :], R1[:, 0, :], R1[:, 0, :], ALU.mult), a)
        d = dve.do(call(nc.vector.tensor_tensor, R1[:, 1, :], bank[b2][:, :], R1[:, 1, :], ALU.mult), d, t2)
        give(b2, d)
        d = act.do(call(nc.scalar.activation, R1[:, 1, :], R1[:, 1, :], ACT.Sqrt, bias=eps[:, :],
                        scale=1.0 / 1024), d)
        d = dve.do(call(nc.vector.reciprocal, R1[:, 1, :], R1[:, 1, :]), d)
        nm_.rb = dve.do(call(nc.vector.tensor_tensor, RB[:, xc], R1[:, 0, :], R1[:, 1, :], ALU.mult), d)
        b = take()
        for i in range(4):
            mmt(bank[b][:, i:i + 1], ACC[:, CH[i]:CH[i] + 128], ones[:, 0:1], True, True)
            t = mmt(bank[b][:, 4 + i:5 + i], ACC2[:, 128 * i:128 * i + 128], ones[:, 0:1], True, True)
        nm_.read = t
        c = act.do(call(nc.scalar.activation, RD[:, 0:4], bank[b][:, 0:4], ACT.Sqrt, bias=eps[:, :],
                        scale=1.0 / 1024), t)
        c = dve.do(call(nc.vector.reciprocal, RD[:, 0:4], RD[:, 0:4]), c)
        d = dve.do(call(nc.vector.tensor_tensor, RD[:, 4:8], RD[:, 0:4], RD[:, 0:4], ALU.mult), c)
        d = dve.do(call(nc.vector.tensor_tensor, RD[:, 4:8], bank[b][:, 4:8], RD[:, 4:8], ALU.mult), d)
        give(b, d)
        d = act.do(call(nc.scalar.activation, RD[:, 4:8], RD[:, 4:8], ACT.Sqrt, bias=eps[:, :], scale=1.0 / 1024), d)
        d = dve.do(call(nc.vector.reciprocal, RD[:, 4:8], RD[:, 4:8]), d)
        nm_.rc = dve.do(call(nc.vector.tensor_tensor, RC[:, 0:4], RD[:, 0:4], RD[:, 4:8], ALU.mult), d)
        for k in range(8):
            h_tok[k] = dve.do(call(nc.vector.scalar_tensor_tensor, H[:, k, xc], H[:, k, xc],
                                   vec[:, V_FIN + k:V_FIN + k + 1], R1[:, 0, :], ALU.mult, ALU.mult), *ready[k],
                              h_tok[k], acc2, nm_.acc)

    fence()
    G = arena(t0, END1)
    Q = G("Q3", [128, 4, NT])
    K = G("K3", [128, 4, NT])
    V = G("V3", [128, 4, NT])
    YU = G("YU", [128, 4, NT])
    LA = G("LA", [64, 2])
    LM = G("LM", [128, 4])
    small = G("small3", [128, 64])
    BH = G("BH", [128, 4, NT])
    R1 = sb("R1", [128, 2, NT], F32, h0 + 16384)
    RD = G("RD", [128, 8])

    GB = sb("GB", [128, 4, 384], F32, h0)
    s_b = new_sem("s_b")
    for h in range(4):
        b = take()
        rel = vec[0:32, V_REL + h:V_REL + h + 1].broadcast_to([32, 128])
        t = mmt(bank[b][:, 0:384], rel, cst[0:32, C_ONEHOT:C_ONEHOT + 384], True, True, t_cst, t_vec)
        t = act.do(call(nc.scalar.activation, GB[:, h, :], bank[b][:, 0:384], ACT.Copy), t)
        give(b, t)
    sp.wait(t)
    load(scratch, GB[:, :, :], s_b)
    sp.wait((s_b, 16))
    skew = bass.AP(scratch.tensor, 127, [[1535, 128], [384, 4], [1, 256]])
    load(BH[:, :, 256:512], skew, s_b)
    far = GB[:, :, 0:1].broadcast_to([128, 4, 256])
    dve.do(call(nc.vector.tensor_copy, BH[:, :, 0:256], far), t)
    diag = BH[:, :, 384:512]
    t_bh = dve.do(call(nc.vector.tensor_tensor, diag, diag, causal.unsqueeze(1).broadcast_to([128, 4, 128]), ALU.add),
                  (s_b, 32), t_cst)

    lv = lambda i: vec[0:64, V_LAM + i:V_LAM + i + 1]
    dve.do(call(nc.vector.tensor_tensor, LA[:, 0:1], lv(0), lv(1), ALU.mult), t_vec)
    t = dve.do(call(nc.vector.tensor_tensor, LA[:, 1:2], lv(2), lv(3), ALU.mult))
    b = take()
    t = mmt(bank[b][:, 0:2], ones[0:64, :], LA[:, :], True, True, t)
    t = act.do(call(nc.scalar.activation, LM[:, 0:2], bank[b][:, 0:2], ACT.Exp), t)
    give(b, t)
    t = dve.do(call(nc.vector.tensor_tensor, LM[:, 2:3], LM[:, 1:2], LM[:, 0:1], ALU.subtract), t)
    t_lm = dve.do(call(nc.vector.tensor_scalar, LM[:, 3:4], LM[:, 2:3], -LAMBDA_INIT, None, ALU.add), t)
    t_sg = dve.do(call(nc.vector.tensor_scalar, LM[:, 0:1], vec[:, V_SUB:V_SUB + 1], 1.0 - LAMBDA_INIT, None, ALU.mult), t_lm)

    lin(8, 4, UH, UL, ready, times_r(Q, 0.125), hook=double_hook)
    lin(8, 4, UH, UL, ready, times_r(K))
    lin_tok(8, UH, UL, ready, CH, rows_r(V, 1))
    t_v = (act.sem, act.n)
    lin(8, 4, UH, UL, ready, times_r(YU))
    fence()

    RQ = G("RQ3", [128, 4])
    U = arena(u0, u1)
    PWT = U("PWT", [128, 3, NT])
    AM = sb("AM3", [128, 2, 256], F32, u0)
    RM = sb("RM3", [128, 256], F32, u0 + 2048)
    NSL = 3
    S4 = U("S4", [128, NSL, 2, NT])
    PT = U("PT3", [128, 4, NT])
    TN = U("TN3", [128, 2, NT])
    PW = U("PW", [128, 4, 128])
    OH = sb("OH3", [128, 4, NT], F32, t0 + 3 * 4 * NT * 4)
    MH = sb("MH3", [128, 8, 256], F32R, h0)
    ML = sb("ML3", [128, 8, 256], F32R, h0 + 16384)
    s_pw = new_sem("s_pw")
    sp.wait((pe.sem, pe.n))
    load(PW[:, :, :], A["pool_w"].rearrange("g c d -> c g d"), s_pw)
    pfree = None
    for g, w in enumerate(WINDOWS):
        src = YU[:, g, :]
        d, t = 1, None
        i = 0
        while d < w:
            dst = PWT[:, i % 2, :]
            pool.do(call(nc.gpsimd.tensor_copy, dst[:, 0:d], src[:, 0:d]), t, pfree)
            t = pool.do(call(nc.gpsimd.tensor_tensor, dst[:, d:NT], src[:, d:NT], src[:, 0:NT - d],
                                                                         ALU.add))
            src = dst
            d *= 2
            i += 1
        p = PWT[:, 2, :]
        u = YU[:, g, :]
        t = dve.do(call(nc.vector.scalar_tensor_tensor, p[:, w:NT], src[:, w:NT], 1.0 / w, u[:, w:NT],
                                                                  ALU.mult, ALU.subtract), t, pfree)
        ci = cst[:, C_CINV + 16 * g:C_CINV + 16 * g + w]
        t2 = dve.do(call(nc.vector.tensor_tensor, p[:, 0:w], src[:, 0:w], ci, ALU.mult), t_cst)
        t = dve.do(call(nc.vector.tensor_tensor, p[:, 0:w], p[:, 0:w], u[:, 0:w], ALU.subtract), t2)
        b = take()
        t = mmt(bank[b][:, :], PW[:, g, :], p, True, True, t, (s_pw, 16))
        pfree = t
        o = TN[:, g % 2, :]
        if g == 0:
            tnf = [None, None]
        t = dve.do(call(nc.vector.tensor_scalar, o, bank[b][:, :], vec[:, V_PS + g:V_PS + g + 1], None,
                                                            ALU.mult), t, tnf[g % 2])
        give(b, t)
        tnf[g % 2] = hilo(HH[:, 4 + g, :], HL[:, 4 + g, :], o, None, t)
        ready_h[4 + g] = [tnf[g % 2]]

    fence()
    fill = Filler([mem_steps(1, MH, ML, AM, RM, RQ)], 1.6)
    fill()
    items = [dict(h=h, i=i, n=h * 4 + i, ns=128 * (i + 1)) for h in range(4) for i in range(4)]
    sf = [None] * NSL
    smf = [None] * 4
    ptf = None
    t_oh = []

    def d0(x):
        h, i, ns = x["h"], x["i"], x["ns"]
        x["b"] = [take(), take()]
        for j in range(2):
            r = slice(64 * j, 64 * j + 64)
            x["t"] = mmt(bank[x["b"][j]][:, 0:ns], Q[r, h, 128 * i:128 * i + 128], K[r, h, 0:ns], True, True)

    def d1(x):
        h, s, ns = x["h"], x["n"] % NSL, x["ns"]
        m = small[:, 8 * (x["n"] % 4):8 * (x["n"] % 4) + 8]
        x["e"] = []
        ts = []
        for j in range(2):
            S, b = S4[:, s, j, 0:ns], x["b"][j]
            t = dve.do(call(nc.vector.tensor_tensor, S, bank[b][:, 0:ns], BH[:, h, NT - ns:NT], ALU.add),
                       x["t"], sf[s], t_bh)
            give(b, t)
            ts.append(t)
        for j in range(2):
            S = S4[:, s, j, 0:ns]
            t = dve.do(call(nc.vector.tensor_reduce, m[:, j:j + 1], S, AX.X, ALU.max, negate=True), ts[j],
                       smf[x["n"] % 4])
            x["e"].append(act.do(call(nc.scalar.activation, S, S, ACT.Exp, bias=m[:, j:j + 1],
                                      accum_out=m[:, 2 + j:3 + j]), t))

    def d2(x):
        s, ns = x["n"] % NSL, x["ns"]
        m = small[:, 8 * (x["n"] % 4):8 * (x["n"] % 4) + 8]
        A_, B_ = S4[:, s, 0, 0:ns], S4[:, s, 1, 0:ns]
        t = dve.do(call(nc.vector.reciprocal, m[:, 4:6], m[:, 2:4]), *x["e"])
        t2 = dve.do(call(nc.vector.tensor_tensor, m[:, 6:7], m[:, 5:6], LM[:, 3:4], ALU.mult), t_lm, t)
        t1 = dve.do(call(nc.vector.tensor_scalar, A_, A_, m[:, 4:5], None, ALU.mult), t)
        x["t"] = dve.do(call(nc.vector.scalar_tensor_tensor, A_, B_, m[:, 6:7], A_, ALU.mult, ALU.add), t1, t2)
        smf[x["n"] % 4] = x["t"]

    def d3(x):
        s = x["n"] % NSL
        b = take()
        pe.wait(x["t"])
        for j in range(x["i"] + 1):
            t = pe.do(call(nc.tensor.transpose, bank[b][:, 128 * j:128 * j + 128],
                           S4[:, s, 0, 128 * j:128 * j + 128], ident))
        sf[s] = t
        x["tb"] = (b, t)

    def d4(x):
        i = x["i"]
        b, t = x["tb"]
        x["a"] = act.do(call(nc.scalar.activation, PT[:, 0:i + 1, 128 * i:128 * i + 128],
                             bank[b][:, 0:128 * (i + 1)].rearrange("p (j n) -> p j n", n=128), ACT.Copy), t, ptf)
        give(b, x["a"])

    def d5(x):
        nonlocal ptf
        if x["i"] < 3:
            return
        h, o = x["h"], take()
        x["o"] = o
        pe.wait(x["a"], t_v)
        for j in range(4):
            ptf = mmt(bank[o][:, 128 * j:NT], V[:, j, 128 * h:128 * h + 128], PT[:, j, 128 * j:NT], j == 0, j == 3)
        x["t"] = ptf

    def d6(x):
        if x["i"] < 3:
            return
        a = act.do(call(nc.scalar.activation, OH[:, x["h"], :], bank[x["o"]][:, :], ACT.Copy), x["t"])
        give(x["o"], a)
        t_oh.append(a)

    pipeline(items, [d0, d1, d2, d3, d4, d5, d6], fill)
    fill.finish()
    pool.wait(*tnf)
    ready_h[0:4] = head_norm(OH, 0, LM[:, 0:1], t_oh[-1], None, TN, t_sg, [*tnf, (pe.sem, pe.n)])
    for g in range(2):
        lin(8, 4, HH, HL, ready_h, residual(4 * g, vec[:, V_XA2:V_XA2 + 8]), ranges=((0, NT),), ks=ORDER2)

    g0 = t0

    def cross(l):
        fence()
        G = arena(g0, END1)
        QX = G(f"QX{l}", [128, 8, NT])
        S = G(f"SX{l}", [128, 4, 2, 256])
        PT = G(f"PX{l}", [128, 2, 4, NT])
        small = G(f"small{l}x", [128, 64])

        for g in range(2):
            def evac(m, p, t, n0, n, g=g):
                return dve.do(call(nc.vector.scalar_tensor_tensor, QX[:, 4 * g + m, :], p, 1.0 / 16, RB[:, xc],
                                   ALU.mult, ALU.mult), t, nm_.rb)
            lin(8, 4, UH, UL, ready, evac, hook=rms_hook if g == 0 else None)
        items = [dict(h=h, i=i, n=4 * h + i) for h in range(2) for i in range(4)]
        sf = [None] * 4
        mf = [None] * 4
        qt = (dve.sem, dve.n)
        pe.wait(qt, (act.sem, act.n))

        def c0(x):
            b = take()
            for j in range(2):
                for d in range(2):
                    k = 4 * x["h"] + 2 * j + d
                    t = mmt(bank[b][:, 256 * j:256 * j + 256], QX[:, k, 128 * x["i"]:128 * x["i"] + 128],
                            KM[l][:, k, :], d == 0, d == 1)
            x["b"], x["t"] = b, t

        def c1(x):
            s = x["n"] % 4
            b = x["b"]
            m = small[:, 8 * s:8 * s + 8]
            t = dve.do(call(nc.vector.tensor_reduce, m[:, 0:2], bank[b][:, :].rearrange("p (j n) -> p j n", j=2), AX.X,
                            ALU.max, negate=True), x["t"], mf[s])
            for j in range(2):
                x["e"] = act.do(call(nc.scalar.activation, S[:, s, j, :], bank[b][:, 256 * j:256 * j + 256], ACT.Exp,
                                     bias=m[:, j:j + 1], accum_out=m[:, 2 + j:3 + j]), t, sf[s])
            give(b, x["e"])

        def c2(x):
            s = x["n"] % 4
            m = small[:, 8 * s:8 * s + 8]
            t = dve.do(call(nc.vector.reciprocal, m[:, 4:6], m[:, 2:4]), x["e"])
            dve.wait(t)
            for j in range(2):
                t = dve.do(call(nc.vector.tensor_scalar, S[:, s, j, :], S[:, s, j, :], m[:, 4 + j:5 + j], None,
                                ALU.mult))
            mf[s] = x["t"] = t

        def c3(x):
            s = x["n"] % 4
            b = take()
            pe.wait(x["t"])
            for j in range(4):
                t = pe.do(call(nc.tensor.transpose, bank[b][:, 128 * j:128 * j + 128],
                               S[:, s, j // 2, 128 * (j % 2):128 * (j % 2) + 128], ident))
            sf[s] = t
            x["tb"] = (b, t)

        def c4(x):
            b, t = x["tb"]
            h, i = x["h"], x["i"]
            o = PT[:, h % 2, :, 128 * i:128 * i + 128]
            src = bank[b][:, :].rearrange("p (j n) -> p j n", n=128)
            if i % 2:
                x["a"] = act.do(call(nc.scalar.activation, o, src, ACT.Copy), t)
            else:
                x["a"] = dve.do(call(nc.vector.tensor_copy, o, src), t)
            give(b, x["a"])
            pe_waits.append(x["a"])

        def c5(x):
            if x["i"] < 3:
                return
            h = x["h"]
            pe.wait(*pe_waits)
            for d in range(4):
                o = take()
                k = 4 * h + d
                for mb in range(2):
                    t = mmt(bank[o][:, :], VM[l][:, mb, 128 * k:128 * k + 128], PT[:, h % 2, 2 * (d // 2) + mb, :],
                            mb == 0, mb == 1)
                a = act.do(call(nc.scalar.activation, HH[:, k, :], bank[o][:, :], ACT.Copy), t)
                t = dve.do(call(nc.vector.tensor_tensor, HL[:, k, :], bank[o][:, :], HH[:, k, :].bitcast(F32),
                                ALU.subtract), a)
                give(o, t)
                ready_h[k] = [t]

        pe_waits = []
        pipeline(items, [c0, c1, c2, c3, c4, c5])
        for g in range(2):
            lin(8, 4, HH, HL, ready_h, residual(4 * g, vec[:, V_MLP2 + 8 * l:V_MLP2 + 8 * l + 8]),
                ranges=((0, NT),))

    def mlp(l, wnext):
        fence()
        F = arena(g0, END1)
        T = F(f"TM{l}", [128, 8, NT])
        tf = [None] * 8
        n = 0
        first = True
        for c in range(4):
            for g in range(2):
                def evac(m, p, tok, n0, nn, g=g):
                    nonlocal n
                    i, j = n % 8, (n + 1) % 8
                    n += 2
                    x, y = T[:, i, :], T[:, j, :]
                    k = 4 * g + m
                    a = dve.do(call(nc.vector.scalar_tensor_tensor, x, p, 0.0, RB[:, xc], ALU.max, ALU.mult), tok, nm_.rb,
                               tf[i])
                    t = act.do(call(nc.scalar.activation, y, x, ACT.Square), a, tf[j])
                    tf[i] = t
                    h = act.do(call(nc.scalar.activation, HH[:, k, :], y, ACT.Copy), t)
                    flush()

                    def lo():
                        tf[j] = dve.do(call(nc.vector.tensor_tensor, HL[:, k, :], y, HH[:, k, :].bitcast(F32),
                                            ALU.subtract), h, t)
                        ready_h[k] = [tf[j]]
                    late.append(lo)
                    return a
                lin(8, 4, UH, UL, ready, evac, hook=rms_hook if first else None)
                first = False
            for g in range(2):
                lin(8, 4, HH, HL, ready_h, residual(4 * g, wnext, last=c == 3), ranges=((0, NT),))

    cross(0)
    mlp(0, vec[:, V_MIX2 + 8:V_MIX2 + 16])

    fence()
    F = arena(g0, END1)
    T = F("TC", [128, 16, NT])
    tf = [None] * 16
    n_ = [0]

    def tmp():
        i = n_[0] % 16
        n_[0] += 1
        return T[:, i, :], i

    for j in range(8):
        got = {}

        def evac(m, p, tok, n0, n, j=j):
            x, i = tmp()
            a = dve.do(call(nc.vector.tensor_tensor, x, p, RB[:, xc], ALU.mult), tok, nm_.rb, tf[i])
            got[m] = (x, i, a)
            if m == 2:
                (bx_, ib, tb), (cx, ic, tc), (xx, ix, tx) = got[0], got[1], got[2]
                t = dve.do(call(nc.vector.tensor_tensor, cx, cx, xx, ALU.mult), tc, tx)
                tf[ix] = t
                y, iy = tmp()
                w = [vec[:, V_CONV + 8 * q + j:V_CONV + 8 * q + j + 1] for q in range(3)]
                t2 = act.do(call(nc.scalar.activation, y, cx, ACT.Copy, scale=w[2]), t, tf[iy])
                t2 = dve.do(call(nc.vector.scalar_tensor_tensor, y[:, 1:NT], cx[:, 0:NT - 1], w[1], y[:, 1:NT], ALU.mult,
                                                             ALU.add), t2)
                t2 = dve.do(call(nc.vector.scalar_tensor_tensor, y[:, 2:NT], cx[:, 0:NT - 2], w[0], y[:, 2:NT], ALU.mult,
                                                             ALU.add), t2)
                tf[ic] = t2
                t2 = dve.do(call(nc.vector.tensor_tensor, y, y, bx_, ALU.mult), t2, tb)
                tf[ib] = t2
                tf[iy] = hilo(HH[:, j, :], HL[:, j, :], y, None, t2)
                ready_h[j] = [tf[iy]]
            return a
        lin(8, 3, UH, UL, ready, evac, hook=rms_hook if j == 0 else None)
    for g in range(2):
        lin(8, 4, HH, HL, ready_h, residual(4 * g, vec[:, V_XA2 + 8:V_XA2 + 16]), ranges=((0, NT),))
    cross(1)
    mlp(1, None)
    rms_hook()
    s_o = new_sem("s_o")
    for k in range(8):
        t = dve.do(call(nc.vector.scalar_tensor_tensor, H[:, k, xc], H[:, k, xc],
                                                         vec[:, V_FIN2 + k:V_FIN2 + k + 1],
                                                         RB[:, xc], ALU.mult, ALU.mult), nm_.rb, nm_.acc)
        sp.wait(t)
        load(out[128 * k:128 * k + 128, :], H[:, k, xc], s_o)
    sp.wait((s_o, 128), (s_b, 32))
    assert st.pos == len(tiles), (st.pos, len(tiles))

    block = nc.Block()
    with block:
        block.sync(lambda e: sp.run(e))
        block.scalar(lambda e: act.run(e))
        block.vector(lambda e: dve.run(e))
        block.gpsimd(lambda e: pool.run(e))
        block.tensor(lambda e: pe.run(e))
    for cm in reversed(held):
        cm.__exit__(None, None, None)


def buckets():
    import math
    out = []
    for n in range(256):
        if n < 16:
            out.append(n)
        else:
            out.append(min(16 + int(math.log(n / 16) / math.log(8) * 16 + 1e-9), 31))
    return out


def constants():
    c = np.zeros((128, NCONST), np.float32)
    c[:, C_ID:C_ID + 128] = np.eye(128)
    i = np.arange(128)
    c[:, C_CAUSAL:C_CAUSAL + 128] = np.where(i[None, :] <= i[:, None], 0.0, -1e30)
    bk = buckets()
    for j in range(384):
        c[bk[max(255 - j, 0)], C_ONEHOT + j] = 1.0
    for g, w in enumerate(WINDOWS):
        for t in range(w):
            c[:, C_CINV + 16 * g + t] = 1.0 / min(t + 1, w)
    m = np.zeros((128, 7, 128), np.float32)
    s, t = i[:, None], i[None, :]
    m[:, 0] = (s // 2 == t // 2) & (s <= t)
    for l, n in enumerate(LEVELS):
        m[:, l + 1] = (s // (2 * n) == t // (2 * n)) & (s % (2 * n) < n) & (t % (2 * n) >= n)
    return c, m.reshape(128, 7 * 128)


def kernel(**inputs):
    import concourse.bacc as bacc
    from concourse.bass_utils import run_bass_kernel_spmd as run

    I = {k: np.asarray(v) for k, v in inputs.items()}
    w_in = I["w_in"][0]
    ff = np.zeros((1024, 128), np.float32)
    ff[:, 0:8] = w_in[:, 1536:1544]
    mats = {"w_in": w_in[:, 0:1536], "ff": ff, "hgrn": w_in[:, 1544:], "w_out": I["w_out"][0],
            "w_ffn_gate": I["w_ffn_gate"][0], "w_ffn_up": I["w_ffn_up"][0], "w_ffn_down": I["w_ffn_down"][0],
            "ab_w_in_2": I["ab_w_in_2"][0], "ab_w_out_2": I["ab_w_out_2"][0], "conv_w_in_2": I["conv_w_in_2"][0],
            "conv_w_out_2": I["conv_w_out_2"][0]}
    for n in ("xattn_wkv_2", "xattn_wq_2", "xattn_wo_2", "mlp_w1_2", "mlp_w2_2"):
        for l in range(2):
            mats[f"{n}.{l}"] = I[n][l]
    tiles = [t for lot in plan() for t in lot]
    stream = np.empty((len(tiles) // 8, 128, 1024), np.float32)
    for i, (n, k, c) in enumerate(tiles):
        stream[i // 8, :, 128 * (i % 8):128 * (i % 8) + 128] = mats[n][128 * k:128 * k + 128, 128 * c:128 * c + 128]

    vecs = np.zeros((128, NVEC), np.float32)

    def put(col, v):
        vecs[:, col:col + v.size // 128] = v.reshape(-1, 128).T

    put(V_MIX, I["norm_mix_w"][0])
    put(V_FFN, I["norm_ffn_w"][0])
    put(V_FIN, I["norm_final_w"])
    put(V_MEM, I["mem_norm_g_2"])
    for l in range(2):
        put(V_MIX2 + 8 * l, I["norm_mix_g_2"][l])
        put(V_XA2 + 8 * l, I["norm_xattn_g_2"][l])
        put(V_MLP2 + 8 * l, I["norm_mlp_g_2"][l])
    put(V_FIN2, I["final_norm_g_2"])
    put(V_LB, I["hgrn_lb_raw"][0])
    put(V_HN, I["hgrn_norm_w"][0])
    put(V_SUB, I["subln_g_2"][0])
    put(V_PS, I["pool_scale_2"][0])
    for q in range(3):
        put(V_CONV + 8 * q, I["conv_w_2"][0, q])
    vecs[0:8, V_FB] = I["fox_f_bias"][0]
    for i, n in enumerate(("lambda_q1_2", "lambda_k1_2", "lambda_q2_2", "lambda_k2_2")):
        vecs[0:64, V_LAM + i] = I[n][0]
    vecs[0:32, V_REL:V_REL + 4] = I["rel_bias_2"]
    consts, masks = constants()
    arrays = {
        "hT": np.ascontiguousarray(np.concatenate([I["meta"], I["x"][0]], 0).T),
        "memT": np.ascontiguousarray(I["mem_2"][0].T),
        "stream": stream, "vecs": vecs, "consts": consts, "masks": masks,
        "pool_w": np.ascontiguousarray(I["pool_w_2"][0]),
    }
    nc = bacc.Bacc("TRN2", target_bir_lowering=False, num_devices=1)
    A = {n: nc.dram_tensor(n, a.shape, mybir.dt.from_np(a.dtype), kind="ExternalInput").ap()
         for n, a in arrays.items()}
    out = nc.dram_tensor("outT", (1024, NT), F32, kind="ExternalOutput").ap()
    scratch = nc.dram_tensor("skew", (128, 4, 384), F32, kind="Internal").ap()
    rows = nc.dram_tensor("rows", (8, NA), F32, kind="Internal").ap()
    build(nc, A, out, scratch, rows)
    r = run(nc, [arrays], core_ids=[0])
    return np.ascontiguousarray(np.asarray(r.results[0]["outT"]).T)[None]
```

```python
import concourse.bass as bass
from concourse import mybir
from collections import deque
import numpy as np

F32 = mybir.dt.float32
F32R = mybir.dt.float32r
U8 = mybir.dt.uint8
ACT = mybir.ActivationFunctionType
ALU = mybir.AluOpType
AX = mybir.AxisListType

NT = 512
NM = 16
NA = NT + NM
EPS = 1e-6
FMIN = float(np.exp(-30.0))
LAMBDA_INIT = 0.2
WINDOWS = (2, 4, 8, 16)
LEVELS = (2, 4, 8, 16, 32, 64)

V_MIX, V_FFN, V_FIN, V_MEM = 0, 8, 16, 24
V_MIX2, V_XA2, V_MLP2, V_FIN2 = 32, 48, 64, 80
V_LB, V_HN, V_SUB, V_PS, V_CONV, V_FB, V_LAM, V_REL = 88, 92, 93, 94, 98, 122, 123, 127
NVEC = 131
C_ID, C_CAUSAL, C_ONEHOT, C_CINV = 0, 128, 256, 640
NCONST = 704

HIDDEN = (8, 8, 6)


def plan():
    out = []

    def lot(name, ks, cols):
        out.append([(name, k, c) for k in ks for c in cols])

    def wide(name, ks, c0, n, w=4):
        for c in range(c0, c0 + n, w):
            lot(name, ks, range(c, c + w))

    k8 = range(8)
    wide("w_in", k8, 0, 8)
    lot("ff", k8, [0])
    wide("w_in", k8, 8, 4)
    wide("hgrn", k8, 8, 4)
    wide("hgrn", k8, 0, 4)
    wide("hgrn", k8, 4, 4, 2)
    wide("hgrn", k8, 12, 4)
    wide("xattn_wkv_2.0", k8, 0, 16)
    wide("w_out", range(0, 4), 0, 8)
    wide("w_out", range(4, 8), 0, 8)
    f0 = 0
    for nh in HIDDEN:
        for j in range(f0, f0 + nh, 2):
            out.append([(n, k, c) for k in range(8)
                        for n, c in (("w_ffn_gate", j), ("w_ffn_gate", j + 1), ("w_ffn_up", j), ("w_ffn_up", j + 1))])
        wide("w_ffn_down", range(f0, f0 + nh), 0, 8)
        f0 += nh
    wide("ab_w_in_2", k8, 12, 4)
    wide("ab_w_in_2", k8, 0, 12)
    wide("xattn_wkv_2.1", k8, 0, 16)
    wide("ab_w_out_2", range(4, 8), 0, 8)
    wide("ab_w_out_2", range(0, 4), 0, 8)
    for l in range(2):
        if l == 1:
            for j in range(8):
                lot("conv_w_in_2", k8, [j, 8 + j, 16 + j])
            wide("conv_w_out_2", k8, 0, 8)
        wide(f"xattn_wq_2.{l}", k8, 0, 8)
        wide(f"xattn_wo_2.{l}", k8, 0, 8)
        for c in range(4):
            wide(f"mlp_w1_2.{l}", k8, 8 * c, 8)
            wide(f"mlp_w2_2.{l}", range(8 * c, 8 * c + 8), 0, 8)
    return out


def call(fn, *args, **kwargs):
    return lambda e: fn(*args, **kwargs)


class Engine:

    def __init__(self, sem):
        self.sem, self.n, self.ops, self.seen = sem, 0, [], {}

    def wait(self, *tokens):
        for t in tokens:
            if t is None:
                continue
            sem, n = t
            if self.seen.get(id(sem), 0) < n:
                self.seen[id(sem)] = n
                self.ops.append(lambda e, sem=sem, n=n: e.wait_ge(sem, n))

    def do(self, fn, *tokens):
        self.wait(*tokens)
        self.n += 1
        self.ops.append(lambda e: fn(e).then_inc(self.sem, 1))
        return (self.sem, self.n)

    def go(self, fn):
        self.ops.append(fn)

    def run(self, e):
        for op in self.ops:
            op(e)


def build(nc, A, out, scratch, rows):
    held = []

    def new_sem(name):
        cm = nc.semaphore(name)
        held.append(cm)
        return cm.__enter__()

    pe, act, dve, pool, sp = (Engine(new_sem(f"s_{n}")) for n in ("pe", "act", "dve", "pool", "sp"))
    at = [16512]

    def sb(name, shape, dt=F32, offset=None):
        size = (int(np.prod(shape[1:])) * (1 if dt == U8 else 4) + 63) // 64 * 64
        if offset is None:
            offset = at[0]
            at[0] += size
            assert at[0] <= 229344, (name, at[0])
        return nc.alloc_sbuf_tensor_at(name, shape, dt, offset=offset)

    def arena(begin, end):
        p = [begin]

        def get(name, shape, dt=F32):
            t = sb(name, shape, dt, p[0])
            p[0] += (int(np.prod(shape[1:])) * (1 if dt == U8 else 4) + 63) // 64 * 64
            assert p[0] <= end, (name, p[0], end)
            return t
        return get

    bank = []
    for i in range(8):
        cm = nc.psum_tensor(f"ps{i}", [128, 512], F32)
        held.append(cm)
        bank.append(cm.__enter__())
    free = deque((i, None) for i in range(8))

    def take():
        i, tok = free.popleft()
        pe.wait(tok)
        return i

    def give(i, tok):
        free.append((i, tok))

    NR, NS = 3, 6
    raw = sb("raw", [128, NR, 1024])
    WH = sb("WH", [128, NS, 512], F32R)
    WL = sb("WL", [128, NS, 512], F32R)
    H = sb("H", [128, 8, NA])
    cst = sb("cst", [128, NCONST])
    msk = sb("msk", [128, 7, 128], U8)
    vec = sb("vec", [128, NVEC])
    ones = sb("ones", [128, 128])
    RB = sb("RB", [128, NA])
    RC = sb("RC", [128, 5])
    DG = sb("DG", [128, 4, 128])
    ACC = sb("ACC", [128, NA])
    SQ = sb("SQ", [128, 2, NA])
    eps = sb("eps", [128, 1])
    LB = sb("LB", [128, 6, 4])
    HN = sb("HN", [128, 16])
    u0 = at[0]
    UH = sb("UH", [128, 8, NA], F32R)
    UL = sb("UL", [128, 8, NA], F32R)
    u1 = at[0]
    h0 = at[0]
    HH = sb("HH", [128, 8, NT], F32R)
    HL = sb("HL", [128, 8, NT], F32R)
    t0 = at[0]
    END = 229344
    END0, END1 = END - 16384, END - 32768
    KM, VM = [], []
    for l, o in enumerate((END0, END1)):
        KM.append(sb(f"KM{l}", [128, 8, 256], F32, o))
        VM.append(sb(f"VM{l}", [128, 2, 1024], F32, o + 8192))
    ident = cst[:, C_ID:C_ID + 128]
    causal = cst[:, C_CAUSAL:C_CAUSAL + 128]

    s_c = new_sem("s_cst")
    s_v = new_sem("s_vec")
    s_h = [new_sem(f"s_h{i}") for i in range(8)]

    def load(dst, src, sem):
        sp.ops.append(lambda e: e.dma_start(dst, src).then_inc(sem, 16))

    load(vec[:, :], A["vecs"], s_v)

    tiles = [t for lot in plan() for t in lot]
    assert len(tiles) % 8 == 0
    NU = len(tiles) // 8
    s_w = [new_sem(f"s_w{i}") for i in range(NR)]
    wdram = A["stream"]

    class Stream:
        made = 0
        lo = {}
        used = {}
        pos = 0

    st = Stream()

    def split(v):
        r, s, c = (v // 2) % NR, v % NS, slice(512 * (v % 2), 512 * (v % 2) + 512)
        if v % 2 == 0:
            sp.wait(st.lo.get(v - 2 * NR + 1))
            load(raw[:, r, :], wdram[v // 2], s_w[r])
        landed = (s_w[r], 16 * (v // 2 // NR + 1))
        hi = act.do(call(nc.scalar.activation, WH[:, s, :], raw[:, r, c], ACT.Copy), landed, st.used.get(v - NS))
        st.lo[v] = dve.do(call(nc.vector.tensor_tensor, WL[:, s, :], raw[:, r, c], WH[:, s, :].bitcast(F32),
                               ALU.subtract), hi, landed, st.used.get(v - NS))

    def weights(n):
        v, j = st.pos // 4, st.pos % 4
        assert j + n <= 4
        if j == 0:
            while st.made < min(v + 5, 2 * NU):
                split(st.made)
                st.made += 1
            pe.wait(st.lo[v])
        st.pos += n
        c = slice(128 * j, 128 * (j + n))
        return WH[:, v % NS, c], WL[:, v % NS, c], (v if st.pos % 4 == 0 else None)

    def mm(o, l, r, start, stop):
        pe.go(call(nc.tensor.matmul, o, l, r, start=start, stop=stop, skip_group_check=True))

    def mmt(o, l, r, start, stop, *tokens):
        return pe.do(call(nc.tensor.matmul, o, l, r, start=start, stop=stop, skip_group_check=True), *tokens)

    def passes(o, ah, al, bh, bl, start, stop, token):
        mm(o, ah, bh, start, False)
        mm(o, ah, bl, False, False)
        return (mmt if token else mm)(o, al, bh, False, stop)

    late = []

    def flush():
        while late:
            late.pop(0)()

    def lin_steps(nk, nm, XH, XL, ready, evac, ranges=((NM, NT),), hook=None, ks=None):
        ks = ks or range(nk)
        bk, fin = {}, {}
        for i, k in enumerate(ks):
            pe.wait(*ready[k])
            end = i == nk - 1
            for m in range(nm):
                wh, wl, last = weights(1)
                for n0, n in ranges:
                    if i == 0:
                        bk[m, n0] = take()
                    o = bank[bk[m, n0]][:, 0:n]
                    mm(o, wh, XH[:, k, n0:n0 + n], i == 0, False)
                    mm(o, wh, XL[:, k, n0:n0 + n], False, False)
                for n0, n in ranges:
                    o = bank[bk[m, n0]][:, 0:n]
                    if end or last is not None:
                        fin[m, n0] = mmt(o, wl, XH[:, k, n0:n0 + n], False, end)
                    else:
                        mm(o, wl, XH[:, k, n0:n0 + n], False, end)
                if last is not None:
                    st.used[last] = fin[m, n0]
            if hook and i in hook:
                hook[i]()
            yield
        for m in range(nm):
            for n0, n in ranges:
                give(bk[m, n0], evac(m, bank[bk[m, n0]][:, 0:n], fin[m, n0], n0, n))
        flush()

    def tok_steps(nk, XH, XL, ready, chunks, evac):
        bk = []
        for k in range(nk):
            pe.wait(*ready[k])
            wh, wl, last = weights(4)
            for i, c in enumerate(chunks):
                if k == 0:
                    bk.append(take())
                tok = passes(bank[bk[i]][:, :], XH[:, k, c:c + 128], XL[:, k, c:c + 128], wh, wl, k == 0,
                             k == nk - 1, True)
            st.used[last] = tok
            yield
        for i, c in enumerate(chunks):
            give(bk[i], evac(i, bank[bk[i]], tok))

    def lin(*args, **kwargs):
        for _ in lin_steps(*args, **kwargs):
            pass

    def lin_tok(*args, **kwargs):
        for _ in tok_steps(*args, **kwargs):
            pass

    class Filler:

        def __init__(self, gens, rate):
            self.gens, self.rate, self.due = list(gens), rate, 0.0

        def __call__(self, n=1.0):
            self.due += n * self.rate
            while self.due >= 1 and self.gens:
                self.due -= 1
                self.one()

        def one(self):
            for _ in self.gens[0]:
                return
            self.gens.pop(0)
            if self.gens:
                self.one()

        def finish(self):
            while self.gens:
                self.one()

    class Norm:
        used = None
        chunks = None
        acc = None
        read = None
        sq = [None, None]
        rb = None
        rc = None
    nm_ = Norm()

    def square_in(k, src, n0, n, tok):
        c = slice(n0, n0 + n)
        if k == 0:
            nm_.acc = act.do(call(nc.scalar.activation, ACC[:, c], src, ACT.Square), tok, nm_.read)
        else:
            s = SQ[:, k % 2, c]
            a = act.do(call(nc.scalar.activation, s, src, ACT.Square), tok, nm_.sq[k % 2])
            nm_.acc = pool.do(call(nc.gpsimd.tensor_tensor, ACC[:, c], ACC[:, c], s, ALU.add), a, nm_.acc)
            nm_.sq[k % 2] = nm_.acc

    def columns(accs, chunks, dst, off, size, tok, *users):
        k = len(chunks)
        b = take()
        pe.wait(tok, t_ones)
        for i, c in enumerate(chunks):
            for j, acc in enumerate(accs):
                t = mmt(bank[b][:, i:i + 1], acc[:, c:c + 128], ones[:, 0:1], j == 0, j == len(accs) - 1)
        a = act.do(call(nc.scalar.activation, dst[:, off:off + k], bank[b][:, 0:k], ACT.Sqrt, bias=eps[:, :],
                        scale=1.0 / size), t, t_eps, *users)
        give(b, a)
        return dve.do(call(nc.vector.reciprocal, dst[:, off:off + k], dst[:, off:off + k]), a), t

    def spread(col, n, dst, places, tok, *users):
        b = take()
        ts = []
        for j, (i, c) in enumerate(places):
            g = DG[:, (dgn[0] + j) % 4, 0:n]
            a = dve.do(call(nc.vector.tensor_scalar, g[0:n, :], cst[0:n, C_ID:C_ID + n], col[0:n, i:i + 1], None,
                            ALU.mult), tok, t_cst, dgf[(dgn[0] + j) % 4])
            t = mmt(bank[b][:, n * j:n * j + n], ones[0:n, :], g[0:n, :], True, True, a)
            dgf[(dgn[0] + j) % 4] = t
        dgn[0] += len(places)
        c0 = places[0][1]
        a = act.do(call(nc.scalar.activation, dst[:, c0:c0 + n * len(places)], bank[b][:, 0:n * len(places)],
                        ACT.Copy), t, *users)
        give(b, a)
        return a

    dgn, dgf = [0], [None] * 4

    def norm_columns(chunks):
        nm_.rc, nm_.read = columns([ACC], chunks, RC, 0, 1024, nm_.acc, nm_.used)
        nm_.chunks = chunks

    def norm_rows():
        p = [(i, c) for i, c in enumerate(nm_.chunks) if c >= NM]
        users = [(dve.sem, dve.n), nm_.rc]
        nm_.rb = spread(RC, 128, RB, p, nm_.rc, *users)
        if len(p) < len(nm_.chunks):
            nm_.rb = spread(RC, NM, RB, [(0, 0)], nm_.rc)
        nm_.used = nm_.rb

    def hilo(hi, lo, src, w, tok, *free_):
        if w is None:
            a = act.do(call(nc.scalar.activation, hi, src, ACT.Copy), tok, *free_)
            return dve.do(call(nc.vector.tensor_tensor, lo, src, hi.bitcast(F32), ALU.subtract), a, tok, *free_)
        a = act.do(call(nc.scalar.activation, hi, src, ACT.Copy, scale=w), tok, *free_)
        return dve.do(call(nc.vector.scalar_tensor_tensor, lo, src, w, hi.bitcast(F32), ALU.mult, ALU.subtract),
                      a, tok, *free_)

    ready = [[] for _ in range(8)]
    all_col = slice(0, NA)
    xc = slice(NM, NA)
    CH = [NM + 128 * i for i in range(4)]

    def residual(m0, wcol, last=True, also=None, tail=None):
        def evac(m, p, tok, n0, n):
            k = m0 + m
            src = H[:, k, xc]
            t = dve.do(call(nc.vector.tensor_tensor, src, p, src, ALU.add), tok, h_tok[k])
            h_tok[k] = t
            flush()
            if last:
                if wcol is not None:
                    w = wcol[:, k:k + 1]
                    a = act.do(call(nc.scalar.activation, UH[:, k, xc], src, ACT.Copy, scale=w), t, t_w2)

                    def lo():
                        ready[k] = [dve.do(call(nc.vector.scalar_tensor_tensor, UL[:, k, xc], src, w,
                                                UH[:, k, xc].bitcast(F32), ALU.mult, ALU.subtract), a, t)]
                    late.append(lo)
                if also:
                    also(k, src, t)
                if tail is not None and k >= 4:
                    q = tail[0][:, k - 4, xc]
                    a = act.do(call(nc.scalar.activation, q, src, ACT.Square), t)

                    def add():
                        nm_.acc = dve.do(call(nc.vector.tensor_tensor, ACC[:, xc], ACC[:, xc], q, ALU.add), a,
                                         nm_.acc)
                    late.append(add)
                else:
                    square_in(k, src, NM, NT, t)
            return t
        return evac

    h_tok = [None] * 8

    t_ones = dve.do(call(nc.vector.memset, ones[:, :], 1.0))
    t_eps = dve.do(call(nc.vector.memset, eps[:, :], EPS))
    t_vec = t_w2 = (s_v, 16)
    t_cst = (s_c, 16)

    P1 = arena(t0, END)
    OM = P1("OM", [128, 4, NA])
    V2 = P1("V2", [128, 5, NT])
    r0 = t0 + (4 * NA + 5 * NT) * 4
    Q = P1("Q", [128, 4, NT])
    K = P1("K", [128, 4, NA])
    V = P1("V", [128, 5, NT])
    CT = P1("CT", [8, NA])
    CC = P1("CC", [128, 4, 8])
    small = P1("small", [128, 64])
    NB = P1("NB", [128, 2, NA])
    NSL = 5
    S2 = P1("S2", [128, NSL, NA])
    PM = P1("PM", [16, NT])
    PT = P1("PT", [128, 4, NT])
    FZ = sb("FZ", [8, 3, NA], F32, END0)
    HQ = sb("HQ", [128, 4, NT], F32, t0 - 4 * NT * 4)
    HG = sb("HG", [128, 4, NT], F32, t0 - 12 * NT * 4)
    MF = sb("MF", [128, 7, 128], F32, h0)

    for k in range(8):
        load(H[:, k, :], A["hT"][128 * k:128 * k + 128, :], s_h[k])
        t = (s_h[k], 16)
        ready[k] = [hilo(UH[:, k, :], UL[:, k, :], H[:, k, :], vec[:, V_MIX + k:V_MIX + k + 1], t, t_vec)]
        square_in(k, H[:, k, :], 0, NA, t)
        if k in (0, 2, 4):
            for v in (k, k + 1):
                if v < 5:
                    split(v)
                    st.made = v + 1
    load(cst[:, :], A["consts"], s_c)

    def load_constants():
        load(MF[:, :, :], A["masks"].rearrange("p (l n) -> p l n", l=7), s_c)
        return dve.do(call(nc.vector.tensor_copy, msk[:, :, :], MF[:, :, :]), (s_c, 32))


    hook0 = {6: lambda: norm_columns([0] + CH), 7: norm_rows}

    def times_r(dst, extra=None):
        off = NA - dst.shape[2]

        def evac(m, p, tok, n0, n):
            o = dst[:, m, n0 - off:n0 - off + n]
            if extra is None:
                return dve.do(call(nc.vector.tensor_tensor, o, p, RB[:, n0:n0 + n], ALU.mult), tok, nm_.rb)
            return dve.do(call(nc.vector.scalar_tensor_tensor, o, p, extra, RB[:, n0:n0 + n], ALU.mult, ALU.mult),
                          tok, nm_.rb)
        return evac

    def rows_r(dst, off):
        def evac(i, p, tok):
            rows = NM if (off == 0 and i == 0) else 128
            return act.do(call(nc.scalar.activation, dst[0:rows, i, :], p[0:rows, :], ACT.Copy,
                                                 scale=RC[0:rows, i:i + 1]), tok, nm_.rc)
        return evac

    lin(8, 4, UH, UL, ready, times_r(Q, 0.125), hook=hook0)
    t_msk = load_constants()
    TWO = ((0, NA // 2), (NA // 2, NA // 2))
    lin(8, 4, UH, UL, ready, times_r(K), ranges=TWO)

    def ff_evac(m, p, tok, n0, n):
        return dve.do(call(nc.vector.tensor_tensor, FZ[:, 0, n0:n0 + n], p[0:8, :], RB[0:8, n0:n0 + n], ALU.mult),
                      tok, nm_.rb)

    lin(8, 1, UH, UL, ready, ff_evac, ranges=TWO)
    t_z = (dve.sem, dve.n)
    t_z = dve.do(call(nc.vector.tensor_scalar, FZ[:, 0, :], FZ[:, 0, :], vec[0:8, V_FB:V_FB + 1], None, ALU.add),
                 t_z, t_vec)
    t = dve.do(call(nc.vector.scalar_tensor_tensor, FZ[:, 1, :], FZ[:, 0, :], -1.0, FZ[:, 0, :], ALU.mult, ALU.max), t_z)
    t = act.do(call(nc.scalar.activation, FZ[:, 1, :], FZ[:, 1, :], ACT.Exp, scale=-1.0), t)
    t = act.do(call(nc.scalar.activation, FZ[:, 2, :], FZ[:, 1, :], ACT.Ln, bias=ones[0:8, 0:1]), t)
    t = dve.do(call(nc.vector.scalar_tensor_tensor, FZ[:, 1, :], FZ[:, 0, :], 0.0, FZ[:, 2, :], ALU.min,
                                                ALU.subtract), t)
    t0_ = dve.do(call(nc.vector.memset, FZ[:, 2, :], -1.0), t)
    t = dve.do(call(nc.vector.tensor_scalar, FZ[:, 0, :], FZ[:, 2, :], -1.0, None, ALU.mult), t0_)
    t_ct = dve.do(call(nc.vector.tensor_tensor_scan, CT[:, :], FZ[:, 0, :], FZ[:, 1, :], 0.0, ALU.mult, ALU.add), t)
    t = dve.do(call(nc.vector.tensor_tensor, FZ[:, 1, :], CT[:, :], FZ[:, 2, :], ALU.mult), t_ct)
    s_nc = new_sem("s_nc")
    s_nb = [new_sem("s_nb0"), new_sem("s_nb1")]
    sp.wait(t)
    load(rows, FZ[:, 1, :], s_nc)
    lin_tok(8, UH, UL, ready, [0] + CH, rows_r(V, 0))
    t_v = (act.sem, act.n)
    b = take()
    for i in range(4):
        t = pe.do(call(nc.tensor.transpose, bank[b][:, 8 * i:8 * i + 8], CT[:, CH[i]:CH[i] + 128],
                                            cst[0:8, C_ID:C_ID + 8]), t_ct, t_cst)
    t_cc = act.do(call(nc.scalar.activation, CC[:, :, :], bank[b][:, 0:32].rearrange("p (i h) -> p i h", h=8),
                                         ACT.Copy), t)
    give(b, t_cc)

    s_m = new_sem("s_m")

    def mem_steps(l, MT, MH, ML, AM, RM, RQ):
        toks = [(pe.sem, pe.n), (dve.sem, dve.n), (act.sem, act.n), (pool.sem, pool.n)]
        yield
        sp.wait(*toks)
        load(MT[:, :, :], A["memT"].rearrange("(k p) n -> p k n", p=128), s_m)
        yield
        yield
        for x in (act, dve, pool):
            x.wait(*toks)
        landed = (s_m, 16 * (l + 1))
        rm = []
        for k in range(8):
            rm.append([hilo(MH[:, k, :], ML[:, k, :], MT[:, k, :], vec[:, V_MEM + k:V_MEM + k + 1], landed)])
            if k == 0:
                acc = act.do(call(nc.scalar.activation, AM[:, :], MT[:, 0, :], ACT.Square), landed)
            else:
                s = SQ[:, k % 2, 0:256]
                a = act.do(call(nc.scalar.activation, s, MT[:, k, :], ACT.Square), landed, nm_.sq[k % 2])
                acc = pool.do(call(nc.gpsimd.tensor_tensor, AM[:, :], AM[:, :], s, ALU.add), a, acc)
                nm_.sq[k % 2] = acc
            if k % 2 and k < 7:
                yield
        tr = tc = None

        def c():
            nonlocal tc
            tc, _ = columns([AM], [0, 128], RQ, 0, 1024, acc)

        def r():
            nonlocal tr
            tr = spread(RQ, 128, RM, [(0, 0), (1, 128)], tc)
        read = rm[7]
        yield
        for g in range(2):
            def evac(m, p, t, n0, n):
                return dve.do(call(nc.vector.tensor_tensor, KM[l][:, 4 * g + m, :], p, RM[:, :], ALU.mult), t, tr,
                              acc, *read)
            yield from lin_steps(8, 4, MH, ML, rm, evac, ranges=((0, 256),), hook={5: c, 7: r} if g == 0 else None)
        for g in range(2):
            def evac_v(i, p, t):
                return act.do(call(nc.scalar.activation, VM[l][:, i, 512 * g:512 * g + 512], p[:, :], ACT.Copy,
                                   scale=RQ[:, i:i + 1]), t, tc)
            yield from tok_steps(8, MH, ML, rm, [0, 128], evac_v)

    lin_tok(8, UH, UL, ready, [0] + CH, rows_r(V2, 0))
    t_v2 = (act.sem, act.n)
    ready_o = [[] for _ in range(8)]
    U = arena(u0, u1)
    MH = U("MH", [128, 8, 256], F32R)
    ML = U("ML", [128, 8, 256], F32R)
    AM = U("AM", [128, 256])
    RM = U("RM", [128, 256])
    RQ = U("RQ", [128, 4])
    OH = U("OH", [128, 4, NT])
    MS = U("MS", [128, NA])
    KD = U("KD", [128, 2, 400])
    MT = sb("MT0", [128, 8, 256], F32, u0 + 2 * 8192 + 2 * 1024 + 64)
    fill = Filler([lin_steps(8, 4, UH, UL, ready, times_r(HQ))]
                  + [lin_steps(8, 2, UH, UL, ready, times_r(OM[:, 2 * i:2 * i + 2, :]), ranges=TWO) for i in range(2)]
                  + [lin_steps(8, 4, UH, UL, ready, times_r(HG)), mem_steps(0, MT, MH, ML, AM, RM, RQ)]
                  + [lin_steps(4, 4, HH, HL, ready_o, residual(4 * g, None, last=False), ranges=((0, NT),))
                     for g in range(2)], 1.0)

    def idle(x):
        pass

    def pipeline(items, stages, fill=None, after=None):
        for step in range(len(items) + len(stages) - 1):
            for s in reversed(range(len(stages))):
                if 0 <= step - s < len(items):
                    stages[s](items[step - s])
            if fill:
                fill()
            if after and step in after:
                after[step]()

    nS = [None] * NSL
    nPT = None
    nNB = [None, None]
    mfree = {}

    def fox_bias(h):
        if h == 0:
            sp.wait((s_nc, 16))
        sp.wait(nNB[h % 2])
        load(NB[:, h % 2, :], rows[h:h + 1, :].broadcast_to([128, NA]), s_nb[h % 2])
        return (s_nb[h % 2], 16 * (h // 2 + 1))

    items = [dict(h=h, i=i, n=h * 4 + i, ns=NM + 128 * (i + 1)) for h in range(8) for i in range(4)]
    head = [dict() for _ in range(8)]
    head[0]["nb"] = fox_bias(0)

    def f0(x):
        h, i, ns = x["h"], x["i"], x["ns"]
        rows_ = slice(64 * (h % 2), 64 * (h % 2) + 64)
        lhs = Q[rows_, h // 2, 128 * i:128 * i + 128]
        x["b"] = [(take(), 0, min(ns, 512))]
        if ns > 512:
            x["b"].append((take(), 512, ns - 512))
        for b, c, n in x["b"]:
            x["t"] = mmt(bank[b][:, 0:n], lhs, K[rows_, h // 2, c:c + n], True, True)

    def f1(x):
        h, i, s = x["h"], x["i"], x["n"] % NSL
        if i == 0 and h < 7:
            head[h + 1]["nb"] = fox_bias(h + 1)
        for b, c, n in x["b"]:
            t = dve.do(call(nc.vector.scalar_tensor_tensor, S2[:, s, c:c + n], bank[b][:, 0:n], CC[:, i, h:h + 1],
                            NB[:, h % 2, c:c + n], ALU.add, ALU.add), x["t"], head[h]["nb"], t_cc, nS[s])
            give(b, t)
        nNB[h % 2] = t
        d = S2[:, s, NM + 128 * i:NM + 128 * i + 128]
        x["t"] = pool.do(call(nc.gpsimd.affine_select, out=d, in_=d, compare_op=ALU.is_ge, fill=-1e30, base=0,
                              pattern=[[-1, 128]], channel_multiplier=1), t)

    def f2(x):
        s, ns = x["n"] % NSL, x["ns"]
        m = small[:, 4 * (x["n"] % 8):4 * (x["n"] % 8) + 4]
        t = dve.do(call(nc.vector.tensor_reduce, m[:, 0:1], S2[:, s, 0:ns], AX.X, ALU.max, negate=True), x["t"],
                   mfree.get(x["n"] % 8))
        x["e"] = act.do(call(nc.scalar.activation, S2[:, s, 0:ns], S2[:, s, 0:ns], ACT.Exp, bias=m[:, 0:1],
                             accum_out=m[:, 1:2]), t)

    def f3(x):
        s, ns = x["n"] % NSL, x["ns"]
        m = small[:, 4 * (x["n"] % 8):4 * (x["n"] % 8) + 4]
        t = dve.do(call(nc.vector.reciprocal, m[:, 2:3], m[:, 1:2]), x["e"])
        x["t"] = dve.do(call(nc.vector.tensor_scalar, S2[:, s, 0:ns], S2[:, s, 0:ns], m[:, 2:3], None, ALU.mult), t)
        mfree[x["n"] % 8] = x["t"]

    def f4(x):
        i, s = x["i"], x["n"] % NSL
        b, b2 = take(), take()
        pe.wait(x["t"])
        pe.go(call(nc.tensor.transpose, bank[b2][0:NM, 0:128], S2[:, s, 0:NM], ident))
        for j in range(i + 1):
            t = pe.do(call(nc.tensor.transpose, bank[b][:, 128 * j:128 * j + 128],
                           S2[:, s, NM + 128 * j:NM + 128 * j + 128], ident))
        nS[s] = t
        x["tb"] = (b, b2, t)

    def f5(x):
        i = x["i"]
        b, b2, t = x["tb"]
        tc = slice(128 * i, 128 * i + 128)
        a = act.do(call(nc.scalar.activation, PT[:, 0:i + 1, tc],
                        bank[b][:, 0:128 * (i + 1)].rearrange("p (j n) -> p j n", n=128), ACT.Copy), t, nPT)
        give(b, a)
        a = act.do(call(nc.scalar.activation, PM[:, tc], bank[b2][0:NM, 0:128], ACT.Copy), t)
        give(b2, a)
        x["a"] = a

    def f6(x):
        nonlocal nPT
        h = x["h"]
        if x["i"] < 3:
            return
        x["o"] = o = take()
        r = slice(64 * (h % 2), 64 * (h % 2) + 64)
        hc = slice(64 * h, 64 * h + 64)
        pe.wait(x["a"], t_v)
        mm(bank[o][r, :], V[0:NM, 0, hc], PM[:, :], True, False)
        for j in range(4):
            nPT = mmt(bank[o][r, 128 * j:NT], V[:, 1 + j, hc], PT[:, j, 128 * j:NT], False, j == 3)
        x["t"] = nPT

    def f7(x):
        h = x["h"]
        if x["i"] < 3:
            return
        o, r = x["o"], slice(64 * (h % 2), 64 * (h % 2) + 64)
        a = act.do(call(nc.scalar.activation, HH[r, h // 2, :], bank[o][r, :], ACT.Copy), x["t"])
        t = dve.do(call(nc.vector.tensor_tensor, HL[r, h // 2, :], bank[o][r, :], HH[r, h // 2, :].bitcast(F32),
                        ALU.subtract), a)
        give(o, t)
        head[h]["out"] = t

    ready_gates = []

    def gate_k():
        lbr = vec[:, V_LB:V_LB + 4]
        t = dve.do(call(nc.vector.tensor_tensor, LB[:, 0, :], lbr, lbr, ALU.subtract), t_vec)
        t = act.do(call(nc.scalar.activation, LB[:, 1, :], LB[:, 0, :], ACT.Exp), t)
        t = dve.do(call(nc.vector.reciprocal, LB[:, 2, :], LB[:, 1, :]), t)
        t = dve.do(call(nc.vector.tensor_tensor, LB[:, 3, :], LB[:, 1, :], LB[:, 2, :], ALU.mult), t)
        t = dve.do(call(nc.vector.tensor_tensor, LB[:, 4, :], LB[:, 3, :], LB[:, 3, :], ALU.subtract), t)
        t_lb = dve.do(call(nc.vector.tensor_scalar, LB[:, 5, :], LB[:, 4, :], -1.0, 1.0, ALU.mult, ALU.add), t)
        t = act.do(call(nc.scalar.activation, OM[:, :, :], OM[:, :, :], ACT.Sigmoid, scale=-1.0),
                   (dve.sem, t_lb[1] - 4))
        dve.wait(t, t_lb)
        for h in range(4):
            t = dve.do(call(nc.vector.tensor_scalar, OM[:, h, :], OM[:, h, :], LB[:, 5, h:h + 1], None, ALU.mult))
        ready_gates.append(t)

    def gate_q():
        t = act.do(call(nc.scalar.activation, HQ[:, :, :], HQ[:, :, :], ACT.Silu), ready_gates[0])
        ready_gates.append(dve.do(call(nc.vector.tensor_scalar, HQ[:, :, :], HQ[:, :, :], float(128 ** -0.5), None,
                                       ALU.mult), t))

    def gate_g():
        ready_gates.append(act.do(call(nc.scalar.activation, HG[:, :, :], HG[:, :, :], ACT.Silu), (dve.sem, dve.n)))

    pe.wait((dve.sem, dve.n))
    pipeline(items, [f0, f1, f2, idle, f3, f4, f5, f6, f7], fill, {34: gate_k, 35: gate_q, 37: gate_g})
    assert len(fill.gens) == 3
    ready_o[0:4] = [[head[2 * k + 1]["out"]] for k in range(4)]

    def fence():
        toks = [(x.sem, x.n) for x in (pe, act, dve, pool) if x.n]
        for x in (act, dve, pool):
            x.wait(*toks)
        return toks

    fence()
    R = arena(r0, END0)
    FG = R("FG", [128, 2, NA])
    B = R("B", [128, 2, NA])
    XL2 = R("XL2", [128, 2, 2, NT])
    GT = sb("GT", [128, 2, NA], F32, r0 + 2 * 2 * NA * 4)
    TN = sb("TN", [128, 2, NT], F32, r0 + 2 * 2 * NA * 4)
    EX2 = R("EX2", [128, 2, 2, NT])
    QE = R("QE", [128, 2, NT])
    KT = R("KT", [128, 2, 2, 128])
    ST = R("ST", [128, 4, 2, 128])
    AT = R("AT", [128, 4, 2, 128])
    EL = R("EL", [128, 4, 4])
    t_u = [(pe.sem, pe.n)]
    t_k, t_q, t_hg = ready_gates
    fill(5)
    fill.rate = 0.88
    t = dve.do(call(nc.vector.memset, MS[:, :], 1.0))
    dve.wait(t)
    for c in (0, 16, 144, 272, 400):
        t_ms = dve.do(call(nc.vector.memset, MS[:, c:c + 1], 0.0))

    def every(x, n):
        return x.unsqueeze(x.ndim).broadcast_to(list(x.shape) + [n])

    def pairs(x, t):
        return x.rearrange("p h (n t) -> p h n t", t=2)[:, :, :, t]

    def halves(x, n, t):
        return x.rearrange("p h (b t n) -> p h b t n", t=2, n=n)[:, :, :, t, :]

    done = [(pe.sem, pe.n)]
    xfree, exfree, last_b = [None, None], [None, None], []
    t_oh = None
    t_qe_last = [None]

    def decays(p):
        om = OM[:, 2 * p:2 * p + 2]
        t = dve.do(call(nc.vector.tensor_scalar, FG[:, :, :], om, -1.0, 1.0, ALU.mult, ALU.add), t_k, *done, *last_b)
        t_f = dve.do(call(nc.vector.tensor_scalar, FG[:, :, :], FG[:, :, :], FMIN, None, ALU.max), t)
        fill(2)
        t_g = act.do(call(nc.scalar.activation, GT[:, :, :], FG[:, :, :], ACT.Ln), t_f, *done, *xfree)
        dve.wait(t_g, t_ms)
        for h in range(2):
            t_b = dve.do(call(nc.vector.tensor_tensor_scan, B[:, h, :], MS[:, :], GT[:, h, :], 0.0, ALU.mult,
                              ALU.add))
        fill(2)
        return t_b

    def two_heads(p, t_b):
        nonlocal done, last_b, t_oh
        om, hq, el = OM[:, 2 * p:2 * p + 2], HQ[:, 2 * p:2 * p + 2], EL[:, 2 * p:2 * p + 2]
        omx, fgx, bx = om[:, :, xc], FG[:, :, xc], B[:, :, xc]
        atok = pool.do(call(nc.gpsimd.memset, AT[:, :, :, :], 0.0), *done)

        def produce(l):
            n, s = LEVELS[l], l % 2
            ex, X = EX2[:, (l + 1) % 2], XL2[:, s]
            midb = every(halves(bx, n, 0)[:, :, :, n - 1], n)
            a = pool.do(call(nc.gpsimd.tensor_tensor, halves(ex, n, 0), midb, halves(bx, n, 0), ALU.subtract),
                        exfree[(l + 1) % 2], t_b)
            d = dve.do(call(nc.vector.tensor_tensor, halves(ex, n, 1), halves(bx, n, 1), midb, ALU.subtract),
                       exfree[(l + 1) % 2], t_b, a)
            x = act.do(call(nc.scalar.activation, ex, ex, ACT.Exp), a, d)
            return ex, X, n, s, x

        nxt = produce(0)

        X0, X1 = XL2[:, 0], XL2[:, 1]
        ex0 = EX2[:, 0, :, 0:256]
        t1 = act.do(call(nc.scalar.activation, ex0, pairs(GT[:, :, xc], 1), ACT.Exp, scale=-1.0), t_b, exfree[0])
        dve.do(call(nc.vector.tensor_copy, pairs(X0, 0), pairs(omx, 0)), t1)
        ta = dve.do(call(nc.vector.tensor_tensor, pairs(X0, 1), pairs(omx, 1), ex0, ALU.mult), t1)
        exfree[0] = ta
        tb = act.do(call(nc.scalar.activation, pairs(X1, 0), pairs(hq, 0), ACT.Copy), t_b, t_q, t1, ta)
        tb = pool.do(call(nc.gpsimd.tensor_tensor, pairs(X1, 1), pairs(hq, 1), pairs(fgx, 1), ALU.mult), tb)

        def consume(l, lhs, rhs, a, d, xs):
            nonlocal atok
            pe.wait(a, d)
            for c in (0, 2):
                b = take()
                for cc in (c, c + 1):
                    for h in range(2):
                        o = 256 * (cc - c) + 128 * h
                        n = slice(128 * cc, 128 * cc + 128)
                        t = mmt(bank[b][:, o:o + 128], lhs[:, h, n], rhs[:, h, n], True, True)
                m = msk[:, l, :].unsqueeze(1).broadcast_to([128, 4, 128])
                atok = dve.do(call(nc.vector.copy_predicated, AT[:, c:c + 2, :, :].rearrange("p c h n -> p (c h) n"), m,
                                   bank[b][:, :].rearrange("p (h n) -> p h n", n=128)), t, atok, t_msk)
                give(b, atok)
            for x in xs:
                xfree[x] = t

        def ends():
            kd4 = KD[:, :, 16:400].rearrange("p h (c n) -> p h c n", n=128)
            b4 = B[:, :, 16:400].rearrange("p h (c n) -> p h c n", n=128)
            pool.do(call(nc.gpsimd.tensor_tensor, KD[:, :, 0:16], every(B[:, :, 15], 16), B[:, :, 0:16],
                         ALU.subtract), t_b, *done)
            t = pool.do(call(nc.gpsimd.tensor_tensor, kd4, every(b4[:, :, :, 127], 128), b4, ALU.subtract))
            t = act.do(call(nc.scalar.activation, KD[:, :, :], KD[:, :, :], ACT.Exp), t)
            t_el = act.do(call(nc.scalar.activation, el[:, :, 0:3], b4[:, :, :, 127], ACT.Exp), t_b)
            t2 = act.do(call(nc.scalar.activation, QE[:, :, :], bx, ACT.Exp), t_b, *done)
            t_kd = pool.do(call(nc.gpsimd.tensor_tensor, KD[:, :, :], KD[:, :, :], om[:, :, 0:400], ALU.mult), t, t_k)
            t_qe = dve.do(call(nc.vector.tensor_tensor, QE[:, :, :], QE[:, :, :], hq, ALU.mult), t2, t_q)
            return t_kd, t_qe, t_el, t2

        stt, ktf, kta = [None] * 4, [None, None], None

        def turn(c):
            nonlocal kta
            n0, n = (0, 16) if c == 0 else (NM + 128 * (c - 1), 128)
            b = take()
            pe.wait(t_kd, t_cst)
            for h in range(2):
                t = pe.do(call(nc.tensor.transpose, bank[b][0:n, 128 * h:128 * h + 128], KD[:, h, n0:n0 + n], ident))
            kta = act.do(call(nc.scalar.activation, KT[0:n, c % 2, :, :],
                              bank[b][0:n, 0:256].rearrange("p (h n) -> p h n", n=128), ACT.Copy), t, ktf[c % 2],
                         *done)
            give(b, kta)

        def state(c):
            n = 16 if c == 0 else 128
            b = take()
            pe.wait(kta, t_v2)
            for h in range(2):
                v = slice(128 * (2 * p + h), 128 * (2 * p + h) + 128)
                t = mmt(bank[b][:, 128 * h:128 * h + 128], KT[0:n, c % 2, h, :], V2[0:n, c, v], True, True)
            ktf[c % 2] = t
            if c == 0:
                s = dve.do(call(nc.vector.tensor_copy, ST[:, 0, :, :],
                                bank[b][:, 0:256].rearrange("p (h n) -> p h n", n=128)), t, *done)
            else:
                dve.wait(t, t_el, stt[c - 1])
                for h in range(2):
                    s = dve.do(call(nc.vector.scalar_tensor_tensor, ST[:, c, h, :], ST[:, c - 1, h, :],
                                    el[:, h, c - 1:c], bank[b][:, 128 * h:128 * h + 128], ALU.mult, ALU.add))
            stt[c] = s
            give(b, s)

        ready_x = (0, X0, X1, ta, tb, [0, 1])
        fill(2)
        consume(*ready_x)
        ready_x = None
        for l in range(len(LEVELS)):
            cur = nxt
            if l + 1 < len(LEVELS):
                nxt = produce(l + 1)
            ex, X, n, s, x = cur
            a = pool.do(call(nc.gpsimd.tensor_tensor, halves(X, n, 0), halves(ex, n, 0), halves(omx, n, 0), ALU.mult),
                        x, xfree[s])
            d = dve.do(call(nc.vector.tensor_tensor, halves(X, n, 1), halves(ex, n, 1), halves(hq, n, 1), ALU.mult),
                       x, xfree[s], t_q, a)
            exfree[(l + 1) % 2] = d
            if ready_x:
                consume(*ready_x)
            if l >= 2:
                turn(l - 2)
            fill()
            ready_x = (l + 1, X, X, a, d, [s])
            if l == 1:
                t_kd, t_qe, t_el, t_e = ends()
            if l >= 2:
                state(l - 2)
        fill()
        consume(*ready_x)
        last_b = [d, a, t_kd, t_e, t_el, t_qe, nxt[4], kta]
        nxt_b = decays(1) if p == 0 else None

        for c in range(1, 5):
            bo = take()
            pe.wait(t_qe, atok, stt[c - 1], t_v2)
            for h in range(2):
                o = bank[bo][:, 128 * h:128 * h + 128]
                v = slice(128 * (2 * p + h), 128 * (2 * p + h) + 128)
                mm(o, ST[:, c - 1, h, :], QE[:, h, 128 * (c - 1):128 * c], True, False)
                to = mmt(o, V2[:, c, v], AT[:, c - 1, h, :], False, True)
            t_oh = act.do(call(nc.scalar.activation, OH[:, 2 * p:2 * p + 2, 128 * (c - 1):128 * c],
                               bank[bo][:, 0:256].rearrange("p (h n) -> p h n", n=128), ACT.Copy), to)
            give(bo, t_oh)
            fill()
        done = [to]
        t_qe_last[0] = t_qe
        return nxt_b

    two_heads(1, two_heads(0, decays(0)))

    t_o = t_oh

    def head_norm(src, dsth, wcol, tok, gate, tmp, wtok, free_=()):
        b = take()
        cols = bank[b]
        rsf = [None, None]
        for h in range(4):
            q = tmp[:, h % 2, :]
            a = act.do(call(nc.scalar.activation, q, src[:, h, :], ACT.Square), tok, rsf[h % 2], *free_)
            pe.wait(a, t_ones)
            for i in range(4):
                rsf[h % 2] = mmt(cols[:, 4 * h + i:4 * h + i + 1], q[:, 128 * i:128 * i + 128], ones[:, 0:1], True,
                                 True)
        a = act.do(call(nc.scalar.activation, HN[:, :], cols[:, 0:16], ACT.Sqrt, bias=eps[:, :], scale=1.0 / 128),
                   rsf[1])
        give(b, a)
        tr = dve.do(call(nc.vector.reciprocal, HN[:, :], HN[:, :]), a)
        fill()
        out_ = []
        xs = [dict(h=h) for h in range(4)]

        def n1(x):
            h = x["h"]
            x["q"] = spread(HN, 128, tmp[:, h % 2, :], [(4 * h + i, 128 * i) for i in range(4)], tr, rsf[h % 2])

        def n2(x):
            h = x["h"]
            t = dve.do(call(nc.vector.scalar_tensor_tensor, src[:, h, :], src[:, h, :], wcol, tmp[:, h % 2, :],
                            ALU.mult, ALU.mult), x["q"], wtok)
            rsf[h % 2] = t
            if gate is not None:
                t = dve.do(call(nc.vector.tensor_tensor, src[:, h, :], src[:, h, :], gate[:, h, :], ALU.mult), t)
            x["t"] = t
            x["a"] = act.do(call(nc.scalar.activation, HH[:, dsth + h, :], src[:, h, :], ACT.Copy), t, *free_)

        def n3(x):
            h = x["h"]
            x["r"] = dve.do(call(nc.vector.tensor_tensor, HL[:, dsth + h, :], src[:, h, :],
                                 HH[:, dsth + h, :].bitcast(F32), ALU.subtract), x["a"], x["t"], *free_)

        pipeline(xs, [n1, n2, n3], fill)
        fill.finish()
        return [[x["r"]] for x in xs]

    fill.rate = 1.0
    ready_o[4:] = head_norm(OH, 4, vec[:, V_HN:V_HN + 1], t_o, HG, TN, t_hg, [t_q, t_qe_last[0], done[0]])

    fence()
    F = arena(t0, END0 - 4 * NT)
    T = F("T", [128, 12, NT])
    SZ = F("SZ", [128, 2, NT])
    ACC2 = sb("ACC2", [128, NT], F32, END0 - 4 * NT)
    WW = F("WW", [128, 8])
    t_w2 = dve.do(call(nc.vector.tensor_tensor, WW[:, :], vec[:, V_FIN:V_FIN + 8], vec[:, V_MIX2:V_MIX2 + 8],
                       ALU.mult), t_vec)
    for g in range(2):
        lin(4, 4, HH, HL, ready_o, residual(4 * g, vec[:, V_FFN:V_FFN + 8]), ranges=((0, NT),), ks=[4, 5, 6, 7])

    rms_hook = {5: lambda: norm_columns(CH), 7: norm_rows}

    tfree = [None] * 12
    tn = [0]

    def temp():
        i = tn[0] % 12
        tn[0] += 1
        return T[:, i, :], i

    ready_h = [[] for _ in range(8)]

    f0_ = 0
    first = True
    for ci, nh in enumerate(HIDDEN):
        for j in range(0, nh, 2):
            store = {}

            def evac(m, p, tok, n0, n, j=j):
                if m < 2:
                    x, i = temp()
                    y, i2 = temp()
                    a = dve.do(call(nc.vector.tensor_tensor, x, p, RB[:, xc], ALU.mult), tok, nm_.rb, tfree[i])
                    s = act.do(call(nc.scalar.activation, y, x, ACT.Silu), a, tfree[i2])
                    tfree[i] = s
                    store[m] = (y, i2, s)
                    return a
                y, i2, s = store[m - 2]
                x, i = temp()
                k = j + m - 2
                a = dve.do(call(nc.vector.tensor_tensor, x, p, RB[:, xc], ALU.mult), tok, nm_.rb, tfree[i])
                t = dve.do(call(nc.vector.tensor_tensor, x, x, y, ALU.mult), a, s)
                tfree[i2] = t
                h = act.do(call(nc.scalar.activation, HH[:, k, :], x, ACT.Copy), t)
                flush()

                def lo():
                    t2 = dve.do(call(nc.vector.tensor_tensor, HL[:, k, :], x, HH[:, k, :].bitcast(F32),
                                     ALU.subtract), h, t)
                    ready_h[k] = [t2]
                    tfree[i] = t2
                late.append(lo)
                return a
            lin(8, 4, UH, UL, ready, evac, hook=rms_hook if first else None)
            first = False
        lastc = ci == len(HIDDEN) - 1
        acc2 = None
        sz = [None, None]

        def also(k, src, t):
            nonlocal acc2
            z = SZ[:, k % 2, :]
            a = act.do(call(nc.scalar.activation, z, src, ACT.Square, scale=vec[:, V_FIN + k:V_FIN + k + 1]), t,
                       sz[k % 2])
            if k == 0:
                acc2 = pool.do(call(nc.gpsimd.tensor_copy, ACC2[:, :], z), a)
            else:
                acc2 = pool.do(call(nc.gpsimd.tensor_tensor, ACC2[:, :], ACC2[:, :], z, ALU.add), a, acc2)
            sz[k % 2] = acc2
        for g in range(2):
            lin(nh, 4, HH, HL, ready_h, residual(4 * g, WW[:, :] if lastc else None, last=lastc,
                                                 also=also if lastc else None), ranges=((0, NT),), hook=None)

    t_x = None

    def double_columns():
        nonlocal t_x
        t_x, _ = columns([ACC], CH, RD, 0, 1024, nm_.acc)
        b = take()
        pe.wait(acc2)
        for i in range(4):
            t = mmt(bank[b][:, i:i + 1], ACC2[:, 128 * i:128 * i + 128], ones[:, 0:1], True, True)
        nm_.read = t
        d = dve.do(call(nc.vector.tensor_tensor, RD[:, 4:8], RD[:, 0:4], RD[:, 0:4], ALU.mult), t_x)
        d = dve.do(call(nc.vector.tensor_tensor, RD[:, 4:8], bank[b][:, 0:4], RD[:, 4:8], ALU.mult), d, t)
        give(b, d)
        d = act.do(call(nc.scalar.activation, RD[:, 4:8], RD[:, 4:8], ACT.Sqrt, bias=eps[:, :], scale=1.0 / 1024), d)
        d = dve.do(call(nc.vector.reciprocal, RD[:, 4:8], RD[:, 4:8]), d)
        nm_.rc = dve.do(call(nc.vector.tensor_tensor, RC[:, 0:4], RD[:, 0:4], RD[:, 4:8], ALU.mult), d)
        nm_.chunks = CH

    def double_rows():
        norm_rows()
        nonlocal t_r1
        t_r1 = spread(RD, 128, R1, [(i, 128 * i) for i in range(4)], t_x, (pe.sem, pe.n))

    t_h = [[*ready[k], h_tok[k], acc2, nm_.acc] for k in range(8)]
    t_r1 = None

    def stream_normed():
        for k in range(8):
            h_tok[k] = dve.do(call(nc.vector.scalar_tensor_tensor, H[:, k, xc], H[:, k, xc],
                                   vec[:, V_FIN + k:V_FIN + k + 1], R1[:, :], ALU.mult, ALU.mult), *t_h[k], t_r1)

    t_before = fence()
    G = arena(t0, END1)
    Q = G("Q3", [128, 4, NT])
    K = G("K3", [128, 4, NT])
    V = G("V3", [128, 4, NT])
    YU = G("YU", [128, 4, NT])
    LA = G("LA", [64, 2])
    LM = G("LM", [128, 4])
    small = G("small3", [128, 64])
    BH = G("BH", [128, 4, NT])
    R1 = sb("R1", [128, NT], F32, h0 + 8192)
    RD = G("RD", [128, 8])

    GB = sb("GB", [128, 4, 384], F32, h0)
    PWT = sb("PWT", [128, 3, NT], F32, h0 + 16384)
    PW = sb("PW", [128, 4, 128], F32, h0 + 16384 + 6144)
    s_pw = new_sem("s_pw")
    s_b = new_sem("s_b")
    tnf = []

    def pooling():
        pfree = None
        for g, w in enumerate(WINDOWS):
            src = YU[:, g, :]
            d, t = 1, t_yu
            i = 0
            while d < w:
                dst = PWT[:, i % 2, :]
                pool.do(call(nc.gpsimd.tensor_copy, dst[:, 0:d], src[:, 0:d]), t, pfree)
                t = pool.do(call(nc.gpsimd.tensor_tensor, dst[:, d:NT], src[:, d:NT], src[:, 0:NT - d], ALU.add))
                src = dst
                d *= 2
                i += 1
            yield
            p = PWT[:, 2, :]
            u = YU[:, g, :]
            t = dve.do(call(nc.vector.scalar_tensor_tensor, p[:, w:NT], src[:, w:NT], 1.0 / w, u[:, w:NT],
                            ALU.mult, ALU.subtract), t, pfree)
            ci = cst[:, C_CINV + 16 * g:C_CINV + 16 * g + w]
            t2 = dve.do(call(nc.vector.tensor_tensor, p[:, 0:w], src[:, 0:w], ci, ALU.mult), t_cst)
            t = dve.do(call(nc.vector.tensor_tensor, p[:, 0:w], p[:, 0:w], u[:, 0:w], ALU.subtract), t2)
            pool_in = t
            yield
            b = take()
            pfree = mmt(bank[b][:, :], PW[:, g, :], p, True, True, pool_in, (s_pw, 16))
            t = dve.do(call(nc.vector.tensor_scalar, u, bank[b][:, :], vec[:, V_PS + g:V_PS + g + 1], None,
                            ALU.mult), pfree)
            give(b, t)
            tnf.append(hilo(HH[:, 4 + g, :], HL[:, 4 + g, :], u, None, t))
            ready_h[4 + g] = [tnf[g]]

    def step(gen):
        for _ in gen:
            return

    lin(8, 4, UH, UL, ready, times_r(YU), hook={6: double_columns, 7: double_rows})
    t_yu = (dve.sem, dve.n)
    sp.wait(*t_before)
    load(PW[:, :, :], A["pool_w"].rearrange("g c d -> c g d"), s_pw)
    pools = pooling()
    step(pools)

    for h in range(4):
        b = take()
        rel = vec[0:32, V_REL + h:V_REL + h + 1].broadcast_to([32, 128])
        t = mmt(bank[b][:, 0:384], rel, cst[0:32, C_ONEHOT:C_ONEHOT + 384], True, True, t_cst, t_vec)
        t = act.do(call(nc.scalar.activation, GB[:, h, :], bank[b][:, 0:384], ACT.Copy), t)
        give(b, t)
    sp.wait(t)
    load(scratch, GB[:, :, :], s_b)
    t_gb = t

    def skewed():
        sp.wait((s_b, 16))
        skew = bass.AP(scratch.tensor, 127, [[1535, 128], [384, 4], [1, 256]])
        load(BH[:, :, 256:512], skew, s_b)

    hooks = {i: lambda: step(pools) for i in (2, 4, 6)}
    hooks[0] = stream_normed
    hooks[1] = skewed
    lin(8, 4, UH, UL, ready, times_r(Q, 0.125), hook=hooks)
    far = GB[:, :, 0:1].broadcast_to([128, 4, 256])
    dve.do(call(nc.vector.tensor_copy, BH[:, :, 0:256], far), t_gb)
    diag = BH[:, :, 384:512]
    t_bh = dve.do(call(nc.vector.tensor_tensor, diag, diag, causal.unsqueeze(1).broadcast_to([128, 4, 128]), ALU.add),
                  (s_b, 32), t_cst)
    lin(8, 4, UH, UL, ready, times_r(K), hook={i: lambda: step(pools) for i in (1, 3, 4, 6, 7)})
    assert len(tnf) == 4

    lv = lambda i: vec[0:64, V_LAM + i:V_LAM + i + 1]
    dve.do(call(nc.vector.tensor_tensor, LA[:, 0:1], lv(0), lv(1), ALU.mult), t_vec)
    t_la = dve.do(call(nc.vector.tensor_tensor, LA[:, 1:2], lv(2), lv(3), ALU.mult))
    MH = sb("MH3", [128, 8, 256], F32R, h0)
    ML = sb("ML3", [128, 8, 256], F32R, h0 + 16384)
    RQ = G("RQ3", [128, 4])
    AM = G("AM3", [128, 256])
    RM = G("RM3", [128, 256])
    fill = Filler([mem_steps(1, sb("MT3", [128, 8, 256], F32, END1), MH, ML, AM, RM, RQ)]
                  + [lin_steps(4, 4, HH, HL, ready_h, residual(4 * g, None, last=False), ranges=((0, NT),),
                               ks=[4, 5, 6, 7]) for g in range(2)], 1.45)
    for i, _ in enumerate(tok_steps(8, UH, UL, ready, CH, rows_r(V, 1))):
        fill.one()
    t_v = (act.sem, act.n)
    b = take()
    t = mmt(bank[b][:, 0:2], ones[0:64, :], LA[:, :], True, True, t_la)
    t = act.do(call(nc.scalar.activation, LM[:, 0:2], bank[b][:, 0:2], ACT.Exp), t)
    give(b, t)
    t = dve.do(call(nc.vector.tensor_tensor, LM[:, 2:3], LM[:, 1:2], LM[:, 0:1], ALU.subtract), t)
    t_lm = dve.do(call(nc.vector.tensor_scalar, LM[:, 3:4], LM[:, 2:3], -LAMBDA_INIT, None, ALU.add), t)
    t_sg = dve.do(call(nc.vector.tensor_scalar, LM[:, 0:1], vec[:, V_SUB:V_SUB + 1], 1.0 - LAMBDA_INIT, None, ALU.mult),
                  t_lm)
    fence()
    U = arena(u0, u1)
    NSL = 5
    S4 = U("S4", [128, NSL, 2, NT])
    PT = U("PT3", [128, 4, NT])
    TN = U("TN3", [128, 2, NT])
    OH = sb("OH3", [128, 4, NT], F32, t0 + 3 * 4 * NT * 4)
    t = tnf[3]

    OHfree = t
    items = [dict(h=h, i=i, n=h * 4 + i, ns=128 * (i + 1)) for h in range(4) for i in range(4)]
    sf = [None] * NSL
    smf = [None] * 8
    ptf = None
    t_oh = []

    def d0(x):
        h, i, ns = x["h"], x["i"], x["ns"]
        x["b"] = [take(), take()]
        for j in range(2):
            r = slice(64 * j, 64 * j + 64)
            x["t"] = mmt(bank[x["b"][j]][:, 0:ns], Q[r, h, 128 * i:128 * i + 128], K[r, h, 0:ns], True, True)

    def d1(x):
        h, s, ns = x["h"], x["n"] % NSL, x["ns"]
        m = small[:, 8 * (x["n"] % 8):8 * (x["n"] % 8) + 8]
        x["e"] = []
        ts = []
        for j in range(2):
            S, b = S4[:, s, j, 0:ns], x["b"][j]
            t = dve.do(call(nc.vector.tensor_tensor, S, bank[b][:, 0:ns], BH[:, h, NT - ns:NT], ALU.add),
                       x["t"], sf[s], t_bh)
            give(b, t)
            ts.append(t)
        for j in range(2):
            S = S4[:, s, j, 0:ns]
            t = dve.do(call(nc.vector.tensor_reduce, m[:, j:j + 1], S, AX.X, ALU.max, negate=True), ts[j],
                       smf[x["n"] % 8])
            x["e"].append(act.do(call(nc.scalar.activation, S, S, ACT.Exp, bias=m[:, j:j + 1],
                                      accum_out=m[:, 2 + j:3 + j]), t))

    def d2(x):
        s, ns = x["n"] % NSL, x["ns"]
        m = small[:, 8 * (x["n"] % 8):8 * (x["n"] % 8) + 8]
        A_, B_ = S4[:, s, 0, 0:ns], S4[:, s, 1, 0:ns]
        t = dve.do(call(nc.vector.reciprocal, m[:, 4:6], m[:, 2:4]), *x["e"])
        t2 = dve.do(call(nc.vector.tensor_tensor, m[:, 6:7], m[:, 5:6], LM[:, 3:4], ALU.mult), t_lm, t)
        x["s"] = t2, act.do(call(nc.scalar.activation, A_, A_, ACT.Copy, scale=m[:, 4:5]), t)

    def d2b(x):
        s, ns = x["n"] % NSL, x["ns"]
        m = small[:, 8 * (x["n"] % 8):8 * (x["n"] % 8) + 8]
        A_, B_ = S4[:, s, 0, 0:ns], S4[:, s, 1, 0:ns]
        t2, t1 = x["s"]
        x["t"] = dve.do(call(nc.vector.scalar_tensor_tensor, A_, B_, m[:, 6:7], A_, ALU.mult, ALU.add), t1, t2)
        smf[x["n"] % 8] = x["t"]

    def d3(x):
        s = x["n"] % NSL
        b = take()
        pe.wait(x["t"])
        for j in range(x["i"] + 1):
            t = pe.do(call(nc.tensor.transpose, bank[b][:, 128 * j:128 * j + 128],
                           S4[:, s, 0, 128 * j:128 * j + 128], ident))
        sf[s] = t
        x["tb"] = (b, t)

    def d4(x):
        i = x["i"]
        b, t = x["tb"]
        x["a"] = act.do(call(nc.scalar.activation, PT[:, 0:i + 1, 128 * i:128 * i + 128],
                             bank[b][:, 0:128 * (i + 1)].rearrange("p (j n) -> p j n", n=128), ACT.Copy), t, ptf)
        give(b, x["a"])

    def d5(x):
        nonlocal ptf
        if x["i"] < 3:
            return
        h, o = x["h"], take()
        x["o"] = o
        pe.wait(x["a"], t_v)
        for j in range(4):
            ptf = mmt(bank[o][:, 128 * j:NT], V[:, j, 128 * h:128 * h + 128], PT[:, j, 128 * j:NT], j == 0, j == 3)
        x["t"] = ptf

    def d6(x):
        if x["i"] < 3:
            return
        a = act.do(call(nc.scalar.activation, OH[:, x["h"], :], bank[x["o"]][:, :], ACT.Copy), x["t"])
        give(x["o"], a)
        t_oh.append(a)

    pe.wait((dve.sem, dve.n))
    pipeline(items, [d0, d1, idle, d2, d2b, d3, d4, d5, d6], fill)
    fill.rate = 1.0
    pool.wait(*tnf)
    ready_h[0:4] = head_norm(OH, 0, LM[:, 0:1], t_oh[-1], None, TN, t_sg, [*tnf, (pe.sem, pe.n)])
    for g in range(2):
        lin(4, 4, HH, HL, ready_h, residual(4 * g, vec[:, V_XA2:V_XA2 + 8]), ranges=((0, NT),))

    g0 = t0

    def cross(l):
        fence()
        G = arena(g0, END1)
        QX = G(f"QX{l}", [128, 8, NT])
        S = G(f"SX{l}", [128, 4, 2, 256])
        PT = G(f"PX{l}", [128, 2, 4, NT])
        small = G(f"small{l}x", [128, 64])

        for g in range(2):
            def evac(m, p, t, n0, n, g=g):
                return dve.do(call(nc.vector.scalar_tensor_tensor, QX[:, 4 * g + m, :], p, 1.0 / 16, RB[:, xc],
                                   ALU.mult, ALU.mult), t, nm_.rb)
            lin(8, 4, UH, UL, ready, evac, hook=rms_hook if g == 0 else None)
        items = [dict(h=h, i=i, n=4 * h + i) for h in range(2) for i in range(4)]
        sf = [None] * 4
        mf = [None] * 4
        qt = (dve.sem, dve.n)
        pe.wait(qt, (act.sem, act.n))

        def c0(x):
            b = take()
            for j in range(2):
                for d in range(2):
                    k = 4 * x["h"] + 2 * j + d
                    t = mmt(bank[b][:, 256 * j:256 * j + 256], QX[:, k, 128 * x["i"]:128 * x["i"] + 128],
                            KM[l][:, k, :], d == 0, d == 1)
            x["b"], x["t"] = b, t

        def c1(x):
            s = x["n"] % 4
            b = x["b"]
            m = small[:, 8 * s:8 * s + 8]
            t = dve.do(call(nc.vector.tensor_reduce, m[:, 0:2], bank[b][:, :].rearrange("p (j n) -> p j n", j=2), AX.X,
                            ALU.max, negate=True), x["t"], mf[s])
            for j in range(2):
                x["e"] = act.do(call(nc.scalar.activation, S[:, s, j, :], bank[b][:, 256 * j:256 * j + 256], ACT.Exp,
                                     bias=m[:, j:j + 1], accum_out=m[:, 2 + j:3 + j]), t, sf[s])
            give(b, x["e"])

        def c2(x):
            s = x["n"] % 4
            m = small[:, 8 * s:8 * s + 8]
            t = dve.do(call(nc.vector.reciprocal, m[:, 4:6], m[:, 2:4]), x["e"])
            dve.wait(t)
            for j in range(2):
                t = dve.do(call(nc.vector.tensor_scalar, S[:, s, j, :], S[:, s, j, :], m[:, 4 + j:5 + j], None,
                                ALU.mult))
            mf[s] = x["t"] = t

        def c3(x):
            s = x["n"] % 4
            b = take()
            pe.wait(x["t"])
            for j in range(4):
                t = pe.do(call(nc.tensor.transpose, bank[b][:, 128 * j:128 * j + 128],
                               S[:, s, j // 2, 128 * (j % 2):128 * (j % 2) + 128], ident))
            sf[s] = t
            x["tb"] = (b, t)

        def c4(x):
            b, t = x["tb"]
            h, i = x["h"], x["i"]
            o = PT[:, h % 2, :, 128 * i:128 * i + 128]
            src = bank[b][:, :].rearrange("p (j n) -> p j n", n=128)
            if i % 2:
                x["a"] = act.do(call(nc.scalar.activation, o, src, ACT.Copy), t)
            else:
                x["a"] = dve.do(call(nc.vector.tensor_copy, o, src), t)
            give(b, x["a"])
            pe_waits.append(x["a"])

        def c5(x):
            if x["i"] < 3:
                return
            h = x["h"]
            pe.wait(*pe_waits)
            for d in range(4):
                o = take()
                k = 4 * h + d
                for mb in range(2):
                    t = mmt(bank[o][:, :], VM[l][:, mb, 128 * k:128 * k + 128], PT[:, h % 2, 2 * (d // 2) + mb, :],
                            mb == 0, mb == 1)
                a = act.do(call(nc.scalar.activation, HH[:, k, :], bank[o][:, :], ACT.Copy), t)
                t = dve.do(call(nc.vector.tensor_tensor, HL[:, k, :], bank[o][:, :], HH[:, k, :].bitcast(F32),
                                ALU.subtract), a)
                give(o, t)
                ready_h[k] = [t]

        pe_waits = []
        pipeline(items, [c0, c1, c2, c3, c4, c5])
        for g in range(2):
            lin(8, 4, HH, HL, ready_h, residual(4 * g, vec[:, V_MLP2 + 8 * l:V_MLP2 + 8 * l + 8]),
                ranges=((0, NT),))

    def mlp(l, wnext, tail=None):
        fence()
        F = arena(g0, END1)
        T = F(f"TM{l}", [128, 8, NT])
        if tail is not None:
            tail[0] = F("SE", [128, 4, NA])
        tf = [None] * 8
        n = 0
        first = True
        for c in range(4):
            for g in range(2):
                def evac(m, p, tok, n0, nn, g=g):
                    nonlocal n
                    i, j = n % 8, (n + 1) % 8
                    n += 2
                    x, y = T[:, i, :], T[:, j, :]
                    k = 4 * g + m
                    a = dve.do(call(nc.vector.scalar_tensor_tensor, x, p, 0.0, RB[:, xc], ALU.max, ALU.mult), tok, nm_.rb,
                               tf[i])
                    t = act.do(call(nc.scalar.activation, y, x, ACT.Square), a, tf[j])
                    tf[i] = t
                    h = act.do(call(nc.scalar.activation, HH[:, k, :], y, ACT.Copy), t)
                    flush()

                    def lo():
                        tf[j] = dve.do(call(nc.vector.tensor_tensor, HL[:, k, :], y, HH[:, k, :].bitcast(F32),
                                            ALU.subtract), h, t)
                        ready_h[k] = [tf[j]]
                    late.append(lo)
                    return a
                lin(8, 4, UH, UL, ready, evac, hook=rms_hook if first else None)
                first = False
            for g in range(2):
                lin(8, 4, HH, HL, ready_h, residual(4 * g, wnext, last=c == 3, tail=tail if c == 3 else None), ranges=((0, NT),))

    cross(0)
    mlp(0, vec[:, V_MIX2 + 8:V_MIX2 + 16])

    fence()
    F = arena(g0, END1)
    T = F("TC", [128, 16, NT])
    tf = [None] * 16
    n_ = [0]

    def tmp():
        i = n_[0] % 16
        n_[0] += 1
        return T[:, i, :], i

    for j in range(8):
        got = {}

        def evac(m, p, tok, n0, n, j=j):
            x, i = tmp()
            a = dve.do(call(nc.vector.tensor_tensor, x, p, RB[:, xc], ALU.mult), tok, nm_.rb, tf[i])
            got[m] = (x, i, a)
            if m == 2:
                (bx_, ib, tb), (cx, ic, tc), (xx, ix, tx) = got[0], got[1], got[2]
                t = dve.do(call(nc.vector.tensor_tensor, cx, cx, xx, ALU.mult), tc, tx)
                tf[ix] = t
                y, iy = tmp()
                w = [vec[:, V_CONV + 8 * q + j:V_CONV + 8 * q + j + 1] for q in range(3)]
                t2 = act.do(call(nc.scalar.activation, y, cx, ACT.Copy, scale=w[2]), t, tf[iy])
                t2 = dve.do(call(nc.vector.scalar_tensor_tensor, y[:, 1:NT], cx[:, 0:NT - 1], w[1], y[:, 1:NT], ALU.mult,
                                                             ALU.add), t2)
                t2 = dve.do(call(nc.vector.scalar_tensor_tensor, y[:, 2:NT], cx[:, 0:NT - 2], w[0], y[:, 2:NT], ALU.mult,
                                                             ALU.add), t2)
                tf[ic] = t2
                t2 = dve.do(call(nc.vector.tensor_tensor, y, y, bx_, ALU.mult), t2, tb)
                tf[ib] = t2
                tf[iy] = hilo(HH[:, j, :], HL[:, j, :], y, None, t2)
                ready_h[j] = [tf[iy]]
            return a
        lin(8, 3, UH, UL, ready, evac, hook=rms_hook if j == 0 else None)
    for g in range(2):
        lin(8, 4, HH, HL, ready_h, residual(4 * g, vec[:, V_XA2 + 8:V_XA2 + 16]), ranges=((0, NT),))
    cross(1)
    tail = [None]
    mlp(1, None, tail)
    norm_columns(CH)
    for k in (2, 5):
        src = H[:, k, xc]
        h_tok[k] = act.do(call(nc.scalar.activation, src, src, ACT.Copy, scale=vec[:, V_FIN2 + k:V_FIN2 + k + 1]),
                          h_tok[k], nm_.acc)
    norm_rows()
    s_o = new_sem("s_o")
    for k in range(8):
        o = H[:, k, xc]
        if k in (2, 5):
            t = pool.do(call(nc.gpsimd.tensor_tensor, o, o, RB[:, xc], ALU.mult), nm_.rb, h_tok[k])
        else:
            t = dve.do(call(nc.vector.scalar_tensor_tensor, o, o, vec[:, V_FIN2 + k:V_FIN2 + k + 1], RB[:, xc],
                            ALU.mult, ALU.mult), nm_.rb, h_tok[k], nm_.acc)
        sp.wait(t)
        load(out[128 * k:128 * k + 128, :], H[:, k, xc], s_o)
    sp.wait((s_o, 128), (s_b, 32))
    assert st.pos == len(tiles), (st.pos, len(tiles))

    block = nc.Block()
    with block:
        block.sync(lambda e: sp.run(e))
        block.scalar(lambda e: act.run(e))
        block.vector(lambda e: dve.run(e))
        block.gpsimd(lambda e: pool.run(e))
        block.tensor(lambda e: pe.run(e))
    for cm in reversed(held):
        cm.__exit__(None, None, None)


def buckets():
    import math
    out = []
    for n in range(256):
        if n < 16:
            out.append(n)
        else:
            out.append(min(16 + int(math.log(n / 16) / math.log(8) * 16 + 1e-9), 31))
    return out


def constants():
    c = np.zeros((128, NCONST), np.float32)
    c[:, C_ID:C_ID + 128] = np.eye(128)
    i = np.arange(128)
    c[:, C_CAUSAL:C_CAUSAL + 128] = np.where(i[None, :] <= i[:, None], 0.0, -1e30)
    bk = buckets()
    for j in range(384):
        c[bk[max(255 - j, 0)], C_ONEHOT + j] = 1.0
    for g, w in enumerate(WINDOWS):
        for t in range(w):
            c[:, C_CINV + 16 * g + t] = 1.0 / min(t + 1, w)
    m = np.zeros((128, 7, 128), np.float32)
    s, t = i[:, None], i[None, :]
    m[:, 0] = (s // 2 == t // 2) & (s <= t)
    for l, n in enumerate(LEVELS):
        m[:, l + 1] = (s // (2 * n) == t // (2 * n)) & (s % (2 * n) < n) & (t % (2 * n) >= n)
    return c, m.reshape(128, 7 * 128)


def kernel(**inputs):
    import concourse.bacc as bacc
    from concourse.bass_utils import run_bass_kernel_spmd as run

    I = {k: np.asarray(v) for k, v in inputs.items()}
    w_in = I["w_in"][0]
    ff = np.zeros((1024, 128), np.float32)
    ff[:, 0:8] = w_in[:, 1536:1544]
    mats = {"w_in": w_in[:, 0:1536], "ff": ff, "hgrn": w_in[:, 1544:], "w_out": I["w_out"][0],
            "w_ffn_gate": I["w_ffn_gate"][0], "w_ffn_up": I["w_ffn_up"][0], "w_ffn_down": I["w_ffn_down"][0],
            "ab_w_in_2": I["ab_w_in_2"][0], "ab_w_out_2": I["ab_w_out_2"][0], "conv_w_in_2": I["conv_w_in_2"][0],
            "conv_w_out_2": I["conv_w_out_2"][0]}
    for n in ("xattn_wkv_2", "xattn_wq_2", "xattn_wo_2", "mlp_w1_2", "mlp_w2_2"):
        for l in range(2):
            mats[f"{n}.{l}"] = I[n][l]
    tiles = [t for lot in plan() for t in lot]
    stream = np.empty((len(tiles) // 8, 128, 1024), np.float32)
    for i, (n, k, c) in enumerate(tiles):
        stream[i // 8, :, 128 * (i % 8):128 * (i % 8) + 128] = mats[n][128 * k:128 * k + 128, 128 * c:128 * c + 128]

    vecs = np.zeros((128, NVEC), np.float32)

    def put(col, v):
        vecs[:, col:col + v.size // 128] = v.reshape(-1, 128).T

    put(V_MIX, I["norm_mix_w"][0])
    put(V_FFN, I["norm_ffn_w"][0])
    put(V_FIN, I["norm_final_w"])
    put(V_MEM, I["mem_norm_g_2"])
    for l in range(2):
        put(V_MIX2 + 8 * l, I["norm_mix_g_2"][l])
        put(V_XA2 + 8 * l, I["norm_xattn_g_2"][l])
        put(V_MLP2 + 8 * l, I["norm_mlp_g_2"][l])
    put(V_FIN2, I["final_norm_g_2"])
    put(V_LB, I["hgrn_lb_raw"][0])
    put(V_HN, I["hgrn_norm_w"][0])
    put(V_SUB, I["subln_g_2"][0])
    put(V_PS, I["pool_scale_2"][0])
    for q in range(3):
        put(V_CONV + 8 * q, I["conv_w_2"][0, q])
    vecs[0:8, V_FB] = I["fox_f_bias"][0]
    for i, n in enumerate(("lambda_q1_2", "lambda_k1_2", "lambda_q2_2", "lambda_k2_2")):
        vecs[0:64, V_LAM + i] = I[n][0]
    vecs[0:32, V_REL:V_REL + 4] = I["rel_bias_2"]
    consts, masks = constants()
    arrays = {
        "hT": np.ascontiguousarray(np.concatenate([I["meta"], I["x"][0]], 0).T),
        "memT": np.ascontiguousarray(I["mem_2"][0].T),
        "stream": stream, "vecs": vecs, "consts": consts, "masks": masks,
        "pool_w": np.ascontiguousarray(I["pool_w_2"][0]),
    }
    nc = bacc.Bacc("TRN2", target_bir_lowering=False, num_devices=1)
    A = {n: nc.dram_tensor(n, a.shape, mybir.dt.from_np(a.dtype), kind="ExternalInput").ap()
         for n, a in arrays.items()}
    out = nc.dram_tensor("outT", (1024, NT), F32, kind="ExternalOutput").ap()
    scratch = nc.dram_tensor("skew", (128, 4, 384), F32, kind="Internal").ap()
    rows = nc.dram_tensor("rows", (8, NA), F32, kind="Internal").ap()
    build(nc, A, out, scratch, rows)
    r = run(nc, [arrays], core_ids=[0])
    return np.ascontiguousarray(np.asarray(r.results[0]["outT"]).T)[None]
```
